# Optimizing a Trainium2 kernel written in Bass

```python
import jax
import jax.numpy as jnp
from jax import lax
import numpy as np

D_MODEL = 1024
BATCH = 1
SEQ = 1024
DEPTH = 2
DEC_BATCH = 8
DEC_SEQ = 4
PAST_LEN = 2048
PAGE_SIZE = 128

N_MIXERS = 2
N_MLA_LAYERS = (DEPTH + 1) // 2
N_RWKV_LAYERS = DEPTH // 2
N_META = 16
D_FF = 4 * D_MODEL
RMS_EPS = 1e-6
NEG_INF = -1e30

MLA_HEADS = 8
QK_NOPE = 128
QK_ROPE = 64
V_HEAD = 128
Q_LORA = 3 * D_MODEL // 8
KV_LORA = D_MODEL // 4
ROPE_THETA = 10000.0
ATTN_SCALE = (QK_NOPE + QK_ROPE) ** -0.5
Q_BLOCK = 128

RWKV_HEAD = 64
RWKV_HEADS = D_MODEL // RWKV_HEAD
DECAY_LORA = 64
AAA_LORA = 64
GATE_LORA = 128
GN_EPS = 64e-5

kernel_name = 'mla_rwkv7_hybrid_step'

def rmsnorm(x, g):
    xf = x.astype(jnp.float32)
    y = xf * lax.rsqrt(jnp.mean(xf * xf, axis=-1, keepdims=True) + RMS_EPS)
    return (y * g.astype(jnp.float32)).astype(x.dtype)

def rope(x, pos):
    half = x.shape[-1] // 2
    inv_freq = ROPE_THETA ** (-jnp.arange(half, dtype=jnp.float32) / half)
    ang = pos.astype(jnp.float32)[:, None] * inv_freq[None, :]
    cos = jnp.cos(ang)[:, None, :]
    sin = jnp.sin(ang)[:, None, :]
    xf = x.astype(jnp.float32)
    x1, x2 = xf[..., :half], xf[..., half:]
    return jnp.concatenate([x1 * cos - x2 * sin, x2 * cos + x1 * sin], axis=-1).astype(x.dtype)

def mla_project(h, pos, w_qkv_a, q_a_norm, kv_a_norm, w_q_b, w_kv_b):
    B, T, _ = h.shape
    a = h @ w_qkv_a
    c_q = rmsnorm(a[..., :Q_LORA], q_a_norm)
    c_kv = rmsnorm(a[..., Q_LORA:Q_LORA + KV_LORA], kv_a_norm)
    k_pe = rope(a[..., Q_LORA + KV_LORA:][:, :, None, :], pos)[:, :, 0]
    q = (c_q @ w_q_b).reshape(B, T, MLA_HEADS, QK_NOPE + QK_ROPE)
    q_pe = rope(q[..., QK_NOPE:], pos)
    w_uk = w_kv_b.reshape(KV_LORA, MLA_HEADS, QK_NOPE + V_HEAD)[..., :QK_NOPE]
    q_lat = jnp.einsum('bthn,chn->bthc', q[..., :QK_NOPE], w_uk)
    return q_lat, q_pe, c_kv, k_pe

def mla_output(o_lat, w_kv_b, w_o):
    B, T = o_lat.shape[:2]
    w_uv = w_kv_b.reshape(KV_LORA, MLA_HEADS, QK_NOPE + V_HEAD)[..., QK_NOPE:]
    o = jnp.einsum('bthc,chv->bthv', o_lat, w_uv).reshape(B, T, MLA_HEADS * V_HEAD)
    return o @ w_o

def mla_prompt_attend(q_lat, q_pe, c_kv, k_pe):
    B, T = q_lat.shape[:2]
    n_blk = -(-T // Q_BLOCK)
    pad = n_blk * Q_BLOCK - T

    def blocks(t):
        t = jnp.pad(t, ((0, 0), (0, pad), (0, 0), (0, 0)))
        return jnp.moveaxis(t.reshape((B, n_blk, Q_BLOCK) + t.shape[2:]), 1, 0)

    key_pos = jnp.arange(T)

    def one_block(args):
        ql, qp, start = args
        s = jnp.einsum('bqhc,bsc->bhqs', ql, c_kv) + jnp.einsum('bqhr,bsr->bhqs', qp, k_pe)
        q_pos = start + jnp.arange(Q_BLOCK)
        s = jnp.where(key_pos[None, :] <= q_pos[:, None], s.astype(jnp.float32) * ATTN_SCALE, NEG_INF)
        p = jax.nn.softmax(s, axis=-1).astype(c_kv.dtype)
        return jnp.einsum('bhqs,bsc->bqhc', p, c_kv)

    o = lax.map(one_block, (blocks(q_lat), blocks(q_pe), jnp.arange(n_blk) * Q_BLOCK))
    o = jnp.moveaxis(o, 0, 1).reshape(B, n_blk * Q_BLOCK, MLA_HEADS, KV_LORA)
    return o[:, :T]

def mla_sample_attend(q_lat, q_pe, c_new, kpe_new, c_past, kpe_past):
    S = q_lat.shape[1]
    P = c_past.shape[1]
    s_past = jnp.einsum('bqhc,bpc->bhqp', q_lat, c_past) + jnp.einsum('bqhr,bpr->bhqp', q_pe, kpe_past)
    s_new = jnp.einsum('bqhc,bsc->bhqs', q_lat, c_new) + jnp.einsum('bqhr,bsr->bhqs', q_pe, kpe_new)
    causal = jnp.arange(S)[None, :] <= jnp.arange(S)[:, None]
    s_new = jnp.where(causal, s_new.astype(jnp.float32) * ATTN_SCALE, NEG_INF)
    s = jnp.concatenate([s_past.astype(jnp.float32) * ATTN_SCALE, s_new], axis=-1)
    p = jax.nn.softmax(s, axis=-1).astype(c_new.dtype)
    return (jnp.einsum('bhqp,bpc->bqhc', p[..., :P], c_past)
            + jnp.einsum('bhqs,bsc->bqhc', p[..., P:], c_new))

def _wkv_step(S, inp):
    r, w, k, v, a, b = inp
    sa = jnp.einsum('bhvk,bhk->bhv', S, a)
    S = S * w[:, :, None, :] + sa[..., None] * b[:, :, None, :] + v[..., None] * k[:, :, None, :]
    return S, jnp.einsum('bhvk,bhk->bhv', S, r)

def rwkv7_time_mix(h, shift_prev, wkv0, mu, w_r, w_k, w_v, w_o, dw0, dw1, dw2,
                   aw0, aw1, aw2, gw1, gw2, k_k, k_a, r_k, ln_w, ln_b):
    B, T, D = h.shape
    H, N = RWKV_HEADS, RWKV_HEAD
    x_prev = jnp.concatenate([shift_prev.astype(h.dtype)[:, None], h[:, :-1]], axis=1)
    xx = x_prev - h
    xr, xw, xk, xv, xa, xg = (h + xx * mu[j] for j in range(6))
    r = xr @ w_r
    k = xk @ w_k
    v = xv @ w_v
    log_w = -jax.nn.softplus(-(dw0 + jnp.tanh(xw @ dw1) @ dw2)) - 0.5
    a = jax.nn.sigmoid(aw0 + (xa @ aw1) @ aw2)
    g = jax.nn.sigmoid(xg @ gw1) @ gw2

    def heads(t):
        return t.astype(jnp.float32).reshape(B, T, H, N)

    kk = heads(k * k_k)
    kk = kk / jnp.maximum(jnp.sqrt(jnp.sum(kk * kk, axis=-1, keepdims=True)), 1e-12)
    k = heads(k * (1.0 + (a - 1.0) * k_a))
    r, v, a = heads(r), heads(v), heads(a)
    decay = jnp.exp(-jnp.exp(heads(log_w)))

    def tm(t):
        return jnp.moveaxis(t, 1, 0)

    S_T, y = lax.scan(_wkv_step, wkv0.astype(jnp.float32),
                      (tm(r), tm(decay), tm(k), tm(v), tm(-kk), tm(kk * a)))
    y = jnp.moveaxis(y, 0, 1)
    mean = jnp.mean(y, axis=-1, keepdims=True)
    var = jnp.mean(jnp.square(y - mean), axis=-1, keepdims=True)
    y = ((y - mean) * lax.rsqrt(var + GN_EPS)).reshape(B, T, D) * ln_w.astype(jnp.float32) + ln_b.astype(jnp.float32)
    y = y + (jnp.sum(r * k * r_k.astype(jnp.float32), axis=-1, keepdims=True) * v).reshape(B, T, D)
    out = (y.astype(h.dtype) * g) @ w_o
    return out, h[:, -1], S_T

def sq_relu_mlp(x, w_up, w_down):
    u = jax.nn.relu(x @ w_up)
    return (u * u) @ w_down

def setup_inputs(seed: int = 0) -> dict:
    key = jax.random.key(seed)
    ks = iter(jax.random.split(key, 48))
    f32 = jnp.float32

    def nrm(shape, scale=1.0):
        return jax.random.normal(next(ks), shape, f32) * scale

    def uni(shape, lo, hi):
        return jax.random.uniform(next(ks), shape, f32, lo, hi)

    n_pages = PAST_LEN // PAGE_SIZE
    pool_pages = (DEC_BATCH * n_pages * 5) // 4
    page_table = jax.random.permutation(next(ks), pool_pages)[:DEC_BATCH * n_pages]
    page_table = page_table.reshape(DEC_BATCH, n_pages).astype(jnp.int32)
    NA, NR, D = N_MLA_LAYERS, N_RWKV_LAYERS, D_MODEL
    H, N = RWKV_HEADS, RWKV_HEAD
    return dict(
        x_prompt=nrm((BATCH, SEQ, D)),
        x_sample=nrm((DEC_BATCH, DEC_SEQ, D)),
        cache_kv_latent=nrm((NA, pool_pages, PAGE_SIZE, KV_LORA)),
        cache_k_rope=nrm((NA, pool_pages, PAGE_SIZE, QK_ROPE)),
        state_wkv=nrm((NR, DEC_BATCH, H, N, N), 0.3),
        state_shift=nrm((NR, DEC_BATCH, D)),
        page_table=page_table,
        meta_tokens=nrm((N_META, D)),
        norm_mix=1.0 + nrm((DEPTH, D), 0.1),
        norm_ffn=1.0 + nrm((DEPTH, D), 0.1),
        norm_final=1.0 + nrm((D,), 0.1),
        mla_w_qkv_a=nrm((NA, D, Q_LORA + KV_LORA + QK_ROPE), D ** -0.5),
        mla_q_a_norm=1.0 + nrm((NA, Q_LORA), 0.1),
        mla_kv_a_norm=1.0 + nrm((NA, KV_LORA), 0.1),
        mla_w_q_b=nrm((NA, Q_LORA, MLA_HEADS * (QK_NOPE + QK_ROPE)), Q_LORA ** -0.5),
        mla_w_kv_b=nrm((NA, KV_LORA, MLA_HEADS * (QK_NOPE + V_HEAD)), KV_LORA ** -0.5),
        mla_w_o=nrm((NA, MLA_HEADS * V_HEAD, D), (MLA_HEADS * V_HEAD) ** -0.5),
        rwkv_mu=uni((NR, 6, D), 0.0, 1.0),
        rwkv_w_r=nrm((NR, D, D), D ** -0.5),
        rwkv_w_k=nrm((NR, D, D), D ** -0.5),
        rwkv_w_v=nrm((NR, D, D), D ** -0.5),
        rwkv_w_o=nrm((NR, D, D), D ** -0.5),
        rwkv_decay_w0=uni((NR, D), -6.0, 1.0),
        rwkv_decay_w1=nrm((NR, D, DECAY_LORA), D ** -0.5),
        rwkv_decay_w2=nrm((NR, DECAY_LORA, D), 0.5 * DECAY_LORA ** -0.5),
        rwkv_a_w0=nrm((NR, D), 0.5),
        rwkv_a_w1=nrm((NR, D, AAA_LORA), D ** -0.5),
        rwkv_a_w2=nrm((NR, AAA_LORA, D), 0.5 * AAA_LORA ** -0.5),
        rwkv_g_w1=nrm((NR, D, GATE_LORA), D ** -0.5),
        rwkv_g_w2=nrm((NR, GATE_LORA, D), GATE_LORA ** -0.5),
        rwkv_k_k=0.85 + nrm((NR, D), 0.1),
        rwkv_k_a=1.0 + nrm((NR, D), 0.1),
        rwkv_r_k=nrm((NR, H, N), 0.1),
        rwkv_ln_w=1.0 + nrm((NR, D), 0.1),
        rwkv_ln_b=nrm((NR, D), 0.02),
        ffn_w_up=nrm((DEPTH, D, D_FF), D ** -0.5),
        ffn_w_down=nrm((DEPTH, D_FF, D), D_FF ** -0.5),
    )

def reference(x_prompt, x_sample, cache_kv_latent, cache_k_rope, state_wkv, state_shift, page_table,
              meta_tokens, norm_mix, norm_ffn, norm_final,
              mla_w_qkv_a, mla_q_a_norm, mla_kv_a_norm, mla_w_q_b, mla_w_kv_b, mla_w_o,
              rwkv_mu, rwkv_w_r, rwkv_w_k, rwkv_w_v, rwkv_w_o,
              rwkv_decay_w0, rwkv_decay_w1, rwkv_decay_w2,
              rwkv_a_w0, rwkv_a_w1, rwkv_a_w2, rwkv_g_w1, rwkv_g_w2,
              rwkv_k_k, rwkv_k_a, rwkv_r_k, rwkv_ln_w, rwkv_ln_b,
              ffn_w_up, ffn_w_down):
    f32 = jnp.float32
    B = x_prompt.shape[0]
    DB = x_sample.shape[0]
    meta = jnp.broadcast_to(meta_tokens.astype(x_prompt.dtype)[None], (B, N_META, D_MODEL))
    hp = jnp.concatenate([meta, x_prompt], axis=1)
    hs = x_sample
    pos_p = jnp.arange(hp.shape[1])
    pos_s = PAST_LEN + jnp.arange(hs.shape[1])
    kv_lat_p, k_rope_p, kv_lat_s, k_rope_s = [], [], [], []
    wkv_p, shift_p, wkv_s, shift_s = [], [], [], []
    for i in range(DEPTH):
        n_p = rmsnorm(hp, norm_mix[i])
        n_s = rmsnorm(hs, norm_mix[i])
        l = i // N_MIXERS
        if i % N_MIXERS == 0:
            proj = (mla_w_qkv_a[l], mla_q_a_norm[l], mla_kv_a_norm[l], mla_w_q_b[l], mla_w_kv_b[l])
            ql, qp, c_p, kp_p = mla_project(n_p, pos_p, *proj)
            y_p = mla_output(mla_prompt_attend(ql, qp, c_p, kp_p), mla_w_kv_b[l], mla_w_o[l])
            ql, qp, c_s, kp_s = mla_project(n_s, pos_s, *proj)
            c_past = cache_kv_latent[l, page_table].reshape(DB, -1, KV_LORA)
            kp_past = cache_k_rope[l, page_table].reshape(DB, -1, QK_ROPE)
            y_s = mla_output(mla_sample_attend(ql, qp, c_s, kp_s, c_past, kp_past), mla_w_kv_b[l], mla_w_o[l])
            kv_lat_p.append(c_p)
            k_rope_p.append(kp_p)
            kv_lat_s.append(c_s)
            k_rope_s.append(kp_s)
        else:
            rw = (rwkv_mu[l], rwkv_w_r[l], rwkv_w_k[l], rwkv_w_v[l], rwkv_w_o[l],
                  rwkv_decay_w0[l], rwkv_decay_w1[l], rwkv_decay_w2[l],
                  rwkv_a_w0[l], rwkv_a_w1[l], rwkv_a_w2[l], rwkv_g_w1[l], rwkv_g_w2[l],
                  rwkv_k_k[l], rwkv_k_a[l], rwkv_r_k[l], rwkv_ln_w[l], rwkv_ln_b[l])
            zero_shift = jnp.zeros((B, D_MODEL), f32)
            zero_state = jnp.zeros((B, RWKV_HEADS, RWKV_HEAD, RWKV_HEAD), f32)
            y_p, sh_p, st_p = rwkv7_time_mix(n_p, zero_shift, zero_state, *rw)
            y_s, sh_s, st_s = rwkv7_time_mix(n_s, state_shift[l], state_wkv[l], *rw)
            wkv_p.append(st_p)
            shift_p.append(sh_p)
            wkv_s.append(st_s)
            shift_s.append(sh_s)
        hp = hp + y_p
        hs = hs + y_s
        hp = hp + sq_relu_mlp(rmsnorm(hp, norm_ffn[i]), ffn_w_up[i], ffn_w_down[i])
        hs = hs + sq_relu_mlp(rmsnorm(hs, norm_ffn[i]), ffn_w_up[i], ffn_w_down[i])
    y_prompt = rmsnorm(hp, norm_final)[:, N_META:]
    y_sample = rmsnorm(hs, norm_final)
    return (y_prompt, y_sample,
            jnp.stack(kv_lat_p), jnp.stack(k_rope_p), jnp.stack(kv_lat_s), jnp.stack(k_rope_s),
            jnp.stack(wkv_p), jnp.stack(shift_p), jnp.stack(wkv_s), jnp.stack(shift_s))


_drawn_inputs = setup_inputs


def setup_inputs(seed=0):
    import zlib

    import numpy as np

    out = dict(_drawn_inputs(seed))
    spreads = {}
    factors = {'mla_q_a_norm': 3.885, 'rwkv_ln_b': 8.0}
    for name, (base, spread) in spreads.items():
        noise = np.random.default_rng([zlib.crc32(name.encode()), seed]).standard_normal(out[name].shape)
        drawn = base * np.exp(spread * noise) if base else spread * noise
        out[name] = jnp.asarray(drawn.astype(out[name].dtype))
    for name, factor in factors.items():
        out[name] = (out[name] * factor).astype(out[name].dtype)
    return out
```

```python
from contextlib import ExitStack

import concourse.bass as bass
from concourse import mybir

F32 = mybir.dt.float32
F32R = mybir.dt.float32r
I32 = mybir.dt.int32
ALU = mybir.AluOpType
ACT = mybir.ActivationFunctionType
AX = mybir.AxisListType.X

P = 128
D = 1024
KT = D // P
NMETA, SEQ = 16, 1024
NP = NMETA + SEQ
DB, DS = 8, 4
ND = DB * DS
T = NP + ND
PIECES = [(0, 384), (384, 384), (768, T - 768)]
NT = 9
TAIL = T - 8 * P
EPS = 1e-6
NEG = -1e30

H, NOPE, ROPE, VH = 8, 128, 64, 128
QL, KVL = 384, 256
SCALE = float((NOPE + ROPE) ** -0.5)
QT = 104
NQ = NP // QT
PAST, PAGE = 2048, 128
NPG = PAST // PAGE
POOL = DB * NPG * 5 // 4
FF = 4096
FG = 256
NG = FF // FG

RH, RN = 16, 64
W_SCALE = float(2.718281828459045 ** -0.5)
GN_EPS = 64e-5
CH = 128
LEVELS = 7
ATT_A = sum(-(-(q + 1) // 4) for q in range(NQ))
ATT_V = ATT_A + NQ
DVE_HEADS = 44
DVE_SAMPLES = 4
DVE_CHUNK = 27

R_MIX, R_FFN, R_FIN, R_MU, R_DW0, R_AW0, R_KK, R_KA, R_RK, R_QN, R_KVN, R_SHIFT = 0, 2, 4, 5, 11, 12, 13, 14, 15, 16, 17, 18
NROW = R_SHIFT + DB

def columns(*parts):
    at, out = 0, {}
    for name, n in parts:
        out[name] = (at, n)
        at += n
    return out, at


TABLE, NTABLE = columns(("ident", P), ("ones", P), ("halves", P), ("rot", P), ("causal", QT), ("new_keys", DB * ND))
MIXTAB, NMIXTAB = columns(("below", P), ("upto", P), ("tail_below", TAIL), ("tail_upto", TAIL), ("first_pairs", P),
                          ("siblings", 6 * P), ("restart", 8 * P), ("tail_restart", TAIL), ("seq_rows", 9),
                          ("seq_cols", 9 * TAIL), ("head_cols", 2))


class Tally:

    def __init__(self, sem, n=0):
        self.sem, self.n, self.i, self.step, self.start = sem, n, None, 0, 0

    def enter(self, i, step):
        self.i, self.step, self.start = i, step, self.n

    def leave(self, reps, name="", ring=1):
        assert self.step % ring == 0
        assert self.n - self.start == self.step, f"{name} step is {self.n - self.start}"
        self.i, self.n = None, self.start + reps * self.step

    def value(self, back=0):
        v = self.n - back
        return v if self.i is None or not self.step else self.i * self.step + v

    def add(self, ins, by=1):
        ins.then_inc(self.sem, by)
        self.n += by
        return ins

    def expect(self, by=1):
        self.n += by


class Fill:

    def __init__(self, eng, banks, filled, drained):
        self.eng, self.banks, self.filled, self.drained = eng, banks, Tally(filled), drained

    def bank(self, free=False):
        n = self.filled.n
        if n >= len(self.banks) and not free:
            self.eng.wait_ge(self.drained, self.filled.value(len(self.banks) - 1))
        return self.banks[n % len(self.banks)]

    def done(self, ins):
        self.filled.add(ins)

    def wait_drained(self, back=0):
        self.eng.wait_ge(self.drained, self.filled.value(back))


class Beat:

    def __init__(self, sem, per=1):
        self.sem, self.per, self.tally = sem, per, None

    def wait(self, eng, chunk, n=None):
        eng.wait_ge(self.sem, chunk * self.per + (self.per if n is None else n))


class Drain:

    def __init__(self, eng, banks, filled, drained):
        self.eng, self.banks, self.filled, self.drained = eng, banks, filled, Tally(drained)

    def bank(self):
        self.eng.wait_ge(self.filled, self.drained.value(-1))
        return self.banks[self.drained.n % len(self.banks)]


class Lane:

    def __init__(self, eng, order):
        self.eng, self.order, self.last = eng, Tally(order), None

    def do(self, ins, tally=None):
        self.last = self.order if tally is None else tally
        self.last.add(ins)

    def settle(self):
        self.eng.wait_ge(self.last.sem, self.last.value())


def program(nc, A, O):
    ctx = ExitStack()
    with ctx:
        def sb(name, shape, dt=F32):
            return ctx.enter_context(nc.sbuf_tensor(name, shape, dt))

        def sem(name):
            return ctx.enter_context(nc.semaphore(name))

        banks = [ctx.enter_context(nc.psum_tensor(f"bank{i}", [P, 512], F32)) for i in range(8)]
        BA, BV = banks[0:4], banks[4:8]

        hT = sb("hT", [P, KT, T])
        table = sb("table", [P, NTABLE])
        prm = sb("prm", [P, KT, NROW])
        std = sb("std", [P, T])
        eps = sb("eps", [P, 2])
        ARENA = 42300
        with ExitStack() as place:
            def piece(name, shape, dt=F32R):
                return place.enter_context(nc.sbuf_tensor(name, shape, dt))

            n_hi, n_lo = piece("n_hi", [P, KT, T]), piece("n_lo", [P, KT, T])
            with nc.sbuf_tensor("n32", [P, KT, T], F32) as n32:
                pass
            u_hi, u_lo = piece("u_hi", [P, 2, T]), piece("u_lo", [P, 2, T])
            up_hi, up_lo = piece("up_hi", [P, KT, FG]), piece("up_lo", [P, KT, FG])
            dn_hi, dn_lo = piece("dn_hi", [P, 2, D]), piece("dn_lo", [P, 2, D])
        SPLIT = 2 * (KT + 2) * T + 4 * KT * FG
        arena = sb("arena", [P, ARENA])

        class Carve:

            def __init__(self, at=0):
                self.at = at

            def __call__(self, *dims):
                n = 1
                for d in dims:
                    n *= d
                v = arena[:, self.at:self.at + n]
                self.at += n
                assert self.at <= ARENA, self.at
                if len(dims) == 1:
                    return v
                names = "abcde"[:len(dims)]
                pattern = f"p ({' '.join(names)}) -> p {' '.join(names)}"
                return v.rearrange(pattern, **{k: d for k, d in zip(names[1:], dims[1:])})

        def tab(name, rows=P):
            at, n = TABLE[name]
            return table[0:rows, at:at + n]

        ident, ones, halves, rot = tab("ident"), tab("ones"), tab("halves"), tab("rot")

        c = Carve()
        nT = c(KT, T)
        c_in = Carve(c.at)
        xin = c_in(NT, D)
        rows_in = c_in(D)
        m = Carve(c.at)
        oT = m(KT, T)
        cq = m(3, T)
        ckv = m(2, T)
        kraw = m(T)
        kfull = m(T)
        kz = m(2, T)
        cosT = m(T)
        sinT = m(T)
        qlat = m(3, DB, H * DS)
        olT = m(2, H, DB, DS)
        wa = Carve(m.at)(KT, 768)
        n2 = Carve()
        ctok = n2(NQ + 1, KVL + ROPE)
        n3 = Carve(n2.at)
        qraw = n3(T)
        rtmp = n3(T)
        vtok = n3(NQ * VH)
        m2 = Carve(m.at)
        wq = m2(3, 384)
        wqp = m2(3, P)
        wkv = m2(2, 512)
        wukT = m2(2 * P)
        qpe = m2(T)
        qn = [m2(T) for _ in range(2)]
        kn = [m2(T) for _ in range(2)]
        probs = [m2(NP) for _ in range(2)]
        stat = m2(2, 4)
        pT = [m2(NQ * QT), n3(NQ * QT)]
        assert n3.at <= c.at
        n4 = Carve(n2.at)
        cT = [n4(3, 512) for _ in range(2)]
        pTd = n4(NPG + 1, ND)
        qcur = n4(3, ND)
        ol = n4(KVL)
        dstat = n4(4)
        assert n4.at <= c.at
        m3 = Carve(m.at)
        dlat = [m3(NPG, KVL) for _ in range(2)]
        drope = [m3(NPG, P), Carve(c.at + (KT + 9) * T)(NPG, P)]
        sd = Carve(c.at + KT * T)(PAST + ND)
        wv = Carve(c.at + (KT + 7) * T)(2, H, VH)
        wo = Carve(m.at)(KT, D)
        f = Carve(SPLIT)
        w_up = [f(KT, FG) for _ in range(2)]
        w_dn = [f(2, D) for _ in range(2)]
        relu = [f(384) for _ in range(4)]
        g = Carve(c.at)
        lora = g(T)
        gate = g(T)
        xm = [g(KT, T) for _ in range(2)]
        wb = [g(KT, 256) for _ in range(2)]
        wl = g(KT, P)
        wg = g(KT, P)
        stage = [g(NT * 256) for _ in range(2)]
        shift_out = stage[0][0:9, 0:D]
        q = Carve(c.at + 2 * T)
        zT = nT
        mixtab = q(NMIXTAB)
        w_dec, w_rate, w_gate = q(D), q(D), q(D)
        lnw, lnb = q(D), q(D)
        S, Sm = q(8, P), q(8, P)
        rc, kc, vt = q(8, P), q(8, P), q(D)
        AR = q(8, 2, P)
        Bt, Kt = q(8, P), q(8, P)
        Bz, Kz = q(8, 2, P), q(8, 2, P)
        Btok, Ktok = q(D), q(D)
        sw, rate, pinc, pinv, cum, kk, kx = [q(8, P) for _ in range(7)]
        y = q(D)
        hx = hT[:, :, :].rearrange("p k t -> p (k t)")
        MR = [hx[:, i * 1024:(i + 1) * 1024] for i in range(2)]
        NR = [hx[:, (2 + i) * 1024:(3 + i) * 1024] for i in range(2)]
        XT = [hx[:, (8 + i) * 512:(9 + i) * 512] for i in range(2)]
        X = [hx[:, (10 + i) * 512:(11 + i) * 512] for i in range(2)]
        W = [hx[:, (12 + i) * 512:(13 + i) * 512] for i in range(2)]
        small = hx[:, 16 * 512:KT * T]
        coef, mean, var, mid, dmid, dend = [small[:, i * 16:(i + 1) * 16] for i in range(6)]
        gc = small[:, 96:96 + P]

        def mix(name, rows=P):
            at, n = MIXTAB[name]
            return mixtab[0:rows, at:at + n]

        P1, SA = [t.rearrange("p k t -> p (k t)") for t in (cum, kk)]
        Bm, Km = [t.rearrange("p k t -> p (k t)") for t in (rate, pinv)]
        wo2 = Carve(q.at - KT * D)(KT, D)
        mixw_n = 6 * 16
        out_n = 4 * 16

        yout = Carve(c.at)(NT, D)

        meet_s = sem("all_engines_here")
        a_filled, a_drained = sem("a_filled"), sem("a_drained")
        v_filled, v_drained = sem("v_filled"), sem("v_drained")
        act_order, dve_order = sem("act_order"), sem("dve_order")
        mark = {}
        in_s, rows_s, zero_s = sem("tables_loaded"), sem("rows_loaded"), sem("zeroed")
        sq_s, norm_s = sem("squares_ready"), sem("normed_ready")
        wa_s, rope_s, kz_s = sem("w_a_loaded"), sem("roped"), sem("kz_ready")
        out_s, eps_s = sem("stored"), sem("eps_ready")
        wq_s, wq_used, wkv_used = sem("w_q_loaded"), sem("w_q_used"), sem("w_kv_used")
        max_s, exp_s, prob_s = sem("max_ready"), sem("exp_ready"), sem("probs_ready")
        page_s = [sem(f"pages_loaded{i}") for i in range(2)]
        page_used, pt_s, qcur_s = sem("pages_used"), sem("page_table_loaded"), sem("q_copied")
        wo_s, narrow_s = sem("w_o_loaded"), sem("narrow_waits")
        up_s = [sem(f"w_up_loaded{i}") for i in range(2)]
        dn_s = [sem(f"w_down_loaded{i}") for i in range(2)]
        u_s, hi_s, lo_s = sem("u_ready"), sem("weights_rounded"), sem("weights_split")
        nhi_s, nlo_s = sem("normed_rounded"), sem("normed_split")
        pages = ctx.enter_context(nc.sbuf_tensor("pages", [1, DB * NPG], I32))

        hid_s = sem("hidden_stored")
        xm_s, xm_used = sem("mixed_ready"), sem("mixed_used")
        wb_s = [sem(f"w_mix_loaded{i}") for i in range(2)]
        wb_used, wl_s, stg_s = sem("w_mix_used"), sem("w_lora_loaded"), [sem(f"staged_stored{i}") for i in range(2)]
        chunk_in = Beat(sem("chunk_loaded"), 48)
        rkv_free = Beat(sem("chunk_inputs_used"))
        sw_b, rate_b, cum_b, dec_b = Beat(sem("decay_rates")), Beat(sem("rates")), Beat(sem("decay_sums")), Beat(sem("decays"))
        cumx_b, decx_b, kk_b, sq_b = Beat(sem("sums_before")), Beat(sem("decays_before")), Beat(sem("keys_scaled")), Beat(sem("keys_squared"))
        clamp_b, root_b, ab_b, bk_b = Beat(sem("norms_clamped")), Beat(sem("norms")), Beat(sem("a_r_ready")), Beat(sem("b_k_ready"))
        split_b, bonus_b, gc_b, x1_b = Beat(sem("b_k_split")), Beat(sem("bonus_ready")), Beat(sem("gate_copied")), Beat(sem("first_inverse"), 4)
        yc_b, ysq_b, var_b, ystd_b, z_b = Beat(sem("centred")), Beat(sem("centred_squared")), Beat(sem("variances")), Beat(sem("deviations")), Beat(sem("z_ready"))
        s_b = Beat(sem("state_scaled"))
        mixw_s, z_used = sem("mix_tables_loaded"), Beat(sem("z_turned"))
        st_in, st_used, st_ready, st_s2 = sem("state_loaded"), sem("state_in_used"), sem("state_turned"), sem("state_stored")
        arm_s, arm_used, bm_s, bm_used, snew_s = sem("queries_masked"), sem("masked_used"), sem("keys_masked"), sem("keys_masked_used"), sem("state_new")
        wo2_s = sem("w_out_loaded")
        r_d = nc.dram_tensor("r_scratch", (NT, P, 8, P), F32).ap()
        k_d = nc.dram_tensor("k_scratch", (NT, P, 8, P), F32).ap()
        v_d = nc.dram_tensor("v_scratch", (NT, P, D), F32).ap()
        h_d = nc.dram_tensor("hidden_scratch", (P, KT * T), F32).ap()

        def meet(eng, here):
            here.add(eng.drain())
            here.n += 4
            eng.wait_ge(meet_s, here.n)

        block = ctx.enter_context(nc.Block())

        @block.tensor
        def _(pe):
            here = Tally(meet_s)
            ra = Fill(pe, BA, a_filled, a_drained)
            rv = Fill(pe, BV, v_filled, v_drained)
            sq_t, norm_t = Tally(sq_s), Tally(norm_s)
            wq_t, wkv_t, prob_t = Tally(wq_s), Tally(wkv_used), Tally(prob_s)
            wo_t = Tally(wo_s)

            def mm(out, lhsT, rhs, first, last, group=False):
                return pe.matmul(out, lhsT, rhs, start=first, stop=last, skip_group_check=group)

            def apart(semaphore, value):
                pe.wait_ge(semaphore, value)
                pe.sem_inc(narrow_s, 1)

            def turn(out, src, rows):
                return pe.transpose(out, src, ident[0:rows, 0:rows])

            def norm(scratch, n):
                for at, w in PIECES:
                    sq_t.expect()
                    pe.wait_ge(sq_s, sq_t.n)
                    b = ra.bank()
                    for k in range(n):
                        ins = mm(b[:, 0:w], ones, scratch[:, k, at:at + w], k == 0, k == n - 1)
                    ra.done(ins)

            def normed():
                norm_t.expect(3)
                pe.wait_ge(norm_s, norm_t.n)

            def product(ring, weights, acts, n, m=P, at=0, w=P):
                b = ring.bank()
                for k in range(n):
                    ins = mm(b[0:m, 0:w], weights(k), acts(k), k == 0, k == n - 1)
                ring.done(ins)

            pe.wait_ge(in_s, 192)
            pe.wait_ge(rows_s, 192)
            b = rv.bank()
            for k in range(KT):
                ins = turn(b[:, k * NROW:(k + 1) * NROW], rows_in[0:NROW, k * P:(k + 1) * P], NROW)
            rv.done(ins)
            for t in range(NT):
                w = P if t < 8 else TAIL
                for half, ring in enumerate((ra, rv)):
                    b = ring.bank()
                    for k in range(4):
                        ins = turn(b[:, k * w:(k + 1) * w], xin[0:w, t, (4 * half + k) * P:(4 * half + k + 1) * P], w)
                    ring.done(ins)
            meet(pe, here)

            mark["norm0"] = ra.filled.n
            norm(nT, KT)
            normed()
            pe.wait_ge(wa_s, 64)
            mark["down"] = rv.filled.n
            for k in range(6):
                for at, w in PIECES:
                    product(ra if k < 3 else rv, lambda j: wa[:, j, k * P:(k + 1) * P],
                            lambda j: nT[:, j, at:at + w], KT, w=w)
            mark["norm_q"] = ra.filled.n
            norm(oT, 3)
            rv.wait_drained()
            for at, w in PIECES:
                product(rv, lambda j: rot, lambda j: kraw[:, at:at + w], 1, w=w)
            norm(oT[:, 3:5, :], 2)
            norm_t.expect(3)
            normed()
            meet(pe, here)
            mark["latents"] = ra.filled.n
            for t in range(NQ + 1):
                w = QT if t < NQ else ND
                b = ra.bank()
                for k in range(2):
                    turn(b[0:w, k * P:(k + 1) * P], ckv[:, k, t * QT:t * QT + w], P)
                ra.done(turn(b[0:w, KVL:KVL + ROPE], kfull[0:ROPE, t * QT:t * QT + w], ROPE))
            with pe.Fori(0, H // 2) as i:
                ra.filled.enter(i, 2 * (8 + ATT_A))
                rv.filled.enter(i, 6 + 2 * (3 + ATT_V))
                prob_t.enter(i, 2 * NQ)
                wq_t.enter(i, 64)
                wkv_t.enter(i, 1)
                wq_t.expect(64)
                pe.wait_ge(wq_s, wq_t.value())
                for at, w in PIECES:
                    product(rv, lambda j: wqp[:, j, :], lambda j: cq[:, j, at:at + w], 3, w=w)
                rv.wait_drained()
                for at, w in PIECES:
                    product(rv, lambda j: rot, lambda j: qraw[:, at:at + w], 1, w=w)
                for hh in range(2):
                    for at, w in PIECES:
                        product(ra, lambda j: wq[:, j, hh * 192:hh * 192 + NOPE], lambda j: cq[:, j, at:at + w], 3, w=w)
                        product(rv, lambda j: wkv[:, j, hh * 256:hh * 256 + NOPE], lambda j: ckv[:, j, at:at + w], 2, w=w)
                    for t0, n in [(0, 4), (4, 4), (8, 2)]:
                        b = ra.bank()
                        for t in range(n):
                            for k in range(2):
                                ins = mm(b[0:QT, t * VH:(t + 1) * VH], ckv[:, k, (t0 + t) * QT:(t0 + t + 1) * QT],
                                         wkv[:, k, hh * 256 + NOPE:(hh + 1) * 256], k == 0, k == 1)
                        ra.done(ins)
                    b = ra.bank()
                    for k in range(2):
                        ins = turn(b[:, k * P:(k + 1) * P], wkv[:, k, hh * 256:hh * 256 + NOPE], P)
                    ra.done(ins)
                    ra.wait_drained()
                    rv.wait_drained()
                    b = ra.bank()
                    for k in range(2):
                        ins = mm(b[:, k * ND:(k + 1) * ND], wukT[:, k * P:(k + 1) * P], qn[hh][:, NP:T], True, True)
                    ra.done(ins)
                    if hh == 1:
                        wkv_t.add(pe.drain())

                    def scores(q):
                        for j in range(0, q + 1, 4):
                            n = min(4, q + 1 - j)
                            b = rv.bank()
                            mm(b[0:QT, 0:n * QT], qn[hh][:, q * QT:(q + 1) * QT], kn[hh][:, j * QT:(j + n) * QT], True, False)
                            rv.done(mm(b[0:QT, 0:n * QT], qpe[:, q * QT:(q + 1) * QT], kz[:, hh, j * QT:(j + n) * QT],
                                       False, True))

                    def turn_probs(q):
                        prob_t.expect()
                        pe.wait_ge(prob_s, prob_t.value())
                        for j in range(0, q + 1, 4):
                            n = min(4, q + 1 - j)
                            b = ra.bank()
                            for t in range(n):
                                ins = turn(b[0:QT, t * QT:(t + 1) * QT], probs[q % 2][0:QT, (j + t) * QT:(j + t + 1) * QT], QT)
                            ra.done(ins)

                    def values(q):
                        ra.wait_drained()
                        b = rv.bank()
                        for j in range(q + 1):
                            ins = mm(b[:, 0:QT], vtok[0:QT, j * VH:(j + 1) * VH], pT[q % 2][0:QT, j * QT:(j + 1) * QT],
                                     j == 0, j == q)
                        rv.done(ins)

                    for q in range(NQ + 2):
                        if q < NQ:
                            scores(q)
                        if q >= 2:
                            values(q - 2)
                        if 1 <= q <= NQ:
                            turn_probs(q - 1)
                ra.filled.leave(4, "pe heads a")
                rv.filled.leave(4, "pe heads v")
                prob_t.leave(4)
                wq_t.leave(4)
                wkv_t.leave(4)
            meet(pe, here)
            mark["samples"] = rv.filled.n
            page_t = [Tally(s) for s in page_s]
            used_t, qcur_t = Tally(page_used), Tally(qcur_s)
            with pe.Fori(0, DB // 2) as i:
                ra.filled.enter(i, 2 * 16)
                rv.filled.enter(i, 2 * 6)
                prob_t.enter(i, 2)
                used_t.enter(i, 2)
                qcur_t.enter(i, 2)
                for par in range(2):
                    page_t[par].enter(i, 48 * NPG)
                    page_t[par].expect(48 * NPG)
                    pe.wait_ge(page_s[par], page_t[par].value())
                    qcur_t.expect()
                    pe.wait_ge(qcur_s, qcur_t.value())

                    def turn_pages(n):
                        for k in range(3):
                            b = ra.bank()
                            for g in range(4):
                                src = dlat[par][:, 4 * n + g, k * P:(k + 1) * P] if k < 2 else drope[par][:, 4 * n + g, :]
                                ins = turn(b[:, g * P:(g + 1) * P], src, P)
                            ra.done(ins)

                    def score(rhs, w):
                        b = rv.bank()
                        for k in range(3):
                            ins = mm(b[0:ND, 0:w], qcur[:, k, :], rhs(k), k == 0, k == 2)
                        rv.done(ins)

                    turn_pages(0)
                    for n in range(4):
                        ra.wait_drained()
                        if n < 3:
                            turn_pages(n + 1)
                        score(lambda k: cT[n % 2][:, k, :], 512)
                    score(lambda k: ckv[:, k, NP:T] if k < 2 else kfull[:, NP:T], ND)
                    prob_t.expect()
                    apart(exp_s, prob_t.value())
                    for half in range(2):
                        b = ra.bank(free=True)
                        for n in range(NPG // 2):
                            at = (half * (NPG // 2) + n) * P
                            ins = turn(b[:, n * ND:(n + 1) * ND], sd[0:ND, at:at + P], ND)
                        ra.done(ins)
                    b = ra.bank(free=True)
                    ra.done(turn(b[0:ND, 0:ND], sd[0:ND, PAST:PAST + ND], ND))
                    ra.wait_drained()
                    b = rv.bank()
                    for n in range(NPG):
                        mm(b[0:ND, 0:KVL], pTd[:, n, :], dlat[par][:, n, :], n == 0, False)
                    rv.done(mm(b[0:ND, 0:KVL], pTd[0:ND, NPG, :], ctok[0:ND, NQ, 0:KVL], False, True))
                    used_t.add(pe.drain())
                    apart(v_drained, rv.filled.value())
                    b = ra.bank(free=True)
                    for k in range(2):
                        ins = turn(b[:, k * ND:(k + 1) * ND], ol[0:ND, k * P:(k + 1) * P], ND)
                    ra.done(ins)
                for t in (ra.filled, rv.filled, prob_t, used_t, qcur_t, page_t[0], page_t[1]):
                    t.leave(4, "pe samples")
            ra.wait_drained()
            pe.wait_ge(wo_s, 32)
            for h in range(H):
                product(rv, lambda j: wv[:, j, h, :], lambda j: olT[:, j, h, :, :].rearrange("p b q -> p (b q)"), 2, w=ND)
            meet(pe, here)
            pe.wait_ge(wo_s, 48)
            for k in range(KT):
                for at, w in PIECES:
                    product(rv, lambda j: wo[:, j, k * P:(k + 1) * P], lambda j: oT[:, j, at:at + w], H, w=w)
            meet(pe, here)

            u_t, lo_t, nlo_t = Tally(u_s), Tally(lo_s), Tally(nlo_s)

            def product3(ring, weights, acts, n, w):
                (w_hi, w_lo), (x_hi, x_lo) = weights, acts
                b = ring.bank()
                for k in range(n):
                    mm(b[:, 0:w], w_hi(k), x_hi(k), k == 0, False)
                    mm(b[:, 0:w], w_hi(k), x_lo(k), False, False)
                    ins = mm(b[:, 0:w], w_lo(k), x_hi(k), False, k == n - 1)
                ring.done(ins)

            def feed(layer):
                mark[f"feed_norm{layer}"] = ra.filled.n
                norm(n32, KT)
                nlo_t.expect(3)
                pe.wait_ge(nlo_s, nlo_t.n)
                norm_t.expect(3)
                mark[f"feed{layer}"] = ra.filled.n
                mark[f"feed_v{layer}"] = rv.filled.n
                u_t.expect(4)
                with pe.Fori(0, NG // 2) as i:
                    ra.filled.enter(i, 12)
                    rv.filled.enter(i, 48)
                    u_t.enter(i, 12)
                    lo_t.enter(i, 4)
                    for par in range(2):
                        lo_t.expect()
                        pe.wait_ge(lo_s, lo_t.value())
                        for k in range(2):
                            cols = slice(k * P, (k + 1) * P)
                            for at, w in PIECES:
                                product3(ra, (lambda j: up_hi[:, j, cols], lambda j: up_lo[:, j, cols]),
                                         (lambda j: n_hi[:, j, at:at + w], lambda j: n_lo[:, j, at:at + w]), KT, w)
                                u_t.expect()
                        lo_t.expect()
                        pe.wait_ge(lo_s, lo_t.value())
                        pe.wait_ge(u_s, u_t.value())
                        for k in range(KT):
                            cols = slice(k * P, (k + 1) * P)
                            for at, w in PIECES:
                                product3(rv, (lambda j: dn_hi[:, j, cols], lambda j: dn_lo[:, j, cols]),
                                         (lambda j: u_hi[:, j, at:at + w], lambda j: u_lo[:, j, at:at + w]), 2, w)
                    ra.filled.leave(NG // 2, "pe feed a", 4)
                    rv.filled.leave(NG // 2, "pe feed v", 4)
                    u_t.leave(NG // 2)
                    lo_t.leave(NG // 2)

            feed(0)
            meet(pe, here)
            mark["norm1"] = ra.filled.n
            norm(nT, KT)
            normed()
            mark["shift"] = ra.filled.n
            for half in range(2):
                b = ra.bank()
                for k in range(4):
                    ins = turn(b[0:9, k * P:(k + 1) * P], nT[:, 4 * half + k, NP - 1:T:DS], P)
                ra.done(ins)
            mark["mixing"] = ra.filled.n
            wb_t, xm_t, xu_t, wbu_t = [Tally(s) for s in wb_s], Tally(xm_s), Tally(xm_used), Tally(wb_used)
            pe.wait_ge(wl_s, 48)

            def mixed(n):
                xm_t.expect()
                pe.wait_ge(xm_s, xm_t.n)
                return xm[n % 2]

            def through(tally):
                tally.add(pe.drain())

            def lora_in(n, weights):
                x = mixed(n)
                for at, w in PIECES:
                    product(ra, lambda j: weights[:, j, :], lambda j: x[:, j, at:at + w], KT, w=w)
                through(xu_t)

            def big(n, token_major):
                x = mixed(n)
                with pe.Fori(0, 2) as i:
                    ra.filled.enter(i, 12)
                    wbu_t.enter(i, 2)
                    for par in range(2):
                        wb_t[par].enter(i, 16)
                        wb_t[par].expect(16)
                        pe.wait_ge(wb_s[par], wb_t[par].value())
                        if token_major:
                            for tiles in [(0, 1), (2, 3), (4, 5), (6,), (7,), (8,)]:
                                b = ra.bank()
                                for u, t in enumerate(tiles):
                                    w = P if t < 8 else TAIL
                                    for k in range(KT):
                                        ins = mm(b[0:w, u * 256:(u + 1) * 256], x[:, k, t * P:t * P + w], wb[par][:, k, :],
                                                 k == 0, k == KT - 1)
                                ra.done(ins)
                        else:
                            for m_ in range(2):
                                for at, w in PIECES:
                                    product(ra, lambda j: wb[par][:, j, m_ * P:(m_ + 1) * P], lambda j: x[:, j, at:at + w],
                                            KT, w=w)
                        through(wbu_t)
                        wb_t[par].leave(2)
                    ra.filled.leave(2, "pe big", 4)
                    wbu_t.leave(2)
                through(xu_t)

            big(0, False)
            lora_in(1, wl)
            big(2, False)
            lora_in(3, wl)
            big(4, True)
            lora_in(5, wg)
            meet(pe, here)
            pe.wait_ge(mixw_s, mixw_n)
            pe.wait_ge(zero_s, 2)
            mark["chunks_a"], mark["chunks_v"] = ra.filled.n, rv.filled.n

            def elementwise_part(c, at, w):
                for wt in (w_dec, w_rate):
                    for half in range(2):
                        b = ra.bank()
                        for k in range(4):
                            ins = mm(b[:, k * w:(k + 1) * w], wt[:, (4 * half + k) * P:(4 * half + k + 1) * P],
                                     lora[:, bass.ds(at, w)], True, True)
                        ra.done(ins)
                sq_b.wait(pe, c)
                for half in range(2):
                    b = rv.bank()
                    for k in range(4):
                        ins = mm(b[:, k * w:(k + 1) * w], halves, kx[:, 4 * half + k, 0:w], True, True)
                    rv.done(ins)
                bk_b.wait(pe, c)
                for src in (Bt, Kt):
                    for half in range(2):
                        b = ra.bank()
                        for k in range(4):
                            ins = turn(b[0:w, k * P:(k + 1) * P], src[:, 4 * half + k, 0:w], P)
                        ra.done(ins)
                bonus_b.wait(pe, c)
                mark["coef"] = ra.filled.n - ra.filled.start
                for half in range(2):
                    b = ra.bank()
                    for k in range(4):
                        ins = mm(b[0:w, 2 * k:2 * k + 2], kx[:, 4 * half + k, 0:w], mix("head_cols"), True, True)
                    ra.done(ins)

            def inverses(c, first, hg, w, levels):
                hb = hg // 2
                if first == 0:
                    split_b.wait(pe, c)
                    ab_b.wait(pe, c)
                for gi in range(2):
                    for src in (Bz, Kz):
                        for half in range(2):
                            b = rv.bank()
                            for j in range(hb):
                                h = first + gi * hg + half * hb + j
                                ins = mm(b[0:w, j * 2 * w:(j + 1) * 2 * w].rearrange("p (a w) -> p a w", a=2),
                                         src[:, h // 2, h % 2, 0:w], AR[:, h // 2, :, 0:w], True, True)
                            rv.done(ins)

                def mat(m, gi, j):
                    return m[gi][0:w, j * w:(j + 1) * w]

                def turn_group(gi):
                    b = ra.bank()
                    for j in range(hg):
                        ins = turn(b[0:w, j * w:(j + 1) * w], mat(XT, gi, j), w)
                    ra.done(ins)

                for gi in range(2):
                    x1_b.wait(pe, c, first // hg + gi + 1)
                    turn_group(gi)
                for l in range(1, levels):
                    for gi in range(2):
                        ra.wait_drained(1 - gi)
                        b = rv.bank()
                        for j in range(hg):
                            ins = mm(b[0:w, j * w:(j + 1) * w], MR[gi][0:w, j * 2 * w:j * 2 * w + w], mat(X, gi, j), True, True)
                        rv.done(ins)
                    for gi in range(2):
                        rv.wait_drained(1)
                        b = rv.bank()
                        for j in range(hg):
                            ins = mm(b[0:w, j * w:(j + 1) * w], mat(W, gi, j), mat(XT, gi, j), True, True)
                        rv.done(ins)
                    if l < levels - 1:
                        for gi in range(2):
                            rv.wait_drained(1 - gi)
                            turn_group(gi)
                rv.wait_drained()

            def chunk(c, at):
                w = P
                chunk_in.wait(pe, c)
                elementwise_part(c, at, w)
                for d in range(2):
                    inverses(c, 8 * d, 4, w, LEVELS)
                    s_b.wait(pe, c)
                    b = ra.bank()
                    for k in range(4):
                        mm(b[:, k * P:(k + 1) * P], AR[:, 4 * d + k, 0, :], Sm[:, 4 * d + k, :], k == 0, False, True)
                    for j in range(8):
                        h = 8 * d + j
                        ins = mm(b[:, j * RN:(j + 1) * RN], NR[j // 4][:, (j % 4) * 2 * P:(j % 4) * 2 * P + P],
                                 vt[:, h * RN:(h + 1) * RN], False, j == 7, True)
                    ra.done(ins)
                    ra.wait_drained()
                    b = ra.bank()
                    for j in range(8):
                        h = 8 * d + j
                        ins = mm(b[:, j * RN:(j + 1) * RN], XT[j // 4][:, (j % 4) * P:(j % 4 + 1) * P],
                                 P1[:, h * RN:(h + 1) * RN], True, True)
                    ra.done(ins)
                    ra.wait_drained()
                    b = rv.bank()
                    for k in range(4):
                        ct = 4 * d + k
                        mm(b[:, k * P:(k + 1) * P], Btok[:, ct * P:(ct + 1) * P], SA[:, ct * P:(ct + 1) * P], True, False)
                        ins = mm(b[:, k * P:(k + 1) * P], Ktok[:, ct * P:(ct + 1) * P], vt[:, ct * P:(ct + 1) * P], False, True)
                    rv.done(ins)
                    b = ra.bank()
                    for k in range(4):
                        mm(b[:, k * P:(k + 1) * P], AR[:, 4 * d + k, 1, :], Sm[:, 4 * d + k, :], k == 0, False, True)
                    for j in range(8):
                        h = 8 * d + j
                        m_at = (j % 4) * 2 * P + P
                        mm(b[:, j * RN:(j + 1) * RN], MR[j // 4][:, m_at:m_at + P], SA[:, h * RN:(h + 1) * RN], False, False, True)
                        ins = mm(b[:, j * RN:(j + 1) * RN], NR[j // 4][:, m_at:m_at + P], vt[:, h * RN:(h + 1) * RN],
                                 False, j == 7, True)
                    mark[f"y{d}"] = ra.filled.n - ra.filled.start
                    ra.done(ins)
                finish(c, at, w)

            def finish(c, at, w):
                gc_b.wait(pe, c)
                for n in range(4):
                    b = rv.bank()
                    rv.done(mm(b[0:w, 0:256], gc[:, 0:w], w_gate[:, n * 256:(n + 1) * 256], True, True))
                z_b.wait(pe, c)
                for n in range(4):
                    b = ra.bank()
                    for k in range(2):
                        ct = 2 * n + k
                        ins = turn(b[:, k * w:(k + 1) * w], y[0:w, ct * P:(ct + 1) * P], w)
                    ra.done(ins)

            ra.filled.start = ra.filled.n
            with pe.Fori(0, 8) as c:
                ra.filled.enter(c, 44)
                rv.filled.enter(c, 72)
                chunk(c, c * P)
                ra.filled.leave(8, "pe chunks a", 4)
                rv.filled.leave(8, "pe chunks v", 4)
            w = TAIL
            c = 8
            ra.filled.start = ra.filled.n
            chunk_in.wait(pe, c)
            elementwise_part(c, 8 * P, w)
            inverses(c, 0, 8, w, 4)
            arm_t, used_t, sin_t, siu_t = Tally(arm_s), Tally(arm_used), Tally(st_in), Tally(st_used)

            acc = [BV[(rv.filled.n + n) % 4] for n in range(4)]
            rv.wait_drained()

            def state_in():
                sin_t.expect(32)
                pe.wait_ge(st_in, sin_t.value())
                for n in range(4):
                    b = ra.bank()
                    for k in range(2):
                        ins = turn(b[:, k * P:(k + 1) * P], rc[:, 2 * n + k, :], P)
                    ra.done(ins)
                siu_t.add(pe.drain())
                ra.wait_drained()

            def from_state(state, first):
                arm_t.expect()
                pe.wait_ge(arm_s, arm_t.value())
                for u in range(2):
                    for ct in range(8):
                        mm(acc[2 * u + ct // 4][0:w, (ct % 4) * P:(ct % 4 + 1) * P], Bz[:, ct, u, 0:w], state[:, ct, :],
                           first and ct % 4 == 0, False, True)
                used_t.add(pe.drain())

            from_state(S, True)
            with pe.Fori(0, DB) as i:
                ra.filled.enter(i, 4)
                for t in (arm_t, used_t, siu_t):
                    t.enter(i, 1)
                sin_t.enter(i, 32)
                state_in()
                from_state(kc, False)
                for t in (arm_t, used_t, siu_t, sin_t):
                    t.leave(DB)
                ra.filled.leave(DB, "pe states a", 4)
            for half in range(2):
                for j in range(8):
                    h = 8 * half + j
                    ins = mm(acc[half][0:w, j * RN:(j + 1) * RN], NR[half][0:w, j * 2 * w:j * 2 * w + w],
                             vt[0:w, h * RN:(h + 1) * RN], False, j == 7, True)
                rv.done(ins)
            rv.wait_drained()
            for half in range(2):
                b = ra.bank()
                for j in range(8):
                    h = 8 * half + j
                    ins = mm(b[0:w, j * RN:(j + 1) * RN], XT[half][0:w, j * w:(j + 1) * w],
                             P1[0:w, h * RN:(h + 1) * RN], True, True)
                ra.done(ins)
            ra.wait_drained()
            for half in range(2):
                for j in range(8):
                    h = 8 * half + j
                    m_at = j * 2 * w + w
                    mm(acc[2 + half][0:w, j * RN:(j + 1) * RN], MR[half][0:w, m_at:m_at + w], SA[0:w, h * RN:(h + 1) * RN],
                       False, False, True)
                    ins = mm(acc[2 + half][0:w, j * RN:(j + 1) * RN], NR[half][0:w, m_at:m_at + w],
                             vt[0:w, h * RN:(h + 1) * RN], False, j == 7, True)
                rv.done(ins)
            finish(c, 8 * P, w)
            bm_t, bmu_t, sn_t = Tally(bm_s), Tally(bm_used), Tally(snew_s)

            def state_out():
                bm_t.expect()
                pe.wait_ge(bm_s, bm_t.value())
                for n in range(4):
                    b = rv.bank()
                    for k in range(2):
                        cols = slice((2 * n + k) * P, (2 * n + k + 1) * P)
                        mm(b[:, k * P:(k + 1) * P], Bm[0:w, cols], SA[0:w, cols], True, False)
                        ins = mm(b[:, k * P:(k + 1) * P], Km[0:w, cols], vt[0:w, cols], False, True)
                    rv.done(ins)
                bmu_t.add(pe.drain())
                sn_t.expect()
                pe.wait_ge(snew_s, sn_t.value())
                for n in range(4):
                    b = ra.bank()
                    for k in range(2):
                        ins = turn(b[:, k * P:(k + 1) * P], kx[:, 2 * n + k, :], P)
                    ra.done(ins)

            mark["state_out"] = ra.filled.n
            state_out()
            with pe.Fori(0, DB) as i:
                ra.filled.enter(i, 8)
                rv.filled.enter(i, 4)
                for t in (bm_t, bmu_t, sn_t, siu_t):
                    t.enter(i, 1)
                sin_t.enter(i, 32)
                state_in()
                state_out()
                for t in (bm_t, bmu_t, sn_t, siu_t, sin_t):
                    t.leave(DB)
                ra.filled.leave(DB, "pe new states a", 4)
                rv.filled.leave(DB, "pe new states v", 4)
            meet(pe, here)
            pe.wait_ge(wo2_s, 16)
            for k in range(KT):
                for at, w in PIECES:
                    product(rv, lambda j: wo2[:, j, k * P:(k + 1) * P], lambda j: zT[:, j, at:at + w], KT, w=w)
            meet(pe, here)
            feed(1)
            meet(pe, here)
            mark["norm_final"] = ra.filled.n
            norm(nT, KT)
            normed()
            for t in range(NT):
                w = P if t < 8 else TAIL
                for half, ring in enumerate((ra, rv)):
                    b = ring.bank()
                    for k in range(4):
                        ins = turn(b[0:w, k * P:(k + 1) * P], nT[:, 4 * half + k, t * P:t * P + w], P)
                    ring.done(ins)
            mark["end_a"], mark["end_v"] = ra.filled.n, rv.filled.n

        @block.sync
        def _(sp):
            here = Tally(meet_s)
            in_t, rows_t, wa_t, out_t = Tally(in_s), Tally(rows_s), Tally(wa_s), Tally(out_s)

            def load(dst, src, tally):
                tally.add(sp.dma_start(dst, src), 16)

            load(table[:, :], A["table"], in_t)
            sp.wait_ge(zero_s, 1)
            for r, name, n in [(R_MIX, "norm_mix", 2), (R_FFN, "norm_ffn", 2)]:
                load(rows_in[r:r + n, :], A[name], rows_t)
            load(rows_in[R_FIN:R_FIN + 1, :], A["norm_final"].rearrange("(a d) -> a d", a=1), rows_t)
            load(rows_in[R_MU:R_MU + 6, :], A["rwkv_mu"][0], rows_t)
            for r, name in [(R_DW0, "rwkv_decay_w0"), (R_AW0, "rwkv_a_w0"), (R_KK, "rwkv_k_k"), (R_KA, "rwkv_k_a")]:
                load(rows_in[r:r + 1, :], A[name], rows_t)
            load(rows_in[R_RK:R_RK + 1, :], A["rwkv_r_k"].rearrange("a h n -> a (h n)"), rows_t)
            load(rows_in[R_SHIFT:NROW, :], A["state_shift"][0], rows_t)
            load(rows_in[R_QN:R_QN + 1, 0:QL], A["mla_q_a_norm"], rows_t)
            load(rows_in[R_KVN:R_KVN + 1, 0:KVL], A["mla_kv_a_norm"], rows_t)
            x = A["x_prompt"][0]
            load(xin[0:NMETA, 0, :], A["meta_tokens"], in_t)
            load(xin[NMETA:P, 0, :], x[0:P - NMETA, :], in_t)
            for t in range(1, 8):
                load(xin[:, t, :], x[t * P - NMETA:(t + 1) * P - NMETA, :], in_t)
            load(xin[0:NMETA, 8, :], x[8 * P - NMETA:SEQ, :], in_t)
            load(xin[NMETA:TAIL, 8, :], A["x_sample"].rearrange("b s d -> (b s) d"), in_t)
            meet(sp, here)
            w = A["mla_w_qkv_a"][0].rearrange("(k p) n -> p k n", p=P)
            load(wa[:, :, 0:704], w, wa_t)
            load(wa[:, :, 704:768], w[:, :, 640:704], wa_t)
            load(cosT, A["cos"], wa_t)
            load(sinT, A["sin"], wa_t)
            meet(sp, here)
            lat_p = O["lat_p"][0, 0].rearrange("(t p) n -> p t n", p=QT)
            rope_p = O["rope_p"][0, 0].rearrange("(t p) n -> p t n", p=QT)
            wq_t = Tally(wq_s)
            wqd = A["mla_w_q_b"][0].rearrange("(k p) n -> p k n", p=P)
            wkd = A["mla_w_kv_b"][0].rearrange("(k p) n -> p k n", p=P)

            def load_pair(i):
                load(wq, wqd[:, :, bass.ds(i * 384, 384)], wq_t)
                for hh in range(2):
                    load(wqp[:, :, hh * ROPE:(hh + 1) * ROPE], wqd[:, :, bass.ds(i * 384 + hh * 192 + NOPE, ROPE)], wq_t)
                load(wkv, wkd[:, :, bass.ds(i * 512, 512)], wq_t)

            load_pair(0)
            sp.wait_ge(a_drained, mark["latents"] + NQ + 1)
            load(lat_p, ctok[0:QT, 0:NQ, 0:KVL], out_t)
            load(rope_p, ctok[0:QT, 0:NQ, KVL:KVL + ROPE], out_t)
            load(O["lat_s"].rearrange("a b s n -> (a b s) n"), ctok[0:ND, NQ, 0:KVL], out_t)
            load(O["rope_s"].rearrange("a b s n -> (a b s) n"), ctok[0:ND, NQ, KVL:KVL + ROPE], out_t)
            with sp.Fori(0, H // 2 - 1) as i:
                wq_t.enter(i, 64)
                sp.wait_ge(wkv_used, i + 1)
                load_pair(i + 1)
                wq_t.leave(3, "wq")
            sp.wait_ge(out_s, out_t.n)
            meet(sp, here)
            pt_t, wo_t = Tally(pt_s), Tally(wo_s)
            load(pages[:, :], A["page_table"].rearrange("(a b) n -> a (b n)", a=1), pt_t)
            sp.wait_ge(pt_s, 16)
            for k in range(2):
                load(wv[:, k, :, :], A["mla_w_kv_b"][0, k * P:(k + 1) * P].rearrange("p (h n) -> p h n", n=256)[:, :, NOPE:256],
                     wo_t)
            page_t = [Tally(s) for s in page_s]

            def load_seq(b, par):
                for n in range(NPG):
                    page = sp.value_load(pages[0:1, bass.ds(b * NPG + n, 1)], min_val=0, max_val=POOL - 1)
                    src_l = A["cache_kv_latent"][0, bass.ds(page, 1), :, :].rearrange("a p n -> (a p) n")
                    src_r = A["cache_k_rope"][0, bass.ds(page, 1), :, :].rearrange("a p n -> (a p) n")
                    load(dlat[par][:, n, :], src_l, page_t[par])
                    load(drope[par][:, n, 0:ROPE], src_r, page_t[par])
                    load(drope[par][:, n, ROPE:P], src_r, page_t[par])

            load_seq(0, 0)
            load_seq(1, 1)
            with sp.Fori(0, DB // 2 - 1) as i:
                for par in range(2):
                    page_t[par].enter(i, 48 * NPG)
                    sp.wait_ge(page_used, i * 2 + par + 1)
                    load_seq((i + 1) * 2 + par, par)
                    page_t[par].leave(3, "page")
            meet(sp, here)
            load(wo, A["mla_w_o"][0].rearrange("(k p) n -> p k n", p=P), wo_t)
            meet(sp, here)
            up_t, dn_t = [Tally(s) for s in up_s], [Tally(s) for s in dn_s]

            def feed_weights(layer):
                wu = A["ffn_w_up"][layer].rearrange("(k p) n -> p k n", p=P)
                wd = A["ffn_w_down"][layer].rearrange("(g k p) n -> p g k n", p=P, k=2)

                def group(g, par):
                    load(w_up[par], wu[:, :, bass.ds(g * FG, FG)], up_t[par])
                    load(w_dn[par], wd[:, bass.ds(g, 1), :, :].rearrange("p g k n -> p (g k) n"), dn_t[par])

                group(0, 0)
                group(1, 1)
                with sp.Fori(0, NG // 2 - 1) as i:
                    for par in range(2):
                        up_t[par].enter(i, 16)
                        dn_t[par].enter(i, 16)
                        sp.wait_ge(lo_s, i * 4 + layer * 2 * NG + 2 * par + 2)
                        group((i + 1) * 2 + par, par)
                        up_t[par].leave(NG // 2 - 1, "up")
                        dn_t[par].leave(NG // 2 - 1, "down")

            feed_weights(0)
            meet(sp, here)
            load(h_d, hT[:, :, :].rearrange("p k t -> p (k t)"), Tally(hid_s))
            wl_t = Tally(wl_s)
            for dst, name in [(wl[:, :, 0:64], "rwkv_decay_w1"), (wl[:, :, 64:P], "rwkv_a_w1"), (wg, "rwkv_g_w1")]:
                load(dst, A[name][0].rearrange("(k p) n -> p k n", p=P), wl_t)
            sp.wait_ge(a_drained, mark["shift"] + 2)
            load(O["shift_p"][0], shift_out[0:1, :], out_t)
            load(O["shift_s"][0], shift_out[1:9, :], out_t)
            wb_t = [Tally(s) for s in wb_s]
            n = 0
            for name in ("rwkv_w_r", "rwkv_w_k", "rwkv_w_v"):
                wd = A[name][0].rearrange("(k p) n -> p k n", p=P)
                for blk in range(4):
                    if n >= 2:
                        sp.wait_ge(wb_used, n - 1)
                    load(wb[n % 2], wd[:, :, blk * 256:(blk + 1) * 256], wb_t[n % 2])
                    n += 1
            sp.wait_ge(out_s, out_t.n)
            sp.wait_ge(hid_s, 16)
            meet(sp, here)
            mixw_t = Tally(mixw_s)
            load(mixtab, A["mixtable"], mixw_t)
            sp.wait_ge(zero_s, 2)
            load(w_dec[0:64, :], A["rwkv_decay_w2"][0], mixw_t)
            load(w_rate[64:P, :], A["rwkv_a_w2"][0], mixw_t)
            load(w_gate, A["rwkv_g_w2"][0], mixw_t)
            load(lnw, A["rwkv_ln_w"][0].partition_broadcast(P), mixw_t)
            load(lnb, A["rwkv_ln_b"][0].partition_broadcast(P), mixw_t)
            chunk_t, st_t = Tally(chunk_in.sem), Tally(st_in)

            def load_chunk(c):
                load(rc, r_d[bass.ds(c, 1)].rearrange("a p k t -> p (a k) t"), chunk_t)
                load(kc, k_d[bass.ds(c, 1)].rearrange("a p k t -> p (a k) t"), chunk_t)
                load(vt, v_d[bass.ds(c, 1)].rearrange("a p d -> p (a d)"), chunk_t)

            load_chunk(0)
            with sp.Fori(1, 8) as c:
                sp.wait_ge(rkv_free.sem, c)
                load_chunk(c)
            sp.wait_ge(rkv_free.sem, 8)
            for dst, src in [(rc, r_d), (kc, k_d)]:
                load(dst[:, :, 0:TAIL], src[8, :, :, 0:TAIL], chunk_t)
            load(vt[0:TAIL, :], v_d[8, 0:TAIL, :], chunk_t)

            def load_state(j):
                src = A["state_wkv"][0, bass.ds(j, 1)].rearrange("b (c z) v k -> z v (b c) k", z=2)
                for z in range(2):
                    load(rc[z * RN:(z + 1) * RN, :, z * RN:(z + 1) * RN], src[z], st_t)

            sp.wait_ge(zero_s, 3)
            load_state(0)
            with sp.Fori(1, DB) as i:
                sp.wait_ge(st_used, i)
                load_state(i)
            with sp.Fori(0, DB) as i:
                sp.wait_ge(st_used, i + DB)
                load_state(i)
            meet(sp, here)
            load(wo2, A["rwkv_w_o"][0].rearrange("(k p) n -> p k n", p=P), Tally(wo2_s))
            load(hT[:, :, :].rearrange("p k t -> p (k t)"), h_d, Tally(hid_s))
            meet(sp, here)
            feed_weights(1)
            meet(sp, here)
            sp.wait_ge(a_drained, mark["end_a"])
            sp.wait_ge(v_drained, mark["end_v"])
            yp = O["y_prompt"][0]
            load(yp[0:P - NMETA, :], yout[NMETA:P, 0, :], out_t)
            load(yp[P - NMETA:8 * P - NMETA, :].rearrange("(t p) d -> p t d", p=P), yout[:, 1:8, :], out_t)
            load(yp[8 * P - NMETA:SEQ, :], yout[0:NMETA, 8, :], out_t)
            load(O["y_sample"].rearrange("b s d -> (b s) d"), yout[NMETA:TAIL, 8, :], out_t)
            sp.wait_ge(out_s, out_t.n)

        @block.gpsimd
        def _(pool):
            here = Tally(meet_s)
            pool.memset(rows_in[0:NROW, :], 0.0).then_inc(zero_s, 1)
            pool.memset(kz[:, :, :], 0.0)
            pool.memset(qlat[:, 2, :, :], 0.0).then_inc(kz_s, 1)
            for _ in range(5):
                meet(pool, here)
            lo_t, hi_t = Tally(lo_s), Tally(hi_s)

            def feed(layer):
                with pool.Fori(0, NG // 2) as i:
                    lo_t.enter(i, 4)
                    hi_t.enter(i, 4)
                    for par in range(2):
                        for lo, raw, hi in ((up_lo, w_up[par], up_hi), (dn_lo, w_dn[par], dn_hi)):
                            hi_t.expect()
                            pool.wait_ge(hi_s, hi_t.value())
                            lo_t.add(pool.tensor_tensor(lo[:, :, :], raw[:, :, :], hi[:, :, :].bitcast(F32), ALU.subtract))
                    lo_t.leave(NG // 2)
                    hi_t.leave(NG // 2)

            feed(0)
            meet(pool, here)
            stg_t = [Tally(s) for s in stg_s]
            seen = Tally(a_drained, mark["mixing"])

            def store_mixed(scratch):
                with pool.Fori(0, 2) as i:
                    seen.enter(i, 12)
                    for par in range(2):
                        seen.expect(6)
                        pool.wait_ge(a_drained, seen.value())
                        t = stg_t[par]
                        if scratch is v_d:
                            t.enter(i, 32)
                            src = stage[par].rearrange("p (t n) -> p t n", n=256)
                            cols = bass.ds(i * 512 + par * 256, 256)
                            t.add(pool.dma_start(v_d[0:8, :, cols].rearrange("t p n -> p t n"), src[:, 0:8, :]), 16)
                            t.add(pool.dma_start(v_d[8, 0:TAIL, cols], src[0:TAIL, 8, :]), 16)
                        else:
                            t.enter(i, 64)
                            for m_ in range(2):
                                src = stage[par][:, m_ * T:(m_ + 1) * T]
                                ct = bass.ds(i * 4 + par * 2 + m_, 1)
                                t.add(pool.dma_start(scratch[0:8, :, ct, :].rearrange("c p a t -> p c (a t)"),
                                                     src[:, 0:8 * P].rearrange("p (c t) -> p c t", c=8)), 16)
                                t.add(pool.dma_start(scratch[8, :, ct, 0:TAIL].rearrange("p a t -> p (a t)"),
                                                     src[:, 8 * P:T]), 16)
                        t.leave(2, "pool store")
                    seen.leave(2, "pool seen")
                seen.expect(3)

            for scratch in (r_d, k_d, v_d):
                store_mixed(scratch)
            for par in range(2):
                pool.wait_ge(stg_s[par], stg_t[par].n)
            meet(pool, here)
            for buf in (w_dec, w_rate, S[:, :, :], Bz[:, :, :, :], Kz[:, :, :, :]):
                ins = pool.memset(buf, 0.0)
            ins.then_inc(zero_s, 1)
            rkv_free.wait(pool, 8)
            pool.memset(rc[:, :, :], 0.0).then_inc(zero_s, 1)
            so_t = Tally(st_s2)
            seen = Tally(a_drained, mark["state_out"])

            def store_state(dst):
                seen.expect(4)
                pool.wait_ge(a_drained, seen.value())
                d = dst.rearrange("b (c z) v k -> z v (b c) k", z=2)
                for z in range(2):
                    so_t.add(pool.dma_start(d[z], y[z * RN:(z + 1) * RN, :].rearrange("p (c k) -> p c k", k=P)[:, :, z * RN:(z + 1) * RN]), 16)

            store_state(O["wkv_p"][0])
            with pool.Fori(0, DB) as i:
                seen.enter(i, 8)
                so_t.enter(i, 32)
                seen.expect(4)
                store_state(O["wkv_s"][0, bass.ds(i, 1)])
                seen.leave(DB)
                so_t.leave(DB)
            pool.wait_ge(st_s2, so_t.n)
            meet(pool, here)
            meet(pool, here)
            feed(1)
            meet(pool, here)

        @block.scalar
        def _(act):
            here = Tally(meet_s)
            lane = Lane(act, act_order)
            ring = Drain(act, BA, a_filled, a_drained)
            sq_t, norm_t, max_t = Tally(sq_s), Tally(norm_s), Tally(max_s)

            def take(dst, rows, cols, view=None):
                b = ring.bank()[0:rows, 0:cols]
                lane.do(act.copy(dst, b if view is None else view(b)), ring.drained)

            def norm(src, scratch, n):
                for at, w in PIECES:
                    lane.do(act.activation(scratch[:, 0:n, at:at + w], src[:, 0:n, at:at + w], ACT.Square), sq_t)
                if norm_t.n:
                    act.wait_ge(norm_s, norm_t.n)
                for at, w in PIECES:
                    b = ring.bank()
                    lane.do(act.activation(std[:, at:at + w], b[:, 0:w], ACT.Sqrt, bias=eps[:, 0:1],
                                           scale=1.0 / (n * P)), ring.drained)
                norm_t.expect(3)

            for t in range(NT):
                w = P if t < 8 else TAIL
                take(hT[:, 0:4, t * P:t * P + w], P, 4 * w, lambda b: b.rearrange("p (k w) -> p k w", k=4))
            act.wait_ge(eps_s, 1)
            meet(act, here)
            norm(hT, nT, KT)
            for k in range(3):
                for at, w in PIECES:
                    take(cq[:, k, at:at + w], P, w)
            lane.settle()
            norm(cq, oT, 3)
            act.wait_ge(v_drained, mark["down"] + 9)
            norm(ckv, oT[:, 3:5, :], 2)
            meet(act, here)
            for t in range(NQ + 1):
                w = QT if t < NQ else ND
                take(ctok[0:w, t, :], w, KVL + ROPE)
            exp_t = Tally(exp_s)
            with act.Fori(0, H // 2) as i:
                ring.drained.enter(i, 2 * (8 + ATT_A))
                exp_t.enter(i, 2 * NQ)
                for hh in range(2):
                    for at, w in PIECES:
                        take(qn[hh][:, at:at + w], P, w)
                    for at, n in [(0, 4), (4, 4), (8, 2)]:
                        take(vtok[0:QT, at * VH:(at + n) * VH], QT, n * VH)
                    take(wukT, P, 2 * P)
                    b = ring.bank()
                    for k in range(2):
                        ins = act.copy(qlat[:, k, :, bass.ds((i * 2 + hh) * DS, DS)],
                                       b[:, k * ND:(k + 1) * ND].rearrange("p (b q) -> p b q", q=DS))
                    lane.do(ins, ring.drained)

                    def turn(q):
                        for j in range(0, q + 1, 4):
                            n = min(4, q + 1 - j)
                            take(pT[q % 2][0:QT, j * QT:(j + n) * QT], QT, n * QT)

                    for q in range(NQ):
                        act.wait_ge(max_s, exp_t.value(-1))
                        pr = probs[q % 2][0:QT, 0:(q + 1) * QT]
                        lane.do(act.activation(pr, pr, ACT.Exp, bias=stat[0:QT, q % 2, 1:2], scale=SCALE,
                                               accum_out=stat[0:QT, q % 2, 2:3]), exp_t)
                        if q >= 1:
                            turn(q - 1)
                    turn(NQ - 1)
                ring.drained.leave(4, "act heads")
                exp_t.leave(4)
            meet(act, here)
            with act.Fori(0, DB // 2) as i:
                ring.drained.enter(i, 2 * 16)
                exp_t.enter(i, 2)
                for par in range(2):
                    for n in range(4):
                        for k in range(3):
                            take(cT[n % 2][:, k, :], P, 512)
                    act.wait_ge(max_s, exp_t.value(-1))
                    lane.do(act.activation(sd[0:ND, :], sd[0:ND, :], ACT.Exp, bias=dstat[0:ND, 1:2], scale=SCALE,
                                           accum_out=dstat[0:ND, 2:3]), exp_t)
                    for half in range(2):
                        take(pTd[:, half * 8:half * 8 + 8, :], P, 8 * ND, lambda b: b.rearrange("p (n r) -> p n r", n=8))
                    take(pTd[0:ND, NPG, :], ND, ND)
                    b = ring.bank()
                    for k in range(2):
                        ins = act.copy(olT[:, k, :, bass.ds(i * 2 + par, 1), :],
                                       b[:, k * ND:(k + 1) * ND].rearrange("p (h a q) -> p h a q", h=H, a=1))
                    lane.do(ins, ring.drained)
                ring.drained.leave(4, "act samples")
                exp_t.leave(4)
            meet(act, here)
            meet(act, here)
            u_t, hi_t, nhi_t = Tally(u_s), Tally(hi_s), Tally(nhi_s)
            up_t, dn_t = [Tally(s) for s in up_s], [Tally(s) for s in dn_s]

            def feed(layer):
                norm(hT, n32, KT)
                for n, (at, w) in enumerate(PIECES):
                    act.wait_ge(norm_s, norm_t.n - 2 + n)
                    lane.do(act.activation(n_hi[:, :, at:at + w], n32[:, :, at:at + w], ACT.Copy), nhi_t)
                act.wait_ge(nlo_s, nhi_t.n)
                down = Tally(v_filled, mark[f"feed_v{layer}"])
                with act.Fori(0, NG // 2) as i:
                    ring.drained.enter(i, 12)
                    down.enter(i, 48)
                    u_t.enter(i, 12)
                    hi_t.enter(i, 4)
                    for par in range(2):
                        for t in (up_t[par], dn_t[par]):
                            t.enter(i, 16)
                            t.expect(16)
                        act.wait_ge(up_s[par], up_t[par].value())
                        lane.do(act.activation(up_hi[:, :, :], w_up[par][:, :, :], ACT.Copy), hi_t)
                        act.wait_ge(dn_s[par], dn_t[par].value())
                        act.wait_ge(v_filled, down.value())
                        lane.do(act.activation(dn_hi[:, :, :], w_dn[par][:, :, :], ACT.Copy), hi_t)
                        down.expect(24)
                        for k in range(2):
                            for at, w in PIECES:
                                b = ring.bank()
                                u_t.expect()
                                act.wait_ge(u_s, u_t.value())
                                lane.do(act.activation(relu[(u_t.n - 1) % 4][:, 0:w], b[:, 0:w], ACT.Relu), ring.drained)
                        up_t[par].leave(NG // 2)
                        dn_t[par].leave(NG // 2)
                    ring.drained.leave(NG // 2, "act feed")
                    down.leave(NG // 2)
                    u_t.leave(NG // 2)
                    hi_t.leave(NG // 2)
                u_t.expect(4)

            feed(0)
            meet(act, here)
            norm(hT, nT, KT)
            for half in range(2):
                take(shift_out[:, half * 512:(half + 1) * 512], 9, 512)
            act.wait_ge(out_s, out_n + 32)
            stg_t = [Tally(s) for s in stg_s]

            def lay_out(first, token_major):
                per = 32 if token_major else 64
                if first:
                    for i in range(2):
                        for par in range(2):
                            if i:
                                stg_t[par].expect(per)
                                act.wait_ge(stg_s[par], stg_t[par].n)
                            block_out(par, token_major)
                    return
                with act.Fori(0, 2) as i:
                    ring.drained.enter(i, 12)
                    for par in range(2):
                        t = stg_t[par]
                        act.wait_ge(stg_s[par], i * per + t.n + 64)
                        block_out(par, token_major)
                    ring.drained.leave(2, "act mixed")
                for t in stg_t:
                    t.expect(64 + per if per == 64 else 96)

            def block_out(par, token_major):
                if token_major:
                    for tiles in [(0, 1), (2, 3), (4, 5), (6,), (7,), (8,)]:
                        rows = P if tiles[0] < 8 else TAIL
                        take(stage[par][0:rows, tiles[0] * 256:(tiles[-1] + 1) * 256], rows, 256 * len(tiles))
                else:
                    for m_ in range(2):
                        for at, w in PIECES:
                            take(stage[par][:, m_ * T + at:m_ * T + at + w], P, w)

            lay_out(True, False)
            for at, w in PIECES:
                b = ring.bank()
                lane.do(act.activation(lora[0:64, at:at + w], b[0:64, 0:w], ACT.Tanh), ring.drained)
            lay_out(False, False)
            for at, w in PIECES:
                b = ring.bank()
                lane.do(act.copy(lora[64:P, at:at + w], b[64:P, 0:w]), ring.drained)
            lay_out(False, True)
            for at, w in PIECES:
                b = ring.bank()
                lane.do(act.activation(gate[:, at:at + w], b[:, 0:w], ACT.Sigmoid), ring.drained)
            meet(act, here)

            def signal(ins, beat):
                ins.then_inc(beat.sem, 1)

            def elementwise_part(c, at, w, last=False):
                signal(act.copy(gc[:, 0:w], gate[:, bass.ds(at, w)]), gc_b)
                for dst, row, beat in ((sw, R_DW0, sw_b), (rate, R_AW0, rate_b)):
                    for half in range(2):
                        b = ring.bank()
                        for k in range(4):
                            ct = 4 * half + k
                            ins = act.activation(dst[:, ct, 0:w], b[:, k * w:(k + 1) * w], ACT.Sigmoid,
                                                 bias=prm[:, ct, row:row + 1])
                        lane.do(ins, ring.drained)
                    signal(act.drain(), beat)
                kk_b.wait(act, c)
                signal(act.activation(kx[:, :, 0:w], kk[:, :, 0:w], ACT.Square), sq_b)
                cum_b.wait(act, c)
                act.activation(pinc[:, :, 0:w], cum[:, :, 0:w], ACT.Exp, scale=-W_SCALE)
                if not last:
                    act.activation(dmid[:, 0:8], mid[:, 0:8], ACT.Exp, scale=-W_SCALE)
                signal(act.activation(pinv[:, :, 0:w], cum[:, :, 0:w], ACT.Exp, scale=W_SCALE), dec_b)
                cumx_b.wait(act, c)
                signal(act.activation(sw[:, :, 0:w], sw[:, :, 0:w], ACT.Exp, scale=-W_SCALE), decx_b)
                clamp_b.wait(act, c)
                signal(act.activation(kx[:, :, 0:w], kx[:, :, 0:w], ACT.Sqrt), root_b)
                bk_b.wait(act, c)
                for src, dst in ((Bt, Bz), (Kt, Kz)):
                    for z in range(2):
                        part = slice(z * RN, (z + 1) * RN)
                        ins = act.copy(dst[part, :, z, 0:w], src[part, :, 0:w])
                signal(ins, split_b)
                for dst in (Btok, Ktok):
                    for half in range(2):
                        take(dst[0:w, half * 512:(half + 1) * 512], w, 512)
                for half in range(2):
                    take(coef[0:w, half * 8:half * 8 + 8], w, 8)

            def inverses(hg, w, levels):
                for l in range(levels - 1):
                    for gi in range(2):
                        take(X[gi][0:w, 0:hg * w], w, hg * w)

            def finish(c, at, w):
                yc_b.wait(act, c)
                signal(act.activation(kx[0:w].rearrange("p k t -> p (k t)"), y[0:w, :], ACT.Square), ysq_b)
                var_b.wait(act, c)
                signal(act.activation(var[0:w, :], var[0:w, :], ACT.Sqrt, bias=eps[0:w, 1:2], scale=1.0 / RN), ystd_b)
                for n in range(4):
                    take(zT[:, 2 * n:2 * n + 2, bass.ds(at, w)], P, 2 * w, lambda b: b.rearrange("p (k w) -> p k w", k=2))

            with act.Fori(0, 8) as c:
                ring.drained.enter(c, 44)
                elementwise_part(c, c * P, P)
                for d in range(2):
                    inverses(4, P, LEVELS)
                    take(P1[:, d * 512:(d + 1) * 512], P, 512)
                    take(SA[:, d * 512:(d + 1) * 512], P, 512)
                    take(y[:, d * 512:(d + 1) * 512], P, 512)
                finish(c, c * P, P)
                ring.drained.leave(8, "act chunks")
            c = 8
            elementwise_part(c, 8 * P, TAIL, True)
            inverses(8, TAIL, 4)

            def state_in():
                for n in range(4):
                    take(kc[:, 2 * n:2 * n + 2, :], P, 256, lambda b: b.rearrange("p (k w) -> p k w", k=2))

            with act.Fori(0, DB) as i:
                ring.drained.enter(i, 4)
                state_in()
                ring.drained.leave(DB)
            for half in range(2):
                take(SA[0:TAIL, half * 512:(half + 1) * 512], TAIL, 512)
            finish(c, 8 * P, TAIL)

            def state_out():
                for n in range(4):
                    take(y[:, n * 256:(n + 1) * 256], P, 256)

            state_out()
            with act.Fori(0, DB) as i:
                ring.drained.enter(i, 8)
                state_in()
                act.wait_ge(st_s2, i * 32 + 32)
                state_out()
                ring.drained.leave(DB)
            meet(act, here)
            meet(act, here)
            feed(1)
            meet(act, here)
            norm(hT, nT, KT)
            for t in range(NT):
                w = P if t < 8 else TAIL
                take(yout[0:w, t, 0:512], w, 512)

        @block.vector
        def _(dve):
            here = Tally(meet_s)
            lane = Lane(dve, dve_order)
            ring = Drain(dve, BV, v_filled, v_drained)
            norm_t = Tally(norm_s)

            def take(dst, rows, cols, view=None):
                b = ring.bank()[0:rows, 0:cols]
                lane.do(dve.tensor_copy(dst, b if view is None else view(b)), ring.drained)

            def norm(src, dst, n, row, at_mark):
                seen = Tally(a_drained, at_mark)
                for at, w in PIECES:
                    seen.expect()
                    dve.wait_ge(a_drained, seen.n)
                    lane.do(dve.reciprocal(std[:, at:at + w], std[:, at:at + w]))
                    lane.settle()
                    for k in range(n):
                        ins = dve.scalar_tensor_tensor(out=dst[:, k, at:at + w], in0=src[:, k, at:at + w],
                                                       scalar=prm[:, k, row:row + 1], in1=std[:, at:at + w],
                                                       op0=ALU.mult, op1=ALU.mult)
                    lane.do(ins, norm_t)

            def add_hidden(k, at, w):
                b = ring.bank()
                lane.do(dve.tensor_tensor(hT[:, k, at:at + w], hT[:, k, at:at + w], b[:, 0:w], ALU.add), ring.drained)

            dve.memset(eps[:, 0:1], EPS)
            dve.memset(eps[:, 1:2], GN_EPS).then_inc(eps_s, 1)
            take(prm[:, :, :], P, KT * NROW, lambda b: b.rearrange("p (k r) -> p k r", k=KT))
            for t in range(NT):
                w = P if t < 8 else TAIL
                take(hT[:, 4:8, t * P:t * P + w], P, 4 * w, lambda b: b.rearrange("p (k w) -> p k w", k=4))
            meet(dve, here)
            norm(hT, nT, KT, R_MIX, mark["norm0"])
            for k in range(2):
                for at, w in PIECES:
                    take(ckv[:, k, at:at + w], P, w)
            for at, w in PIECES:
                take(kraw[:, at:at + w], P, w)
            norm(cq, cq, 3, R_QN, mark["norm_q"])
            dve.wait_ge(wa_s, 64)

            def rope(raw, out, tmp):
                lane.do(dve.tensor_tensor(out, raw, cosT, ALU.mult))
                lane.settle()
                for at, w in PIECES:
                    b = ring.bank()
                    lane.do(dve.tensor_tensor(tmp[:, at:at + w], b[:, 0:w], sinT[:, at:at + w], ALU.mult), ring.drained)
                lane.settle()
                lane.do(dve.tensor_tensor(out, out, tmp, ALU.add))
                lane.settle()

            rope(kraw, kfull, kraw)
            dve.wait_ge(kz_s, 1)
            lane.do(dve.tensor_copy(kz[0:ROPE, 0, :], kfull[0:ROPE, :]))
            lane.do(dve.tensor_copy(kz[ROPE:P, 1, :], kfull[ROPE:P, :]))
            norm(ckv, ckv, 2, R_KVN, mark["norm_q"] + 3)
            meet(dve, here)
            max_t, prob_t, exp_t = Tally(max_s), Tally(prob_s), Tally(exp_s)
            with dve.Fori(0, H // 2) as i:
                ring.drained.enter(i, 6 + 2 * (3 + ATT_V))
                lane.order.enter(i, DVE_HEADS)
                for t in (max_t, prob_t, exp_t):
                    t.enter(i, 2 * NQ)
                for at, w in PIECES:
                    take(qraw[:, at:at + w], P, w)
                lane.settle()
                rope(qraw, qpe, rtmp)
                for hh in range(2):
                    half = slice(hh * ROPE, (hh + 1) * ROPE)
                    lane.do(dve.tensor_copy(qlat[half, 2, :, bass.ds((i * 2 + hh) * DS, DS)],
                                            qpe[half, NP:T].rearrange("p (b q) -> p b q", q=DS)))
                for hh in range(2):
                    for at, w in PIECES:
                        take(kn[hh][:, at:at + w], P, w)

                    def maxima(q):
                        for j in range(0, q + 1, 4):
                            n = min(4, q + 1 - j)
                            b = ring.bank()
                            last = j + n == q + 1
                            if last:
                                if n > 1:
                                    dve.tensor_copy(probs[q % 2][0:QT, j * QT:q * QT], b[0:QT, 0:(n - 1) * QT])
                                lane.do(dve.tensor_tensor(probs[q % 2][0:QT, q * QT:(q + 1) * QT],
                                                          b[0:QT, (n - 1) * QT:n * QT], tab("causal", QT), ALU.add),
                                        ring.drained)
                            else:
                                lane.do(dve.tensor_copy(probs[q % 2][0:QT, j * QT:(j + n) * QT], b[0:QT, 0:n * QT]),
                                        ring.drained)
                        lane.settle()
                        lane.do(dve.tensor_reduce(stat[0:QT, q % 2, 0:1], probs[q % 2][0:QT, 0:(q + 1) * QT], AX, ALU.max))
                        lane.settle()
                        lane.do(dve.tensor_scalar(stat[0:QT, q % 2, 1:2], stat[0:QT, q % 2, 0:1], -SCALE, None, ALU.mult),
                                max_t)

                    def scaled(q):
                        exp_t.expect()
                        dve.wait_ge(exp_s, exp_t.value())
                        lane.do(dve.reciprocal(stat[0:QT, q % 2, 3:4], stat[0:QT, q % 2, 2:3]))
                        lane.settle()
                        pr = probs[q % 2][0:QT, 0:(q + 1) * QT]
                        lane.do(dve.tensor_scalar(pr, pr, stat[0:QT, q % 2, 3:4], None, ALU.mult), prob_t)

                    for q in range(NQ + 2):
                        if q < NQ:
                            maxima(q)
                        if q >= 2:
                            take(oT[:, bass.ds(i * 2 + hh, 1), (q - 2) * QT:(q - 1) * QT], P, QT,
                                 lambda b: b.rearrange("p (a w) -> p a w", a=1))
                        if 1 <= q <= NQ:
                            scaled(q - 1)
                ring.drained.leave(4, "dve heads v")
                lane.order.leave(4, "DVE_HEADS")
                for t in (max_t, prob_t, exp_t):
                    t.leave(4)
            meet(dve, here)
            qcur_t = Tally(qcur_s)
            with dve.Fori(0, DB // 2) as i:
                ring.drained.enter(i, 2 * 6)
                lane.order.enter(i, DVE_SAMPLES)
                for t in (max_t, exp_t, qcur_t):
                    t.enter(i, 2)
                for par in range(2):
                    b_ = i * 2 + par
                    lane.do(dve.tensor_copy(qcur[:, :, :], qlat[:, :, bass.ds(b_, 1), :].rearrange("p k b r -> p k (b r)")),
                            qcur_t)
                    for n in range(4):
                        take(sd[0:ND, n * 512:(n + 1) * 512], ND, 512)
                    b = ring.bank()
                    at = TABLE["new_keys"][0]
                    lane.do(dve.tensor_tensor(sd[0:ND, PAST:PAST + ND], b[0:ND, 0:ND],
                                              table[0:ND, bass.ds(b_ * ND + at, ND)], ALU.add), ring.drained)
                    lane.settle()
                    lane.do(dve.tensor_reduce(dstat[0:ND, 0:1], sd[0:ND, :], AX, ALU.max))
                    lane.settle()
                    lane.do(dve.tensor_scalar(dstat[0:ND, 1:2], dstat[0:ND, 0:1], -SCALE, None, ALU.mult), max_t)
                    exp_t.expect()
                    dve.wait_ge(exp_s, exp_t.value())
                    lane.do(dve.reciprocal(dstat[0:ND, 3:4], dstat[0:ND, 2:3]))
                    lane.settle()
                    b = ring.bank()
                    lane.do(dve.tensor_scalar(ol[0:ND, :], b[0:ND, 0:KVL], dstat[0:ND, 3:4], None, ALU.mult), ring.drained)
                ring.drained.leave(4, "dve samples v")
                lane.order.leave(4, "DVE_SAMPLES")
                for t in (max_t, exp_t, qcur_t):
                    t.leave(4)
            for h in range(H):
                take(oT[:, h, NP:T], P, ND)
            meet(dve, here)
            for k in range(KT):
                for at, w in PIECES:
                    add_hidden(k, at, w)
            meet(dve, here)
            u_t, nhi_t, nlo_t = Tally(u_s), Tally(nhi_s), Tally(nlo_s)

            def feed(layer):
                norm(hT, n32, KT, R_FFN + layer, mark[f"feed_norm{layer}"])
                for at, w in PIECES:
                    nhi_t.expect()
                    dve.wait_ge(nhi_s, nhi_t.n)
                    lane.do(dve.tensor_tensor(n_lo[:, :, at:at + w], n32[:, :, at:at + w], n_hi[:, :, at:at + w].bitcast(F32),
                                              ALU.subtract), nlo_t)
                u_t.add(dve.drain(), 4)
                seen = Tally(a_drained, mark[f"feed{layer}"])
                with dve.Fori(0, NG // 2) as i:
                    ring.drained.enter(i, 48)
                    seen.enter(i, 12)
                    u_t.enter(i, 12)
                    lane.order.enter(i, 24)
                    for par in range(2):
                        for k in range(2):
                            for at, w in PIECES:
                                r = relu[(seen.n - mark[f"feed{layer}"]) % 4][:, 0:w]
                                seen.expect()
                                dve.wait_ge(a_drained, seen.value())
                                lane.do(dve.tensor_tensor(r, r, r, ALU.mult))
                                lane.settle()
                                lane.do(dve.tensor_copy(u_hi[:, k, at:at + w], r))
                                lane.settle()
                                lane.do(dve.tensor_tensor(u_lo[:, k, at:at + w], r, u_hi[:, k, at:at + w].bitcast(F32),
                                                          ALU.subtract), u_t)
                        for k in range(KT):
                            for at, w in PIECES:
                                add_hidden(k, at, w)
                    ring.drained.leave(NG // 2, "dve feed v")
                    seen.leave(NG // 2)
                    u_t.leave(NG // 2)
                    lane.order.leave(NG // 2, "dve feed order")

            feed(0)
            meet(dve, here)
            norm(hT, nT, KT, R_MIX + 1, mark["norm1"])
            xm_t = Tally(xm_s)
            lane.settle()
            for n, row in enumerate((0, 1, 2, 4, 3, 5)):
                x = xm[n % 2]
                if n >= 2:
                    dve.wait_ge(xm_used, n - 1)
                lane.do(dve.tensor_tensor(x[:, :, 1:T], nT[:, :, 0:T - 1], nT[:, :, 1:T], ALU.subtract))
                lane.do(dve.tensor_scalar(x[:, :, 0:1], nT[:, :, 0:1], -1.0, None, ALU.mult))
                lane.settle()
                lane.do(dve.tensor_tensor(x[:, :, NP:T:DS], prm[:, :, R_SHIFT:NROW], nT[:, :, NP:T:DS], ALU.subtract))
                lane.settle()
                for k in range(KT):
                    ins = dve.scalar_tensor_tensor(out=x[:, k, :], in0=x[:, k, :], scalar=prm[:, k, R_MU + row:R_MU + row + 1],
                                                   in1=nT[:, k, :], op0=ALU.mult, op1=ALU.add)
                lane.do(ins, xm_t)
            meet(dve, here)
            dve.wait_ge(mixw_s, mixw_n)
            dve.wait_ge(zero_s, 2)
            hiddens = None

            def signal(ins, beat):
                lane.do(ins, beat.tally)

            def wide(row, w):
                return prm[:, :, row:row + 1].broadcast_to([P, 8, w])

            def flat(t, w):
                return t[0:w].rearrange("p k t -> p (k t)")

            def tt(out, a, b, op):
                lane.do(dve.tensor_tensor(out, a, b, op))

            def elementwise_part(c, w, last=False):
                t = slice(0, w)
                chunk_in.wait(dve, c)
                signal(dve.tensor_tensor(kk[:, :, t], kc[:, :, t], wide(R_KK, w), ALU.mult), kk_b)
                sw_b.wait(dve, c)
                if last:
                    for k in range(8):
                        ins = dve.tensor_tensor_scan(cum[:, k, t], mix("tail_restart"), sw[:, k, t], 0.0, ALU.mult, ALU.add)
                    signal(ins, cum_b)
                    lane.settle()
                else:
                    lane.do(dve.tensor_tensor_scan(flat(cum, P), mix("restart"), flat(sw, P), 0.0, ALU.mult, ALU.add))
                    lane.settle()
                    lane.do(dve.tensor_copy(mid[:, 0:8].unsqueeze(2), cum[:, :, 63:64]))
                    lane.settle()
                    signal(dve.tensor_tensor(cum[:, :, t], cum[:, :, t], mid[:, 0:8].unsqueeze(2).broadcast_to([P, 8, w]),
                                             ALU.subtract), cum_b)
                    lane.settle()
                signal(dve.tensor_tensor(sw[:, :, t], cum[:, :, t], sw[:, :, t], ALU.subtract), cumx_b)
                for half in range(2):
                    b = ring.bank()
                    lane.do(dve.tensor_scalar(kx[:, 4 * half:4 * half + 4, t], b[:, 0:4 * w].rearrange("p (k w) -> p k w", k=4),
                                              1e-24, None, ALU.max), ring.drained)
                signal(dve.drain(), clamp_b)
                root_b.wait(dve, c)
                lane.do(dve.reciprocal(kx[:, :, t], kx[:, :, t]))
                lane.settle()
                tt(kk[:, :, t], kk[:, :, t], kx[:, :, t], ALU.mult)
                lane.settle()
                decx_b.wait(dve, c)
                lane.do(dve.scalar_tensor_tensor(out=AR[:, :, 0, t], in0=kk[:, :, t], scalar=-1.0, in1=sw[:, :, t],
                                                 op0=ALU.mult, op1=ALU.mult))
                rate_b.wait(dve, c)
                lane.settle()
                tt(kk[:, :, t], kk[:, :, t], rate[:, :, t], ALU.mult)
                lane.do(dve.scalar_tensor_tensor(out=kx[:, :, t], in0=rate[:, :, t], scalar=-1.0, in1=wide(R_KA, w),
                                                 op0=ALU.add, op1=ALU.mult))
                dec_b.wait(dve, c)
                lane.settle()
                tt(Bt[:, :, t], kk[:, :, t], pinv[:, :, t], ALU.mult)
                lane.do(dve.scalar_tensor_tensor(out=kx[:, :, t], in0=kx[:, :, t], scalar=1.0, in1=kc[:, :, t],
                                                 op0=ALU.add, op1=ALU.mult))
                lane.settle()
                signal(dve.tensor_tensor(Kt[:, :, t], kx[:, :, t], pinv[:, :, t], ALU.mult), bk_b)
                signal(dve.tensor_tensor(AR[:, :, 1, t], rc[:, :, t], pinc[:, :, t], ALU.mult), ab_b)
                lane.settle()
                tt(kx[:, :, t], kx[:, :, t], rc[:, :, t], ALU.mult)
                lane.settle()
                signal(dve.tensor_tensor(kx[:, :, t], kx[:, :, t], wide(R_RK, w), ALU.mult), bonus_b)
                if not last:
                    lane.do(dve.tensor_copy(dend[:, 0:8].unsqueeze(2), pinc[:, :, P - 1:P]))
                    signal(dve.tensor_tensor(Sm[:, :, :], S[:, :, :], dmid[:, 0:8].unsqueeze(2).broadcast_to([P, 8, P]),
                                             ALU.mult), s_b)

            def inverses(first, hg, w, levels):
                hb = hg // 2
                names = ("below", "tail_below") if w == P else ("tail_below", "tail_below")
                at = MIXTAB["below" if w == P else "tail_below"][0]
                masks = mixtab[0:w, at:at + 2 * w].unsqueeze(1).broadcast_to([w, hb, 2 * w])
                for gi in range(2):
                    for dst in (MR, NR):
                        for half in range(2):
                            b = ring.bank()
                            lane.do(dve.tensor_tensor(
                                dst[gi][0:w, half * hb * 2 * w:(half + 1) * hb * 2 * w].rearrange("p (h w) -> p h w", h=hb),
                                b[0:w, 0:hb * 2 * w].rearrange("p (h w) -> p h w", h=hb), masks, ALU.mult), ring.drained)
                    lane.settle()
                    xt = XT[gi][0:w, 0:hg * w].rearrange("p (h w) -> p h w", h=hg)
                    mt = MR[gi][0:w, 0:hg * 2 * w].rearrange("p (h a w) -> p h a w", h=hg, a=2)[:, :, 0, :]
                    tt(xt, mt, mix("first_pairs", w)[:, 0:w].unsqueeze(1).broadcast_to([w, hg, w]), ALU.mult)
                    lane.settle()
                    signal(dve.tensor_tensor(xt, xt, ident[0:w, 0:w].unsqueeze(1).broadcast_to([w, hg, w]), ALU.add), x1_b)
                for l in range(1, levels):
                    at = MIXTAB["siblings"][0] + (l - 1) * P
                    m = mixtab[0:w, at:at + w].unsqueeze(1).broadcast_to([w, hg, w])
                    for gi in range(2):
                        b = ring.bank()
                        lane.do(dve.tensor_tensor(W[gi][0:w, 0:hg * w].rearrange("p (h w) -> p h w", h=hg),
                                                  b[0:w, 0:hg * w].rearrange("p (h w) -> p h w", h=hg), m, ALU.mult), ring.drained)
                    for gi in range(2):
                        b = ring.bank()
                        xt = XT[gi][0:w, 0:hg * w]
                        lane.do(dve.tensor_tensor(xt, xt, b[0:w, 0:hg * w], ALU.add), ring.drained)

            def head_view(t, w):
                return t.rearrange("p (h n) -> p h n", n=RN)[0:w]

            def bc(t, w):
                return t[0:w, 0:RH].unsqueeze(2).broadcast_to([w, RH, RN])

            def finish(c, w):
                yh = head_view(y, w)
                lane.do(dve.tensor_reduce(mean[0:w, 0:RH].unsqueeze(2), yh, AX, ALU.add))
                lane.settle()
                lane.do(dve.tensor_scalar(mean[0:w, :], mean[0:w, :], -1.0 / RN, None, ALU.mult))
                lane.settle()
                signal(dve.tensor_tensor(yh, yh, bc(mean, w), ALU.add), yc_b)
                ysq_b.wait(dve, c)
                signal(dve.tensor_reduce(var[0:w, 0:RH].unsqueeze(2), head_view(flat(kx, P), w), AX, ALU.add), var_b)
                tmp = head_view(flat(sw, P), w)
                tt(tmp, head_view(vt, w), bc(coef, w), ALU.mult)
                ystd_b.wait(dve, c)
                lane.do(dve.reciprocal(var[0:w, :], var[0:w, :]))
                lane.settle()
                tt(yh, yh, bc(var, w), ALU.mult)
                lane.settle()
                tt(y[0:w, :], y[0:w, :], lnw[0:w, :], ALU.mult)
                lane.settle()
                tt(y[0:w, :], y[0:w, :], lnb[0:w, :], ALU.add)
                lane.settle()
                tt(yh, yh, tmp, ALU.add)
                lane.settle()
                for n in range(4):
                    b = ring.bank()
                    part = y[0:w, n * 256:(n + 1) * 256]
                    lane.do(dve.tensor_tensor(part, part, b[0:w, 0:256], ALU.mult), ring.drained)
                signal(dve.drain(), z_b)

            beats = [kk_b, cum_b, cumx_b, clamp_b, bk_b, ab_b, bonus_b, s_b, x1_b, yc_b, var_b, z_b, rkv_free]
            for beat in beats:
                beat.tally = Tally(beat.sem)
            with dve.Fori(0, 8) as c:
                ring.drained.enter(c, 72)
                lane.order.enter(c, DVE_CHUNK)
                for beat in beats:
                    beat.tally.enter(c, beat.per)
                elementwise_part(c, P)
                for d in range(2):
                    inverses(8 * d, 4, P, LEVELS)
                    b = ring.bank()
                    cts = slice(4 * d, 4 * d + 4)
                    lane.do(dve.tensor_tensor(cum[:, cts, :], b[:, :].rearrange("p (k w) -> p k w", k=4),
                                              halves.unsqueeze(1).broadcast_to([P, 4, P]), ALU.mult), ring.drained)
                    lane.settle()
                    tt(cum[:, cts, :], cum[:, cts, :], Sm[:, cts, :], ALU.add)
                    lane.settle()
                    tt(S[:, cts, :], cum[:, cts, :], dend[:, 4 * d:4 * d + 4].unsqueeze(2).broadcast_to([P, 4, P]), ALU.mult)
                dve.wait_ge(a_drained, c * 44 + mark["chunks_a"] + mark["y1"] + 1)
                finish(c, P)
                signal(dve.drain(), rkv_free)
                ring.drained.leave(8, "dve chunks")
                lane.order.leave(8, "DVE_CHUNK")
                for beat in beats:
                    beat.tally.leave(8)
            c, w = 8, TAIL
            elementwise_part(c, w, True)
            inverses(0, 8, w, 4)
            signal(dve.drain(), rkv_free)
            arm_t = Tally(arm_s)
            cols_at, rows_at = MIXTAB["seq_cols"][0], MIXTAB["seq_rows"][0]

            def mask_queries(s):
                for u in range(2):
                    ins = dve.tensor_tensor(Bz[:, :, u, 0:w], AR[:, :, u, 0:w],
                                            mixtab[:, bass.ds(s * w + cols_at, w)].unsqueeze(1).broadcast_to([P, 8, w]), ALU.mult)
                lane.do(ins, arm_t)

            mask_queries(0)
            with dve.Fori(0, DB) as i:
                arm_t.enter(i, 1)
                dve.wait_ge(arm_used, i + 1)
                mask_queries(i + 1)
                arm_t.leave(DB)
            for half in range(2):
                take(P1[0:w, half * 512:(half + 1) * 512], w, 512)
            for half in range(2):
                take(y[0:w, half * 512:(half + 1) * 512], w, 512)
            lane.settle()
            finish(c, w)
            bm_t, sn_t = Tally(bm_s), Tally(snew_s)

            def new_state(s, state):
                for dst, src in ((Bm, Btok), (Km, Ktok)):
                    ins = dve.tensor_tensor(dst[0:w, :], src[0:w, :],
                                            mixtab[0:w, bass.ds(s + rows_at, 1)].broadcast_to([w, D]), ALU.mult)
                lane.do(ins, bm_t)
                for n in range(4):
                    b = ring.bank()
                    lane.do(dve.tensor_tensor(kx[:, 2 * n:2 * n + 2, :], b[:, 0:256].rearrange("p (k w) -> p k w", k=2),
                                              halves.unsqueeze(1).broadcast_to([P, 2, P]), ALU.mult), ring.drained)
                lane.settle()
                tt(kx[:, :, :], kx[:, :, :], state[:, :, :], ALU.add)
                lane.settle()
                lane.do(dve.tensor_tensor(kx[:, :, :], kx[:, :, :],
                                          pinc[:, :, bass.ds(s * DS + NMETA - 1, 1)].broadcast_to([P, 8, P]), ALU.mult), sn_t)

            new_state(0, S)
            with dve.Fori(0, DB) as i:
                ring.drained.enter(i, 4)
                lane.order.enter(i, 1)
                bm_t.enter(i, 1)
                sn_t.enter(i, 1)
                dve.wait_ge(bm_used, i + 1)
                dve.wait_ge(a_drained, i * 8 + mark["state_out"] + 8)
                new_state(i + 1, kc)
                ring.drained.leave(DB, "dve states")
                lane.order.leave(DB, "dve states order")
                bm_t.leave(DB)
                sn_t.leave(DB)
            meet(dve, here)
            dve.wait_ge(hid_s, 32)
            for k in range(KT):
                for at, w in PIECES:
                    add_hidden(k, at, w)
            meet(dve, here)
            feed(1)
            meet(dve, here)
            norm(hT, nT, KT, R_FIN, mark["norm_final"])
            for t in range(NT):
                w = P if t < 8 else TAIL
                take(yout[0:w, t, 512:1024], w, 512)


_INS = ["x_prompt", "x_sample", "cache_kv_latent", "cache_k_rope", "state_wkv", "state_shift", "page_table",
        "meta_tokens", "norm_mix", "norm_ffn", "norm_final", "mla_w_qkv_a", "mla_q_a_norm", "mla_kv_a_norm",
        "mla_w_q_b", "mla_w_kv_b", "mla_w_o", "rwkv_mu", "rwkv_w_r", "rwkv_w_k", "rwkv_w_v", "rwkv_w_o",
        "rwkv_decay_w0", "rwkv_decay_w1", "rwkv_decay_w2", "rwkv_a_w0", "rwkv_a_w1", "rwkv_a_w2", "rwkv_g_w1",
        "rwkv_g_w2", "rwkv_k_k", "rwkv_k_a", "rwkv_r_k", "rwkv_ln_w", "rwkv_ln_b", "ffn_w_up", "ffn_w_down"]
_OUTS = [("y_prompt", (1, SEQ, D)), ("y_sample", (DB, DS, D)), ("lat_p", (1, 1, NP, KVL)), ("rope_p", (1, 1, NP, ROPE)),
         ("lat_s", (1, DB, DS, KVL)), ("rope_s", (1, DB, DS, ROPE)), ("wkv_p", (1, 1, RH, RN, RN)),
         ("shift_p", (1, 1, D)), ("wkv_s", (1, DB, RH, RN, RN)), ("shift_s", (1, DB, D))]


def constants():
    import numpy as np

    stays, mixing = np.zeros((P, NTABLE), np.float32), np.zeros((P, NMIXTAB), np.float32)

    def put(name, v):
        t = stays if name in TABLE else mixing
        at, n = TABLE[name] if name in TABLE else MIXTAB[name]
        v = np.asarray(v, np.float32)
        t[:v.shape[0], at:at + n] = v.reshape(v.shape[0], n)

    p = np.arange(P)
    row, col = p[:, None], p[None, :]
    put("ident", row == col)
    put("ones", np.ones((P, P)))
    put("halves", row // RN == col // RN)
    c = col % ROPE
    put("rot", np.where((c < 32) & (row == col + 32), -1.0, 0.0) + np.where((c >= 32) & (row == col - 32), 1.0, 0.0))
    put("below", row < col)
    put("upto", row <= col)
    s = np.arange(TAIL)
    of = np.where(s < NMETA, 0, 1 + (s - NMETA) // DS)
    same = of[:, None] == of[None, :]
    put("tail_below", same & (s[:, None] < s[None, :]))
    put("tail_upto", same & (s[:, None] <= s[None, :]))
    put("first_pairs", (col % 2 == 1) & (row == col - 1))
    put("siblings", np.stack([((row >> l) == (col >> l) + 1) & ((col >> l) % 2 == 0) for l in range(1, 7)], 1))
    q = np.arange(QT)
    put("causal", np.where(q[None, :] <= q[:, None], 0.0, NEG))
    r = np.arange(ND)
    b = np.arange(DB)
    new = (r[None, None, :] // DS == b[None, :, None]) & (r[None, None, :] % DS <= r[:, None, None] % DS)
    put("new_keys", np.where(new, 0.0, NEG))
    put("restart", np.tile(np.tile(p != 0, 8), (P, 1)))
    starts = np.r_[1, np.diff(of)] != 0
    put("tail_restart", np.tile(~starts, (P, 1)))
    put("seq_rows", of[:, None] == np.arange(9)[None, :])
    put("seq_cols", np.tile((of[None, :] == np.arange(9)[:, None]).reshape(-1), (P, 1)))
    put("head_cols", row // RN == np.arange(2)[None, :])
    half = ROPE // 2
    freq = (np.float32(10000.0) ** (-np.arange(half, dtype=np.float32) / np.float32(half))).astype(np.float32)
    pos = np.r_[np.arange(NP), np.tile(PAST + np.arange(DS), DB)].astype(np.float32)
    ang = (freq[:, None] * pos[None, :]).astype(np.float32)
    return {"table": stays, "mixtable": mixing, "cos": np.tile(np.cos(ang), (4, 1)), "sin": np.tile(np.sin(ang), (4, 1))}


def kernel(**inputs):
    import numpy as np
    import concourse.bacc as bacc
    from concourse.bass_utils import run_bass_kernel_spmd

    nc = bacc.Bacc("TRN2", target_bir_lowering=False, num_devices=1)
    arrays, ins, outs = {}, {}, {}
    given = {name: inputs[name] for name in _INS}
    given.update(constants())
    for name, a in given.items():
        a = np.ascontiguousarray(a)
        arrays["in_" + name] = a
        ins[name] = nc.dram_tensor("in_" + name, a.shape, mybir.dt.from_np(a.dtype), kind="ExternalInput").ap()
    for name, shape in _OUTS:
        outs[name] = nc.dram_tensor("out_" + name, shape, F32, kind="ExternalOutput").ap()
    program(nc, ins, outs)
    r = run_bass_kernel_spmd(nc, [arrays], core_ids=[0])
    return tuple(r.results[0]["out_" + name] for name, _ in _OUTS)
```

```python
from contextlib import ExitStack

import concourse.bass as bass
from concourse import mybir

F32 = mybir.dt.float32
F32R = mybir.dt.float32r
I32 = mybir.dt.int32
ALU = mybir.AluOpType
ACT = mybir.ActivationFunctionType
AX = mybir.AxisListType.X

P = 128
D = 1024
KT = D // P
NMETA, SEQ = 16, 1024
NP = NMETA + SEQ
DB, DS = 8, 4
ND = DB * DS
T = NP + ND
PIECES = [(0, 384), (384, 384), (768, T - 768)]
NT = 9
TAIL = T - 8 * P
EPS = 1e-6
NEG = -1e30

H, NOPE, ROPE, VH = 8, 128, 64, 128
QL, KVL = 384, 256
SCALE = float((NOPE + ROPE) ** -0.5)
QT = 104
NQ = NP // QT
PAST, PAGE = 2048, 128
NPG = PAST // PAGE
POOL = DB * NPG * 5 // 4
FF = 4096
FG = 256
NG = FF // FG

RH, RN = 16, 64
W_SCALE = float(2.718281828459045 ** -0.5)
GN_EPS = 64e-5
CH = 128
LEVELS = 7
ATT_A = sum(-(-(q + 1) // 4) for q in range(NQ))
ATT_V = ATT_A + NQ
DVE_HEADS = 44
DVE_SAMPLES = 4
DVE_CHUNK = 40

R_MIX, R_FFN, R_FIN, R_MU, R_DW0, R_AW0, R_KK, R_KA, R_RK, R_QN, R_KVN, R_SHIFT = 0, 2, 4, 5, 11, 12, 13, 14, 15, 16, 17, 18
NROW = R_SHIFT + DB

def columns(*parts):
    at, out = 0, {}
    for name, n in parts:
        out[name] = (at, n)
        at += n
    return out, at


TABLE, NTABLE = columns(("ident", P), ("ones", P), ("halves", P), ("rot", P), ("causal", QT), ("new_keys", DB * ND))
MIXTAB, NMIXTAB = columns(("below", P), ("upto", P), ("tail_below", TAIL), ("tail_upto", TAIL), ("first_pairs", P),
                          ("siblings", 6 * P), ("restart", 8 * P), ("tail_restart", TAIL), ("seq_rows", 9),
                          ("seq_cols", 9 * TAIL), ("head_cols", 2))


class Tally:

    def __init__(self, sem, n=0):
        self.sem, self.n, self.i, self.step, self.start = sem, n, None, 0, 0

    def enter(self, i, step):
        self.i, self.step, self.start = i, step, self.n

    def leave(self, reps, name="", ring=1):
        assert self.step % ring == 0
        assert self.n - self.start == self.step, f"{name} step is {self.n - self.start}"
        self.i, self.n = None, self.start + reps * self.step

    def value(self, back=0):
        v = self.n - back
        return v if self.i is None or not self.step else self.i * self.step + v

    def add(self, ins, by=1):
        ins.then_inc(self.sem, by)
        self.n += by
        return ins

    def expect(self, by=1):
        self.n += by


class Fill:

    def __init__(self, eng, banks, filled, drained):
        self.eng, self.banks, self.filled, self.drained = eng, banks, Tally(filled), drained

    def bank(self, free=False):
        n = self.filled.n
        if n >= len(self.banks) and not free:
            self.eng.wait_ge(self.drained, self.filled.value(len(self.banks) - 1))
        return self.banks[n % len(self.banks)]

    def done(self, ins):
        self.filled.add(ins)

    def wait_drained(self, back=0):
        self.eng.wait_ge(self.drained, self.filled.value(back))


class Beat:

    def __init__(self, sem, per=1):
        self.sem, self.per, self.tally = sem, per, None

    def wait(self, eng, chunk, n=None):
        eng.wait_ge(self.sem, chunk * self.per + (self.per if n is None else n))


class Drain:

    def __init__(self, eng, banks, filled, drained):
        self.eng, self.banks, self.filled, self.drained = eng, banks, filled, Tally(drained)

    def bank(self):
        self.eng.wait_ge(self.filled, self.drained.value(-1))
        return self.banks[self.drained.n % len(self.banks)]


class Lane:

    def __init__(self, eng, order):
        self.eng, self.order, self.last = eng, Tally(order), None

    def do(self, ins, tally=None):
        self.last = self.order if tally is None else tally
        self.last.add(ins)

    def settle(self):
        self.eng.wait_ge(self.last.sem, self.last.value())


def program(nc, A, O):
    ctx = ExitStack()
    with ctx:
        def sb(name, shape, dt=F32):
            return ctx.enter_context(nc.sbuf_tensor(name, shape, dt))

        def sem(name):
            return ctx.enter_context(nc.semaphore(name))

        banks = [ctx.enter_context(nc.psum_tensor(f"bank{i}", [P, 512], F32)) for i in range(8)]
        BA, BV = banks[0:4], banks[4:8]

        hT = sb("hT", [P, KT, T])
        table = sb("table", [P, NTABLE])
        prm = sb("prm", [P, KT, NROW])
        std = sb("std", [P, T])
        eps = sb("eps", [P, 2])
        ARENA = 42300
        with ExitStack() as place:
            def piece(name, shape, dt=F32R):
                return place.enter_context(nc.sbuf_tensor(name, shape, dt))

            n_hi, n_lo = piece("n_hi", [P, KT, T]), piece("n_lo", [P, KT, T])
            with nc.sbuf_tensor("n32", [P, KT, T], F32) as n32:
                pass
            u_hi, u_lo = piece("u_hi", [P, 2, T]), piece("u_lo", [P, 2, T])
            up_hi, up_lo = piece("up_hi", [P, KT, FG]), piece("up_lo", [P, KT, FG])
            dn_hi, dn_lo = piece("dn_hi", [P, 2, D]), piece("dn_lo", [P, 2, D])
        SPLIT = 2 * (KT + 2) * T + 4 * KT * FG
        arena = sb("arena", [P, ARENA])

        class Carve:

            def __init__(self, at=0):
                self.at = at

            def __call__(self, *dims):
                n = 1
                for d in dims:
                    n *= d
                v = arena[:, self.at:self.at + n]
                self.at += n
                assert self.at <= ARENA, self.at
                if len(dims) == 1:
                    return v
                names = "abcde"[:len(dims)]
                pattern = f"p ({' '.join(names)}) -> p {' '.join(names)}"
                return v.rearrange(pattern, **{k: d for k, d in zip(names[1:], dims[1:])})

        def tab(name, rows=P):
            at, n = TABLE[name]
            return table[0:rows, at:at + n]

        ident, ones, halves, rot = tab("ident"), tab("ones"), tab("halves"), tab("rot")

        c = Carve()
        nT = c(KT, T)
        c_in = Carve(c.at)
        xin = c_in(NT, D)
        rows_in = c_in(D)
        m = Carve(c.at)
        oT = m(KT, T)
        cq = m(3, T)
        ckv = m(2, T)
        kraw = m(T)
        kfull = m(T)
        kz = m(2, T)
        cosT = m(T)
        sinT = m(T)
        qlat = m(3, DB, H * DS)
        olT = m(2, H, DB, DS)
        wa = Carve(m.at)(KT, 768)
        n2 = Carve()
        ctok = n2(NQ + 1, KVL + ROPE)
        n3 = Carve(n2.at)
        qraw = n3(T)
        rtmp = n3(T)
        vtok = n3(NQ * VH)
        m2 = Carve(m.at)
        wq = m2(3, 384)
        wqp = m2(3, P)
        wkv = m2(2, 512)
        wukT = m2(2 * P)
        qpe = m2(T)
        qn = [m2(T) for _ in range(2)]
        kn = [m2(T) for _ in range(2)]
        probs = [m2(NP) for _ in range(2)]
        stat = m2(2, 4)
        pT = [m2(NQ * QT), n3(NQ * QT)]
        assert n3.at <= c.at
        n4 = Carve(n2.at)
        cT = [n4(3, 512) for _ in range(2)]
        pTd = n4(NPG + 1, ND)
        qcur = n4(3, ND)
        ol = n4(KVL)
        dstat = n4(4)
        assert n4.at <= c.at
        m3 = Carve(m.at)
        dlat = [m3(NPG, KVL) for _ in range(2)]
        drope = [m3(NPG, P), Carve(c.at + (KT + 9) * T)(NPG, P)]
        sd = Carve(c.at + KT * T)(PAST + ND)
        wv = Carve(c.at + (KT + 7) * T)(2, H, VH)
        wo = Carve(m.at)(KT, D)
        norm_squares = [n32, Carve(ARENA - 1024 - KT * T)(KT, T)]
        f = Carve(SPLIT)
        w_up = [f(KT, FG) for _ in range(2)]
        w_dn = [f(2, D) for _ in range(2)]
        relu = [f(384) for _ in range(4)]
        g = Carve(c.at)
        lora = g(T)
        gate = g(T)
        xm = [g(KT, T) for _ in range(2)]
        wb = [g(KT, 256) for _ in range(2)]
        wl = g(KT, P)
        wg = g(KT, P)
        stage = [g(NT * 256) for _ in range(2)]
        shift_out = stage[0][0:9, 0:D]
        q = Carve(c.at + 2 * T)
        zT = nT
        mixtab = q(NMIXTAB)
        w_dec, w_rate, w_gate = q(D), q(D), q(D)
        lnw, lnb = q(D), q(D)
        S, Sm = q(8, P), q(8, P)
        rc, kc = q(8, P), q(8, P)
        zx = Carve()
        AR = [q(8, 2, P), zx(8, 2, P)]
        vt = [q(D), std[:, 0:D]]
        P1, SA, zbuf = zx(512), zx(512), zx(8, P)
        Bt, Kt = q(8, P), q(8, P)
        bz_at = q.at
        Bz, Kz = q(8, 2, P), q(8, 2, P)
        Btok, Ktok = q(D), q(D)
        sw, rate, pinc, pinv, cum, kk, kx = [q(8, P) for _ in range(7)]
        y = q(D)
        hx = hT[:, :, :].rearrange("p k t -> p (k t)")
        MR = [hx[:, i * 1024:(i + 1) * 1024] for i in range(2)]
        NR = [hx[:, (2 + i) * 1024:(3 + i) * 1024] for i in range(2)]
        XT = [hx[:, (8 + i) * 512:(9 + i) * 512] for i in range(2)]
        X = [hx[:, (10 + i) * 512:(11 + i) * 512] for i in range(2)]
        W = [hx[:, (12 + i) * 512:(13 + i) * 512] for i in range(2)]
        small = hx[:, 16 * 512:KT * T]
        mean, var, mid, dmid, dend = [small[:, i * 16:(i + 1) * 16] for i in range(5)]
        coef = [small[:, (5 + i) * 16:(6 + i) * 16] for i in range(2)]
        gc = small[:, 7 * 16:7 * 16 + P]

        def mix(name, rows=P):
            at, n = MIXTAB[name]
            return mixtab[0:rows, at:at + n]

        P1_tail, SA_tail = [t.rearrange("p k t -> p (k t)") for t in (cum, kk)]
        Bm, Km = [t.rearrange("p k t -> p (k t)") for t in (rate, pinv)]
        wo2_a = Carve(c.at + 2 * T + NMIXTAB)(5, D)
        wo2_b = Carve(bz_at)(3, D)
        assert bz_at + 3 * D <= ARENA - 1024 - KT * T
        mixw_n = 6 * 16
        out_n = 4 * 16

        yout = Carve(c.at)(NT, D)

        meet_s = sem("all_engines_here")
        a_filled, a_drained = sem("a_filled"), sem("a_drained")
        v_filled, v_drained = sem("v_filled"), sem("v_drained")
        act_order, dve_order = sem("act_order"), sem("dve_order")
        mark = {}
        in_s, rows_s, zero_s = sem("tables_loaded"), sem("rows_loaded"), sem("zeroed")
        sq_s, norm_s = sem("squares_ready"), sem("normed_ready")
        wa_s, rope_s, kz_s = sem("w_a_loaded"), sem("roped"), sem("kz_ready")
        out_s, eps_s = sem("stored"), sem("eps_ready")
        wq_s, wq_used, wkv_used = sem("w_q_loaded"), sem("w_q_used"), sem("w_kv_used")
        max_s, exp_s, prob_s = sem("max_ready"), sem("exp_ready"), sem("probs_ready")
        page_s = [sem(f"pages_loaded{i}") for i in range(2)]
        page_used, pt_s, qcur_s = sem("pages_used"), sem("page_table_loaded"), sem("q_copied")
        wv_s, wo_s, narrow_s = sem("w_v_loaded"), sem("w_o_loaded"), sem("narrow_waits")
        up_s = [sem(f"w_up_loaded{i}") for i in range(2)]
        dn_s = [sem(f"w_down_loaded{i}") for i in range(2)]
        u_s, hi_s, lo_s = sem("u_ready"), sem("weights_rounded"), sem("weights_split")
        nhi_s, nlo_s = sem("normed_rounded"), sem("normed_split")
        pages = ctx.enter_context(nc.sbuf_tensor("pages", [1, DB * NPG], I32))

        hid_s = sem("hidden_stored")
        xm_s, xm_used = sem("mixed_ready"), sem("mixed_used")
        wb_s = [sem(f"w_mix_loaded{i}") for i in range(2)]
        wb_used, wl_s, stg_s = sem("w_mix_used"), sem("w_lora_loaded"), [sem(f"staged_stored{i}") for i in range(2)]
        rk_in, v_in, z_out = Beat(sem("r_k_loaded"), 32), [Beat(sem(f"v_loaded{i}"), 16) for i in range(2)], Beat(sem("z_stored"), 16)
        scaled_b, gn_b = Beat(sem("outputs_scaled")), Beat(sem("outputs_normed"))
        coef_b, y_b, zt_b = Beat(sem("bonus_factors")), Beat(sem("outputs_ready")), Beat(sem("z_turned"))
        sw_b, rate_b, cum_b, dec_b = Beat(sem("decay_rates")), Beat(sem("rates")), Beat(sem("decay_sums")), Beat(sem("decays"))
        cumx_b, decx_b, kk_b, sq_b = Beat(sem("sums_before")), Beat(sem("decays_before")), Beat(sem("keys_scaled")), Beat(sem("keys_squared"))
        clamp_b, root_b, r_b, b_b, bk_b = [Beat(sem(n)) for n in ("norms_clamped", "norms", "r_ready", "b_ready", "b_k_ready")]
        split_b, bonus_b, gc_b, x1_b = Beat(sem("b_k_split")), Beat(sem("bonus_ready")), Beat(sem("gate_copied")), Beat(sem("first_inverse"), 4)
        yc_b, ysq_b, var_b, ystd_b, z_b = Beat(sem("centred")), Beat(sem("centred_squared")), Beat(sem("variances")), Beat(sem("deviations")), Beat(sem("z_ready"))
        s_b = Beat(sem("state_scaled"))
        mixw_s, pool_order, z_back = sem("mix_tables_loaded"), sem("pool_order"), sem("z_loaded")
        st_in, st_used, st_ready, st_s2 = sem("state_loaded"), sem("state_in_used"), sem("state_turned"), sem("state_stored")
        arm_s, arm_used, bm_s, bm_used, snew_s = sem("queries_masked"), sem("masked_used"), sem("keys_masked"), sem("keys_masked_used"), sem("state_new")
        wo2_s = sem("w_out_loaded")
        r_d = nc.dram_tensor("r_scratch", (NT, P, 8, P), F32).ap()
        k_d = nc.dram_tensor("k_scratch", (NT, P, 8, P), F32).ap()
        v_d = nc.dram_tensor("v_scratch", (NT, P, D), F32).ap()
        z_d = nc.dram_tensor("z_scratch", (P, KT, 8 * P), F32).ap()
        h_d = nc.dram_tensor("hidden_scratch", (P, KT * T), F32).ap()

        def meet(eng, here):
            here.add(eng.drain())
            here.n += 4
            eng.wait_ge(meet_s, here.n)

        block = ctx.enter_context(nc.Block())

        @block.tensor
        def _(pe):
            here = Tally(meet_s)
            ra = Fill(pe, BA, a_filled, a_drained)
            rv = Fill(pe, BV, v_filled, v_drained)
            sq_t, norm_t = Tally(sq_s), Tally(norm_s)
            wq_t, wkv_t, prob_t = Tally(wq_s), Tally(wkv_used), Tally(prob_s)

            def mm(out, lhsT, rhs, first, last, group=False):
                return pe.matmul(out, lhsT, rhs, start=first, stop=last, skip_group_check=group)

            def apart(semaphore, value):
                pe.wait_ge(semaphore, value)
                pe.sem_inc(narrow_s, 1)

            def turn(out, src, rows):
                return pe.transpose(out, src, ident[0:rows, 0:rows])

            def norm(scratch, n):
                for at, w in PIECES:
                    sq_t.expect()
                    pe.wait_ge(sq_s, sq_t.n)
                    b = ra.bank()
                    for k in range(n):
                        ins = mm(b[:, 0:w], ones, scratch[:, k, at:at + w], k == 0, k == n - 1)
                    ra.done(ins)

            def normed():
                norm_t.expect(3)
                pe.wait_ge(norm_s, norm_t.n)

            def product(ring, weights, acts, n, m=P, at=0, w=P):
                b = ring.bank()
                for k in range(n):
                    ins = mm(b[0:m, 0:w], weights(k), acts(k), k == 0, k == n - 1)
                ring.done(ins)

            pe.wait_ge(in_s, 192)
            pe.wait_ge(rows_s, 192)
            b = rv.bank()
            for k in range(KT):
                ins = turn(b[:, k * NROW:(k + 1) * NROW], rows_in[0:NROW, k * P:(k + 1) * P], NROW)
            rv.done(ins)
            for t in range(NT):
                w = P if t < 8 else TAIL
                for half, ring in enumerate((ra, rv)):
                    b = ring.bank()
                    for k in range(4):
                        ins = turn(b[:, k * w:(k + 1) * w], xin[0:w, t, (4 * half + k) * P:(4 * half + k + 1) * P], w)
                    ring.done(ins)
            meet(pe, here)

            mark["norm0"] = ra.filled.n
            norm(nT, KT)
            normed()
            pe.wait_ge(wa_s, 64)
            mark["down"] = rv.filled.n
            for k in range(6):
                for at, w in PIECES:
                    product(ra if k < 3 else rv, lambda j: wa[:, j, k * P:(k + 1) * P],
                            lambda j: nT[:, j, at:at + w], KT, w=w)
            mark["norm_q"] = ra.filled.n
            norm(oT, 3)
            rv.wait_drained()
            for at, w in PIECES:
                product(rv, lambda j: rot, lambda j: kraw[:, at:at + w], 1, w=w)
            norm(oT[:, 3:5, :], 2)
            norm_t.expect(3)
            normed()
            meet(pe, here)
            mark["latents"] = ra.filled.n
            for t in range(NQ + 1):
                w = QT if t < NQ else ND
                b = ra.bank()
                for k in range(2):
                    turn(b[0:w, k * P:(k + 1) * P], ckv[:, k, t * QT:t * QT + w], P)
                ra.done(turn(b[0:w, KVL:KVL + ROPE], kfull[0:ROPE, t * QT:t * QT + w], ROPE))
            with pe.Fori(0, H // 2) as i:
                ra.filled.enter(i, 2 * (8 + ATT_A))
                rv.filled.enter(i, 6 + 2 * (3 + ATT_V))
                prob_t.enter(i, 2 * NQ)
                wq_t.enter(i, 64)
                wkv_t.enter(i, 1)
                wq_t.expect(64)
                pe.wait_ge(wq_s, wq_t.value())
                for at, w in PIECES:
                    product(rv, lambda j: wqp[:, j, :], lambda j: cq[:, j, at:at + w], 3, w=w)
                rv.wait_drained()
                for at, w in PIECES:
                    product(rv, lambda j: rot, lambda j: qraw[:, at:at + w], 1, w=w)
                for hh in range(2):
                    for at, w in PIECES:
                        product(ra, lambda j: wq[:, j, hh * 192:hh * 192 + NOPE], lambda j: cq[:, j, at:at + w], 3, w=w)
                        product(rv, lambda j: wkv[:, j, hh * 256:hh * 256 + NOPE], lambda j: ckv[:, j, at:at + w], 2, w=w)
                    for t0, n in [(0, 4), (4, 4), (8, 2)]:
                        b = ra.bank()
                        for t in range(n):
                            for k in range(2):
                                ins = mm(b[0:QT, t * VH:(t + 1) * VH], ckv[:, k, (t0 + t) * QT:(t0 + t + 1) * QT],
                                         wkv[:, k, hh * 256 + NOPE:(hh + 1) * 256], k == 0, k == 1)
                        ra.done(ins)
                    b = ra.bank()
                    for k in range(2):
                        ins = turn(b[:, k * P:(k + 1) * P], wkv[:, k, hh * 256:hh * 256 + NOPE], P)
                    ra.done(ins)
                    ra.wait_drained()
                    rv.wait_drained()
                    b = ra.bank()
                    for k in range(2):
                        ins = mm(b[:, k * ND:(k + 1) * ND], wukT[:, k * P:(k + 1) * P], qn[hh][:, NP:T], True, True)
                    ra.done(ins)
                    if hh == 1:
                        wkv_t.add(pe.drain())

                    def scores(q):
                        for j in range(0, q + 1, 4):
                            n = min(4, q + 1 - j)
                            b = rv.bank()
                            mm(b[0:QT, 0:n * QT], qn[hh][:, q * QT:(q + 1) * QT], kn[hh][:, j * QT:(j + n) * QT], True, False)
                            rv.done(mm(b[0:QT, 0:n * QT], qpe[:, q * QT:(q + 1) * QT], kz[:, hh, j * QT:(j + n) * QT],
                                       False, True))

                    def turn_probs(q):
                        prob_t.expect()
                        pe.wait_ge(prob_s, prob_t.value())
                        for j in range(0, q + 1, 4):
                            n = min(4, q + 1 - j)
                            b = ra.bank()
                            for t in range(n):
                                ins = turn(b[0:QT, t * QT:(t + 1) * QT], probs[q % 2][0:QT, (j + t) * QT:(j + t + 1) * QT], QT)
                            ra.done(ins)

                    def values(q):
                        ra.wait_drained()
                        b = rv.bank()
                        for j in range(q + 1):
                            ins = mm(b[:, 0:QT], vtok[0:QT, j * VH:(j + 1) * VH], pT[q % 2][0:QT, j * QT:(j + 1) * QT],
                                     j == 0, j == q)
                        rv.done(ins)

                    for q in range(NQ + 2):
                        if q < NQ:
                            scores(q)
                        if q >= 2:
                            values(q - 2)
                        if 1 <= q <= NQ:
                            turn_probs(q - 1)
                ra.filled.leave(4, "pe heads a")
                rv.filled.leave(4, "pe heads v")
                prob_t.leave(4)
                wq_t.leave(4)
                wkv_t.leave(4)
            meet(pe, here)
            mark["samples"] = rv.filled.n
            page_t = [Tally(s) for s in page_s]
            used_t, qcur_t = Tally(page_used), Tally(qcur_s)
            with pe.Fori(0, DB // 2) as i:
                ra.filled.enter(i, 2 * 16)
                rv.filled.enter(i, 2 * 6)
                prob_t.enter(i, 2)
                used_t.enter(i, 2)
                qcur_t.enter(i, 2)
                for par in range(2):
                    page_t[par].enter(i, 48 * NPG)
                    page_t[par].expect(48 * NPG)
                    pe.wait_ge(page_s[par], page_t[par].value())
                    qcur_t.expect()
                    pe.wait_ge(qcur_s, qcur_t.value())

                    def turn_pages(n):
                        for k in range(3):
                            b = ra.bank()
                            for g in range(4):
                                src = dlat[par][:, 4 * n + g, k * P:(k + 1) * P] if k < 2 else drope[par][:, 4 * n + g, :]
                                ins = turn(b[:, g * P:(g + 1) * P], src, P)
                            ra.done(ins)

                    def score(rhs, w):
                        b = rv.bank()
                        for k in range(3):
                            ins = mm(b[0:ND, 0:w], qcur[:, k, :], rhs(k), k == 0, k == 2)
                        rv.done(ins)

                    turn_pages(0)
                    for n in range(4):
                        ra.wait_drained()
                        if n < 3:
                            turn_pages(n + 1)
                        score(lambda k: cT[n % 2][:, k, :], 512)
                    score(lambda k: ckv[:, k, NP:T] if k < 2 else kfull[:, NP:T], ND)
                    prob_t.expect()
                    apart(exp_s, prob_t.value())
                    for half in range(2):
                        b = ra.bank(free=True)
                        for n in range(NPG // 2):
                            at = (half * (NPG // 2) + n) * P
                            ins = turn(b[:, n * ND:(n + 1) * ND], sd[0:ND, at:at + P], ND)
                        ra.done(ins)
                    b = ra.bank(free=True)
                    ra.done(turn(b[0:ND, 0:ND], sd[0:ND, PAST:PAST + ND], ND))
                    ra.wait_drained()
                    b = rv.bank()
                    for n in range(NPG):
                        mm(b[0:ND, 0:KVL], pTd[:, n, :], dlat[par][:, n, :], n == 0, False)
                    rv.done(mm(b[0:ND, 0:KVL], pTd[0:ND, NPG, :], ctok[0:ND, NQ, 0:KVL], False, True))
                    used_t.add(pe.drain())
                    apart(v_drained, rv.filled.value())
                    b = ra.bank(free=True)
                    for k in range(2):
                        ins = turn(b[:, k * ND:(k + 1) * ND], ol[0:ND, k * P:(k + 1) * P], ND)
                    ra.done(ins)
                for t in (ra.filled, rv.filled, prob_t, used_t, qcur_t, page_t[0], page_t[1]):
                    t.leave(4, "pe samples")
            ra.wait_drained()
            pe.wait_ge(wv_s, 32)
            for h in range(H):
                product(rv, lambda j: wv[:, j, h, :], lambda j: olT[:, j, h, :, :].rearrange("p b q -> p (b q)"), 2, w=ND)
            meet(pe, here)
            pe.wait_ge(wo_s, 32)
            mark["adds0"] = rv.filled.n
            for at, w in PIECES:
                for k in range(KT):
                    product(rv, lambda j: wo[:, j, k * P:(k + 1) * P], lambda j: oT[:, j, at:at + w], H, w=w)

            u_t, lo_t, nlo_t = Tally(u_s), Tally(lo_s), Tally(nlo_s)

            def product3(ring, weights, acts, n, w):
                (w_hi, w_lo), (x_hi, x_lo) = weights, acts
                b = ring.bank()
                for k in range(n):
                    mm(b[:, 0:w], w_hi(k), x_hi(k), k == 0, False)
                    mm(b[:, 0:w], w_hi(k), x_lo(k), False, False)
                    ins = mm(b[:, 0:w], w_lo(k), x_hi(k), False, k == n - 1)
                ring.done(ins)

            def feed(layer):
                mark[f"feed_norm{layer}"] = ra.filled.n
                norm(norm_squares[layer], KT)
                nlo_t.expect(3)
                pe.wait_ge(nlo_s, nlo_t.n)
                norm_t.expect(3)
                mark[f"feed{layer}"] = ra.filled.n
                mark[f"feed_v{layer}"] = rv.filled.n
                u_t.expect(4)
                with pe.Fori(0, NG // 2) as i:
                    ra.filled.enter(i, 12)
                    rv.filled.enter(i, 48)
                    u_t.enter(i, 12)
                    lo_t.enter(i, 4)
                    for par in range(2):
                        lo_t.expect()
                        pe.wait_ge(lo_s, lo_t.value())
                        for k in range(2):
                            cols = slice(k * P, (k + 1) * P)
                            for at, w in PIECES:
                                product3(ra, (lambda j: up_hi[:, j, cols], lambda j: up_lo[:, j, cols]),
                                         (lambda j: n_hi[:, j, at:at + w], lambda j: n_lo[:, j, at:at + w]), KT, w)
                                u_t.expect()
                        lo_t.expect()
                        pe.wait_ge(lo_s, lo_t.value())
                        pe.wait_ge(u_s, u_t.value())
                        for k in range(KT):
                            cols = slice(k * P, (k + 1) * P)
                            for at, w in PIECES:
                                product3(rv, (lambda j: dn_hi[:, j, cols], lambda j: dn_lo[:, j, cols]),
                                         (lambda j: u_hi[:, j, at:at + w], lambda j: u_lo[:, j, at:at + w]), 2, w)
                    ra.filled.leave(NG // 2, "pe feed a", 4)
                    rv.filled.leave(NG // 2, "pe feed v", 4)
                    u_t.leave(NG // 2)
                    lo_t.leave(NG // 2)

            feed(0)
            meet(pe, here)
            mark["norm1"] = ra.filled.n
            norm(nT, KT)
            normed()
            mark["shift"] = ra.filled.n
            for half in range(2):
                b = ra.bank()
                for k in range(4):
                    ins = turn(b[0:9, k * P:(k + 1) * P], nT[:, 4 * half + k, NP - 1:T:DS], P)
                ra.done(ins)
            mark["mixing"] = ra.filled.n
            wb_t, xm_t, xu_t, wbu_t = [Tally(s) for s in wb_s], Tally(xm_s), Tally(xm_used), Tally(wb_used)
            pe.wait_ge(wl_s, 48)

            def mixed(n):
                xm_t.expect()
                pe.wait_ge(xm_s, xm_t.n)
                return xm[n % 2]

            def through(tally):
                tally.add(pe.drain())

            def lora_in(n, weights):
                x = mixed(n)
                for at, w in PIECES:
                    product(ra, lambda j: weights[:, j, :], lambda j: x[:, j, at:at + w], KT, w=w)
                through(xu_t)

            def big(n, token_major):
                x = mixed(n)
                with pe.Fori(0, 2) as i:
                    ra.filled.enter(i, 12)
                    wbu_t.enter(i, 2)
                    for par in range(2):
                        wb_t[par].enter(i, 16)
                        wb_t[par].expect(16)
                        pe.wait_ge(wb_s[par], wb_t[par].value())
                        if token_major:
                            for tiles in [(0, 1), (2, 3), (4, 5), (6,), (7,), (8,)]:
                                b = ra.bank()
                                for u, t in enumerate(tiles):
                                    w = P if t < 8 else TAIL
                                    for k in range(KT):
                                        ins = mm(b[0:w, u * 256:(u + 1) * 256], x[:, k, t * P:t * P + w], wb[par][:, k, :],
                                                 k == 0, k == KT - 1)
                                ra.done(ins)
                        else:
                            for m_ in range(2):
                                for at, w in PIECES:
                                    product(ra, lambda j: wb[par][:, j, m_ * P:(m_ + 1) * P], lambda j: x[:, j, at:at + w],
                                            KT, w=w)
                        through(wbu_t)
                        wb_t[par].leave(2)
                    ra.filled.leave(2, "pe big", 4)
                    wbu_t.leave(2)
                through(xu_t)

            big(0, False)
            lora_in(1, wl)
            big(2, False)
            lora_in(3, wl)
            big(4, True)
            lora_in(5, wg)
            meet(pe, here)
            pe.wait_ge(mixw_s, mixw_n)
            pe.wait_ge(zero_s, 2)
            mark["chunks_a"], mark["chunks_v"] = ra.filled.n, rv.filled.n

            def decays(at, w):
                for wt in (w_dec, w_rate):
                    for half in range(2):
                        b = ra.bank()
                        for k in range(4):
                            ins = mm(b[:, k * w:(k + 1) * w], wt[:, (4 * half + k) * P:(4 * half + k + 1) * P],
                                     lora[:, bass.ds(at, w)], True, True)
                        ra.done(ins)

            def key_sums(c, w):
                sq_b.wait(pe, c)
                for half in range(2):
                    b = rv.bank()
                    for k in range(4):
                        ins = mm(b[:, k * w:(k + 1) * w], halves, kx[:, 4 * half + k, 0:w], True, True)
                    rv.done(ins)

            def turn_b_k(c, w):
                bk_b.wait(pe, c)
                for src in (Bt, Kt):
                    for half in range(2):
                        b = ra.bank()
                        for k in range(4):
                            ins = turn(b[0:w, k * P:(k + 1) * P], src[:, 4 * half + k, 0:w], P)
                        ra.done(ins)

            def bonus_factors(c, w):
                bonus_b.wait(pe, c)
                for half in range(2):
                    b = ra.bank()
                    for k in range(4):
                        ins = mm(b[0:w, 2 * k:2 * k + 2], kx[:, 4 * half + k, 0:w], mix("head_cols"), True, True)
                    ra.done(ins)

            def gates(c, w):
                gc_b.wait(pe, c)
                for n in range(4):
                    b = rv.bank()
                    rv.done(mm(b[0:w, 0:256], gc[:, 0:w], w_gate[:, n * 256:(n + 1) * 256], True, True))

            def turn_z(c, w):
                z_b.wait(pe, c)
                for n in range(4):
                    b = ra.bank()
                    for k in range(2):
                        ct = 2 * n + k
                        ins = turn(b[:, k * w:(k + 1) * w], y[0:w, ct * P:(ct + 1) * P], w)
                    ra.done(ins)

            def inverses(c, first, hg, w, levels, ar, between):
                hb = hg // 2
                if first == 0:
                    split_b.wait(pe, c)
                    r_b.wait(pe, c)
                for gi in range(2):
                    for src in (Bz, Kz):
                        for half in range(2):
                            b = rv.bank()
                            for j in range(hb):
                                h = first + gi * hg + half * hb + j
                                ins = mm(b[0:w, j * 2 * w:(j + 1) * 2 * w].rearrange("p (a w) -> p a w", a=2),
                                         src[:, h // 2, h % 2, 0:w], ar[:, h // 2, :, 0:w], True, True)
                            rv.done(ins)

                def mat(m, gi, j):
                    return m[gi][0:w, j * w:(j + 1) * w]

                turned = [0, 0]

                def turn_group(gi):
                    b = ra.bank()
                    for j in range(hg):
                        ins = turn(b[0:w, j * w:(j + 1) * w], mat(XT, gi, j), w)
                    ra.done(ins)
                    turned[gi] = ra.filled.n

                for gi in range(2):
                    x1_b.wait(pe, c, first // hg + gi + 1)
                    turn_group(gi)
                between(0)
                for l in range(1, levels):
                    for gi in range(2):
                        ra.wait_drained(ra.filled.n - turned[gi])
                        b = rv.bank()
                        for j in range(hg):
                            ins = mm(b[0:w, j * w:(j + 1) * w], MR[gi][0:w, j * 2 * w:j * 2 * w + w], mat(X, gi, j), True, True)
                        rv.done(ins)
                    for gi in range(2):
                        rv.wait_drained(1)
                        b = rv.bank()
                        for j in range(hg):
                            ins = mm(b[0:w, j * w:(j + 1) * w], mat(W, gi, j), mat(XT, gi, j), True, True)
                        rv.done(ins)
                    if l < levels - 1:
                        for gi in range(2):
                            rv.wait_drained(1 - gi)
                            turn_group(gi)
                    else:
                        rv.wait_drained()
                    between(l)

            def chunk(c, par, nth, finish=True, prepare=True):
                ar, v = AR[par], vt[par]
                v_in[par].wait(pe, nth)
                turn_b_k(c, P)

                def between_first(l):
                    if l == 1:
                        bonus_factors(c, P)
                    if prepare and l == 4:
                        key_sums(c + 1, P)
                    if finish and l == 5:
                        gates(c - 1, P)
                    if finish and l == 6:
                        turn_z(c - 1, P)

                def between_second(l):
                    if prepare and l == 0:
                        decays((c + 1) * P, P)

                for d in range(2):
                    inverses(c, 8 * d, 4, P, LEVELS, ar, between_second if d else between_first)
                    s_b.wait(pe, c)
                    b = ra.bank()
                    for k in range(4):
                        mm(b[:, k * P:(k + 1) * P], ar[:, 4 * d + k, 0, :], Sm[:, 4 * d + k, :], k == 0, False, True)
                    for j in range(8):
                        h = 8 * d + j
                        ins = mm(b[:, j * RN:(j + 1) * RN], NR[j // 4][:, (j % 4) * 2 * P:(j % 4) * 2 * P + P],
                                 v[:, h * RN:(h + 1) * RN], False, j == 7, True)
                    ra.done(ins)
                    ra.wait_drained()
                    b = ra.bank()
                    for j in range(8):
                        ins = mm(b[:, j * RN:(j + 1) * RN], XT[j // 4][:, (j % 4) * P:(j % 4 + 1) * P],
                                 P1[:, j * RN:(j + 1) * RN], True, True)
                    ra.done(ins)
                    ra.wait_drained()
                    b = rv.bank()
                    for k in range(4):
                        ct = 4 * d + k
                        mm(b[:, k * P:(k + 1) * P], Btok[:, ct * P:(ct + 1) * P], SA[:, k * P:(k + 1) * P], True, False)
                        ins = mm(b[:, k * P:(k + 1) * P], Ktok[:, ct * P:(ct + 1) * P], v[:, ct * P:(ct + 1) * P], False, True)
                    rv.done(ins)
                    b = ra.bank()
                    for k in range(4):
                        mm(b[:, k * P:(k + 1) * P], ar[:, 4 * d + k, 1, :], Sm[:, 4 * d + k, :], k == 0, False, True)
                    for j in range(8):
                        h = 8 * d + j
                        m_at = (j % 4) * 2 * P + P
                        mm(b[:, j * RN:(j + 1) * RN], MR[j // 4][:, m_at:m_at + P], SA[:, j * RN:(j + 1) * RN], False, False, True)
                        ins = mm(b[:, j * RN:(j + 1) * RN], NR[j // 4][:, m_at:m_at + P], v[:, h * RN:(h + 1) * RN],
                                 False, j == 7, True)
                    ra.done(ins)

            decays(0, P)
            key_sums(0, P)
            chunk(0, 0, 0, finish=False)
            with pe.Fori(0, 3) as i:
                ra.filled.enter(i, 88)
                rv.filled.enter(i, 144)
                for u in range(2):
                    chunk(i * 2 + (u + 1), 1 - u, i + u)
                ra.filled.leave(3, "pe chunks a", 4)
                rv.filled.leave(3, "pe chunks v", 4)
            chunk(7, 1, 3, prepare=False)
            gates(7, P)
            turn_z(7, P)
            w = TAIL
            c = 8
            decays(8 * P, w)
            key_sums(c, w)
            turn_b_k(c, w)

            def between(l):
                if l == 1:
                    bonus_factors(c, w)

            v_in[0].wait(pe, 4)
            inverses(c, 0, 8, w, 4, AR[0], between)
            arm_t, used_t, sin_t, siu_t = Tally(arm_s), Tally(arm_used), Tally(st_in), Tally(st_used)

            acc = [BV[(rv.filled.n + n) % 4] for n in range(4)]
            rv.wait_drained()

            def state_in():
                sin_t.expect(32)
                pe.wait_ge(st_in, sin_t.value())
                for n in range(4):
                    b = ra.bank()
                    for k in range(2):
                        ins = turn(b[:, k * P:(k + 1) * P], rc[:, 2 * n + k, :], P)
                    ra.done(ins)
                siu_t.add(pe.drain())
                ra.wait_drained()

            def from_state(state, first):
                arm_t.expect()
                pe.wait_ge(arm_s, arm_t.value())
                for u in range(2):
                    for ct in range(8):
                        mm(acc[2 * u + ct // 4][0:w, (ct % 4) * P:(ct % 4 + 1) * P], Bz[:, ct, u, 0:w], state[:, ct, :],
                           first and ct % 4 == 0, False, True)
                used_t.add(pe.drain())

            from_state(S, True)
            with pe.Fori(0, DB) as i:
                ra.filled.enter(i, 4)
                for t in (arm_t, used_t, siu_t):
                    t.enter(i, 1)
                sin_t.enter(i, 32)
                state_in()
                from_state(kc, False)
                for t in (arm_t, used_t, siu_t, sin_t):
                    t.leave(DB)
                ra.filled.leave(DB, "pe states a", 4)
            for half in range(2):
                for j in range(8):
                    h = 8 * half + j
                    ins = mm(acc[half][0:w, j * RN:(j + 1) * RN], NR[half][0:w, j * 2 * w:j * 2 * w + w],
                             vt[0][0:w, h * RN:(h + 1) * RN], False, j == 7, True)
                rv.done(ins)
            rv.wait_drained()
            for half in range(2):
                b = ra.bank()
                for j in range(8):
                    h = 8 * half + j
                    ins = mm(b[0:w, j * RN:(j + 1) * RN], XT[half][0:w, j * w:(j + 1) * w],
                             P1_tail[0:w, h * RN:(h + 1) * RN], True, True)
                ra.done(ins)
            ra.wait_drained()
            for half in range(2):
                for j in range(8):
                    h = 8 * half + j
                    m_at = j * 2 * w + w
                    mm(acc[2 + half][0:w, j * RN:(j + 1) * RN], MR[half][0:w, m_at:m_at + w], SA_tail[0:w, h * RN:(h + 1) * RN],
                       False, False, True)
                    ins = mm(acc[2 + half][0:w, j * RN:(j + 1) * RN], NR[half][0:w, m_at:m_at + w],
                             vt[0][0:w, h * RN:(h + 1) * RN], False, j == 7, True)
                rv.done(ins)
            gates(c, w)
            turn_z(c, w)
            bm_t, bmu_t, sn_t = Tally(bm_s), Tally(bm_used), Tally(snew_s)

            def state_out():
                bm_t.expect()
                pe.wait_ge(bm_s, bm_t.value())
                for n in range(4):
                    b = rv.bank()
                    for k in range(2):
                        cols = slice((2 * n + k) * P, (2 * n + k + 1) * P)
                        mm(b[:, k * P:(k + 1) * P], Bm[0:w, cols], SA_tail[0:w, cols], True, False)
                        ins = mm(b[:, k * P:(k + 1) * P], Km[0:w, cols], vt[0][0:w, cols], False, True)
                    rv.done(ins)
                bmu_t.add(pe.drain())
                sn_t.expect()
                pe.wait_ge(snew_s, sn_t.value())
                for n in range(4):
                    b = ra.bank()
                    for k in range(2):
                        ins = turn(b[:, k * P:(k + 1) * P], kx[:, 2 * n + k, :], P)
                    ra.done(ins)

            mark["state_out"] = ra.filled.n
            state_out()
            with pe.Fori(0, DB) as i:
                ra.filled.enter(i, 8)
                rv.filled.enter(i, 4)
                for t in (bm_t, bmu_t, sn_t, siu_t):
                    t.enter(i, 1)
                sin_t.enter(i, 32)
                state_in()
                state_out()
                for t in (bm_t, bmu_t, sn_t, siu_t, sin_t):
                    t.leave(DB)
                ra.filled.leave(DB, "pe new states a", 4)
                rv.filled.leave(DB, "pe new states v", 4)
            meet(pe, here)
            pe.wait_ge(wo2_s, 32)
            pe.wait_ge(z_back, 16)
            mark["adds1"] = rv.filled.n
            for at, w in PIECES:
                for k in range(KT):
                    product(rv, lambda j: (wo2_a[:, j] if j < 5 else wo2_b[:, j - 5])[:, k * P:(k + 1) * P], lambda j: zT[:, j, at:at + w], KT, w=w)
            feed(1)
            meet(pe, here)
            mark["norm_final"] = ra.filled.n
            norm(nT, KT)
            normed()
            for t in range(NT):
                w = P if t < 8 else TAIL
                for half, ring in enumerate((ra, rv)):
                    b = ring.bank()
                    for k in range(4):
                        ins = turn(b[0:w, k * P:(k + 1) * P], nT[:, 4 * half + k, t * P:t * P + w], P)
                    ring.done(ins)
            mark["end_a"], mark["end_v"] = ra.filled.n, rv.filled.n

        @block.sync
        def _(sp):
            here = Tally(meet_s)
            in_t, rows_t, wa_t, out_t = Tally(in_s), Tally(rows_s), Tally(wa_s), Tally(out_s)

            def load(dst, src, tally):
                tally.add(sp.dma_start(dst, src), 16)

            load(table[:, :], A["table"], in_t)
            sp.wait_ge(zero_s, 1)
            for r, name, n in [(R_MIX, "norm_mix", 2), (R_FFN, "norm_ffn", 2)]:
                load(rows_in[r:r + n, :], A[name], rows_t)
            load(rows_in[R_FIN:R_FIN + 1, :], A["norm_final"].rearrange("(a d) -> a d", a=1), rows_t)
            load(rows_in[R_MU:R_MU + 6, :], A["rwkv_mu"][0], rows_t)
            for r, name in [(R_DW0, "rwkv_decay_w0"), (R_AW0, "rwkv_a_w0"), (R_KK, "rwkv_k_k"), (R_KA, "rwkv_k_a")]:
                load(rows_in[r:r + 1, :], A[name], rows_t)
            load(rows_in[R_RK:R_RK + 1, :], A["rwkv_r_k"].rearrange("a h n -> a (h n)"), rows_t)
            load(rows_in[R_SHIFT:NROW, :], A["state_shift"][0], rows_t)
            load(rows_in[R_QN:R_QN + 1, 0:QL], A["mla_q_a_norm"], rows_t)
            load(rows_in[R_KVN:R_KVN + 1, 0:KVL], A["mla_kv_a_norm"], rows_t)
            x = A["x_prompt"][0]
            load(xin[0:NMETA, 0, :], A["meta_tokens"], in_t)
            load(xin[NMETA:P, 0, :], x[0:P - NMETA, :], in_t)
            for t in range(1, 8):
                load(xin[:, t, :], x[t * P - NMETA:(t + 1) * P - NMETA, :], in_t)
            load(xin[0:NMETA, 8, :], x[8 * P - NMETA:SEQ, :], in_t)
            load(xin[NMETA:TAIL, 8, :], A["x_sample"].rearrange("b s d -> (b s) d"), in_t)
            meet(sp, here)
            w = A["mla_w_qkv_a"][0].rearrange("(k p) n -> p k n", p=P)
            load(wa[:, :, 0:704], w, wa_t)
            load(wa[:, :, 704:768], w[:, :, 640:704], wa_t)
            load(cosT, A["cos"], wa_t)
            load(sinT, A["sin"], wa_t)
            meet(sp, here)
            lat_p = O["lat_p"][0, 0].rearrange("(t p) n -> p t n", p=QT)
            rope_p = O["rope_p"][0, 0].rearrange("(t p) n -> p t n", p=QT)
            wq_t = Tally(wq_s)
            wqd = A["mla_w_q_b"][0].rearrange("(k p) n -> p k n", p=P)
            wkd = A["mla_w_kv_b"][0].rearrange("(k p) n -> p k n", p=P)

            def load_pair(i):
                load(wq, wqd[:, :, bass.ds(i * 384, 384)], wq_t)
                for hh in range(2):
                    load(wqp[:, :, hh * ROPE:(hh + 1) * ROPE], wqd[:, :, bass.ds(i * 384 + hh * 192 + NOPE, ROPE)], wq_t)
                load(wkv, wkd[:, :, bass.ds(i * 512, 512)], wq_t)

            load_pair(0)
            sp.wait_ge(a_drained, mark["latents"] + NQ + 1)
            load(lat_p, ctok[0:QT, 0:NQ, 0:KVL], out_t)
            load(rope_p, ctok[0:QT, 0:NQ, KVL:KVL + ROPE], out_t)
            load(O["lat_s"].rearrange("a b s n -> (a b s) n"), ctok[0:ND, NQ, 0:KVL], out_t)
            load(O["rope_s"].rearrange("a b s n -> (a b s) n"), ctok[0:ND, NQ, KVL:KVL + ROPE], out_t)
            with sp.Fori(0, H // 2 - 1) as i:
                wq_t.enter(i, 64)
                sp.wait_ge(wkv_used, i + 1)
                load_pair(i + 1)
                wq_t.leave(3, "wq")
            sp.wait_ge(out_s, out_t.n)
            meet(sp, here)
            pt_t, wv_t, wo_t = Tally(pt_s), Tally(wv_s), Tally(wo_s)
            load(pages[:, :], A["page_table"].rearrange("(a b) n -> a (b n)", a=1), pt_t)
            sp.wait_ge(pt_s, 16)
            for k in range(2):
                load(wv[:, k, :, :], A["mla_w_kv_b"][0, k * P:(k + 1) * P].rearrange("p (h n) -> p h n", n=256)[:, :, NOPE:256],
                     wv_t)
            page_t = [Tally(s) for s in page_s]

            def load_seq(b, par):
                for n in range(NPG):
                    page = sp.value_load(pages[0:1, bass.ds(b * NPG + n, 1)], min_val=0, max_val=POOL - 1)
                    src_l = A["cache_kv_latent"][0, bass.ds(page, 1), :, :].rearrange("a p n -> (a p) n")
                    src_r = A["cache_k_rope"][0, bass.ds(page, 1), :, :].rearrange("a p n -> (a p) n")
                    load(dlat[par][:, n, :], src_l, page_t[par])
                    load(drope[par][:, n, 0:ROPE], src_r, page_t[par])
                    load(drope[par][:, n, ROPE:P], src_r, page_t[par])

            load_seq(0, 0)
            load_seq(1, 1)
            with sp.Fori(0, DB // 2 - 1) as i:
                for par in range(2):
                    page_t[par].enter(i, 48 * NPG)
                    sp.wait_ge(page_used, i * 2 + par + 1)
                    load_seq((i + 1) * 2 + par, par)
                    page_t[par].leave(3, "page")
            w = A["mla_w_o"][0].rearrange("(k p) n -> p k n", p=P)
            for half in range(2):
                sp.wait_ge(page_used, DB - 1 + half)
                load(wo[:, 4 * half:4 * half + 4, :], w[:, 4 * half:4 * half + 4, :], wo_t)
            meet(sp, here)
            up_t, dn_t = [Tally(s) for s in up_s], [Tally(s) for s in dn_s]

            def feed_weights(layer):
                wu = A["ffn_w_up"][layer].rearrange("(k p) n -> p k n", p=P)
                wd = A["ffn_w_down"][layer].rearrange("(g k p) n -> p g k n", p=P, k=2)

                def group(g, par):
                    load(w_up[par], wu[:, :, bass.ds(g * FG, FG)], up_t[par])
                    load(w_dn[par], wd[:, bass.ds(g, 1), :, :].rearrange("p g k n -> p (g k) n"), dn_t[par])

                sp.wait_ge(a_filled, mark[f"feed_norm{layer}"] + 3)
                group(0, 0)
                group(1, 1)
                with sp.Fori(0, NG // 2 - 1) as i:
                    for par in range(2):
                        up_t[par].enter(i, 16)
                        dn_t[par].enter(i, 16)
                        sp.wait_ge(lo_s, i * 4 + layer * 2 * NG + 2 * par + 2)
                        group((i + 1) * 2 + par, par)
                        up_t[par].leave(NG // 2 - 1, "up")
                        dn_t[par].leave(NG // 2 - 1, "down")

            feed_weights(0)
            meet(sp, here)
            load(h_d, hT[:, :, :].rearrange("p k t -> p (k t)"), Tally(hid_s))
            wl_t = Tally(wl_s)
            for dst, name in [(wl[:, :, 0:64], "rwkv_decay_w1"), (wl[:, :, 64:P], "rwkv_a_w1"), (wg, "rwkv_g_w1")]:
                load(dst, A[name][0].rearrange("(k p) n -> p k n", p=P), wl_t)
            sp.wait_ge(a_drained, mark["shift"] + 2)
            load(O["shift_p"][0], shift_out[0:1, :], out_t)
            load(O["shift_s"][0], shift_out[1:9, :], out_t)
            wb_t = [Tally(s) for s in wb_s]
            n = 0
            for name in ("rwkv_w_r", "rwkv_w_k", "rwkv_w_v"):
                wd = A[name][0].rearrange("(k p) n -> p k n", p=P)
                for blk in range(4):
                    if n >= 2:
                        sp.wait_ge(wb_used, n - 1)
                    load(wb[n % 2], wd[:, :, blk * 256:(blk + 1) * 256], wb_t[n % 2])
                    n += 1
            sp.wait_ge(out_s, out_t.n)
            sp.wait_ge(hid_s, 16)
            meet(sp, here)
            mixw_t = Tally(mixw_s)
            load(mixtab, A["mixtable"], mixw_t)
            sp.wait_ge(zero_s, 2)
            load(w_dec[0:64, :], A["rwkv_decay_w2"][0], mixw_t)
            load(w_rate[64:P, :], A["rwkv_a_w2"][0], mixw_t)
            load(w_gate, A["rwkv_g_w2"][0], mixw_t)
            load(lnw, A["rwkv_ln_w"][0].partition_broadcast(P), mixw_t)
            load(lnb, A["rwkv_ln_b"][0].partition_broadcast(P), mixw_t)
            rk_t, v_t, st_t = Tally(rk_in.sem), [Tally(v.sem) for v in v_in], Tally(st_in)

            def load_r_k(c):
                load(rc, r_d[bass.ds(c, 1)].rearrange("a p k t -> p (a k) t"), rk_t)
                load(kc, k_d[bass.ds(c, 1)].rearrange("a p k t -> p (a k) t"), rk_t)

            def load_v(c, par):
                load(vt[par], v_d[bass.ds(c, 1)].rearrange("a p d -> p (a d)"), v_t[par])

            load_r_k(0)
            load_v(0, 0)
            load_v(1, 1)
            bonus_b.wait(sp, 0)
            load_r_k(1)
            with sp.Fori(0, 3) as i:
                for u in range(2):
                    bonus_b.wait(sp, i * 2 + (u + 1))
                    load_r_k(i * 2 + (u + 2))
                    z_b.wait(sp, i * 2 + u)
                    load_v(i * 2 + (u + 2), u)
            bonus_b.wait(sp, 7)
            for dst, src in [(rc, r_d), (kc, k_d)]:
                load(dst[:, :, 0:TAIL], src[8, :, :, 0:TAIL], rk_t)
            z_b.wait(sp, 6)
            load(vt[0][0:TAIL, :], v_d[8, 0:TAIL, :], v_t[0])
            z_out.wait(sp, 7)
            z_b.wait(sp, 7)
            load(zT[:, :, 0:8 * P], z_d[:, :, :], Tally(z_back))

            def load_state(j):
                src = A["state_wkv"][0, bass.ds(j, 1)].rearrange("b (c z) v k -> z v (b c) k", z=2)
                for z in range(2):
                    load(rc[z * RN:(z + 1) * RN, :, z * RN:(z + 1) * RN], src[z], st_t)

            sp.wait_ge(zero_s, 3)
            load_state(0)
            with sp.Fori(1, DB) as i:
                sp.wait_ge(st_used, i)
                load_state(i)
            z_b.wait(sp, 8)
            with sp.Fori(0, DB) as i:
                sp.wait_ge(st_used, i + DB)
                load_state(i)
                load(hx[:, bass.ds(i * T, T)], h_d[:, bass.ds(i * T, T)], Tally(hid_s))
            w = A["rwkv_w_o"][0].rearrange("(k p) n -> p k n", p=P)
            load(wo2_a, w[:, 0:5, :], Tally(wo2_s))
            load(wo2_b, w[:, 5:KT, :], Tally(wo2_s))
            meet(sp, here)
            feed_weights(1)
            meet(sp, here)
            sp.wait_ge(a_drained, mark["end_a"])
            sp.wait_ge(v_drained, mark["end_v"])
            yp = O["y_prompt"][0]
            load(yp[0:P - NMETA, :], yout[NMETA:P, 0, :], out_t)
            load(yp[P - NMETA:8 * P - NMETA, :].rearrange("(t p) d -> p t d", p=P), yout[:, 1:8, :], out_t)
            load(yp[8 * P - NMETA:SEQ, :], yout[0:NMETA, 8, :], out_t)
            load(O["y_sample"].rearrange("b s d -> (b s) d"), yout[NMETA:TAIL, 8, :], out_t)
            sp.wait_ge(out_s, out_t.n)

        @block.gpsimd
        def _(pool):
            here = Tally(meet_s)
            pool.memset(rows_in[0:NROW, :], 0.0).then_inc(zero_s, 1)
            pool.memset(kz[:, :, :], 0.0)
            pool.memset(qlat[:, 2, :, :], 0.0).then_inc(kz_s, 1)
            for _ in range(4):
                meet(pool, here)
            lo_t, hi_t = Tally(lo_s), Tally(hi_s)

            def feed(layer):
                with pool.Fori(0, NG // 2) as i:
                    lo_t.enter(i, 4)
                    hi_t.enter(i, 4)
                    for par in range(2):
                        for lo, raw, hi in ((up_lo, w_up[par], up_hi), (dn_lo, w_dn[par], dn_hi)):
                            hi_t.expect()
                            pool.wait_ge(hi_s, hi_t.value())
                            lo_t.add(pool.tensor_tensor(lo[:, :, :], raw[:, :, :], hi[:, :, :].bitcast(F32), ALU.subtract))
                    lo_t.leave(NG // 2)
                    hi_t.leave(NG // 2)

            feed(0)
            meet(pool, here)
            stg_t = [Tally(s) for s in stg_s]
            seen = Tally(a_drained, mark["mixing"])

            def store_mixed(scratch):
                with pool.Fori(0, 2) as i:
                    seen.enter(i, 12)
                    for par in range(2):
                        seen.expect(6)
                        pool.wait_ge(a_drained, seen.value())
                        t = stg_t[par]
                        if scratch is v_d:
                            t.enter(i, 32)
                            src = stage[par].rearrange("p (t n) -> p t n", n=256)
                            cols = bass.ds(i * 512 + par * 256, 256)
                            t.add(pool.dma_start(v_d[0:8, :, cols].rearrange("t p n -> p t n"), src[:, 0:8, :]), 16)
                            t.add(pool.dma_start(v_d[8, 0:TAIL, cols], src[0:TAIL, 8, :]), 16)
                        else:
                            t.enter(i, 64)
                            for m_ in range(2):
                                src = stage[par][:, m_ * T:(m_ + 1) * T]
                                ct = bass.ds(i * 4 + par * 2 + m_, 1)
                                t.add(pool.dma_start(scratch[0:8, :, ct, :].rearrange("c p a t -> p c (a t)"),
                                                     src[:, 0:8 * P].rearrange("p (c t) -> p c t", c=8)), 16)
                                t.add(pool.dma_start(scratch[8, :, ct, 0:TAIL].rearrange("p a t -> p (a t)"),
                                                     src[:, 8 * P:T]), 16)
                        t.leave(2, "pool store")
                    seen.leave(2, "pool seen")
                seen.expect(3)

            for scratch in (r_d, k_d, v_d):
                store_mixed(scratch)
            for par in range(2):
                pool.wait_ge(stg_s[par], stg_t[par].n)
            meet(pool, here)
            for buf in (w_dec, w_rate, S[:, :, :], Bz[:, :, :, :], Kz[:, :, :, :]):
                ins = pool.memset(buf, 0.0)
            ins.then_inc(zero_s, 1)
            lane = Lane(pool, pool_order)
            beats = [kk_b, r_b, bonus_b, cumx_b, gn_b]
            for beat in beats:
                beat.tally = Tally(beat.sem)
            pool.wait_ge(mixw_s, mixw_n)

            def wide(row, w):
                return prm[:, :, row:row + 1].broadcast_to([P, 8, w])

            def scale_keys(c, w):
                rk_in.wait(pool, c)
                lane.do(pool.tensor_tensor(kk[:, :, 0:w], kc[:, :, 0:w], wide(R_KK, w), ALU.mult), kk_b.tally)

            def decay_r(c, par, w):
                dec_b.wait(pool, c)
                lane.do(pool.tensor_tensor(AR[par][:, :, 1, 0:w], rc[:, :, 0:w], pinc[:, :, 0:w], ALU.mult), r_b.tally)

            def bonus(c, w):
                bk_b.wait(pool, c)
                lane.do(pool.tensor_tensor(kx[:, :, 0:w], kx[:, :, 0:w], rc[:, :, 0:w], ALU.mult))
                lane.settle()
                lane.do(pool.tensor_tensor(kx[:, :, 0:w], kx[:, :, 0:w], wide(R_RK, w), ALU.mult), bonus_b.tally)

            def bonus_terms(c, par, w):
                coef_b.wait(pool, c)
                lane.do(pool.tensor_tensor(sw[0:w].rearrange("p k t -> p (k t)").rearrange("p (h n) -> p h n", n=RN),
                                           vt[par][0:w].rearrange("p (h n) -> p h n", n=RN),
                                           coef[par][0:w, 0:RH].unsqueeze(2).broadcast_to([w, RH, RN]), ALU.mult))

            def sums_before(c, w):
                cum_b.wait(pool, c)
                lane.do(pool.tensor_tensor(sw[:, :, 0:w], cum[:, :, 0:w], sw[:, :, 0:w], ALU.subtract), cumx_b.tally)

            def group_norm(c, w):
                scaled_b.wait(pool, c)
                lane.do(pool.tensor_tensor(y[0:w, :], y[0:w, :], lnw[0:w, :], ALU.mult))
                lane.settle()
                lane.do(pool.tensor_tensor(y[0:w, :], y[0:w, :], lnb[0:w, :], ALU.add))
                lane.settle()
                lane.do(pool.tensor_tensor(y[0:w, :], y[0:w, :], sw[0:w].rearrange("p k t -> p (k t)"), ALU.add), gn_b.tally)

            def store_z(c):
                zt_b.wait(pool, c)
                pool.dma_start(z_d[:, :, bass.ds(c * P, P)], zbuf).then_inc(z_out.sem, 16)

            def chunk(c, par, finish=True, prepare=True):
                if finish:
                    bonus_terms(c - 1, 1 - par, P)
                if prepare:
                    scale_keys(c + 1, P)
                if finish:
                    group_norm(c - 1, P)
                    store_z(c - 1)
                if prepare:
                    sums_before(c + 1, P)
                    decay_r(c + 1, 1 - par, P)
                    bonus(c + 1, P)

            scale_keys(0, P)
            sums_before(0, P)
            decay_r(0, 0, P)
            bonus(0, P)
            chunk(0, 0, finish=False)
            with pool.Fori(0, 3) as i:
                lane.order.enter(i, 8)
                for beat in beats:
                    beat.tally.enter(i, 2)
                for u in range(2):
                    chunk(i * 2 + (u + 1), 1 - u)
                lane.order.leave(3, "pool chunks")
                for beat in beats:
                    beat.tally.leave(3)
            chunk(7, 1, prepare=False)
            bonus_terms(7, 1, P)
            group_norm(7, P)
            store_z(7)
            scale_keys(8, TAIL)
            sums_before(8, TAIL)
            decay_r(8, 0, TAIL)
            bonus(8, TAIL)
            lane.settle()
            pool.memset(rc[:, :, :], 0.0).then_inc(zero_s, 1)
            bonus_terms(8, 0, TAIL)
            group_norm(8, TAIL)
            so_t = Tally(st_s2)
            seen = Tally(a_drained, mark["state_out"])

            def store_state(dst):
                seen.expect(4)
                pool.wait_ge(a_drained, seen.value())
                d = dst.rearrange("b (c z) v k -> z v (b c) k", z=2)
                for z in range(2):
                    so_t.add(pool.dma_start(d[z], y[z * RN:(z + 1) * RN, :].rearrange("p (c k) -> p c k", k=P)[:, :, z * RN:(z + 1) * RN]), 16)

            store_state(O["wkv_p"][0])
            with pool.Fori(0, DB) as i:
                seen.enter(i, 8)
                so_t.enter(i, 32)
                seen.expect(4)
                store_state(O["wkv_s"][0, bass.ds(i, 1)])
                seen.leave(DB)
                so_t.leave(DB)
            pool.wait_ge(st_s2, so_t.n)
            meet(pool, here)
            feed(1)
            meet(pool, here)

        @block.scalar
        def _(act):
            here = Tally(meet_s)
            lane = Lane(act, act_order)
            ring = Drain(act, BA, a_filled, a_drained)
            sq_t, norm_t, max_t = Tally(sq_s), Tally(norm_s), Tally(max_s)

            def take(dst, rows, cols, view=None):
                b = ring.bank()[0:rows, 0:cols]
                lane.do(act.copy(dst, b if view is None else view(b)), ring.drained)

            def norm(src, scratch, n, adds=None):
                for i, (at, w) in enumerate(PIECES):
                    if adds is not None:
                        act.wait_ge(v_drained, adds + KT * (i + 1))
                    lane.do(act.activation(scratch[:, 0:n, at:at + w], src[:, 0:n, at:at + w], ACT.Square), sq_t)
                if norm_t.n:
                    act.wait_ge(norm_s, norm_t.n)
                for at, w in PIECES:
                    b = ring.bank()
                    lane.do(act.activation(std[:, at:at + w], b[:, 0:w], ACT.Sqrt, bias=eps[:, 0:1],
                                           scale=1.0 / (n * P)), ring.drained)
                norm_t.expect(3)

            for t in range(NT):
                w = P if t < 8 else TAIL
                take(hT[:, 0:4, t * P:t * P + w], P, 4 * w, lambda b: b.rearrange("p (k w) -> p k w", k=4))
            act.wait_ge(eps_s, 1)
            meet(act, here)
            norm(hT, nT, KT)
            for k in range(3):
                for at, w in PIECES:
                    take(cq[:, k, at:at + w], P, w)
            lane.settle()
            norm(cq, oT, 3)
            act.wait_ge(v_drained, mark["down"] + 9)
            norm(ckv, oT[:, 3:5, :], 2)
            meet(act, here)
            for t in range(NQ + 1):
                w = QT if t < NQ else ND
                take(ctok[0:w, t, :], w, KVL + ROPE)
            exp_t = Tally(exp_s)
            with act.Fori(0, H // 2) as i:
                ring.drained.enter(i, 2 * (8 + ATT_A))
                exp_t.enter(i, 2 * NQ)
                for hh in range(2):
                    for at, w in PIECES:
                        take(qn[hh][:, at:at + w], P, w)
                    for at, n in [(0, 4), (4, 4), (8, 2)]:
                        take(vtok[0:QT, at * VH:(at + n) * VH], QT, n * VH)
                    take(wukT, P, 2 * P)
                    b = ring.bank()
                    for k in range(2):
                        ins = act.copy(qlat[:, k, :, bass.ds((i * 2 + hh) * DS, DS)],
                                       b[:, k * ND:(k + 1) * ND].rearrange("p (b q) -> p b q", q=DS))
                    lane.do(ins, ring.drained)

                    def turn(q):
                        for j in range(0, q + 1, 4):
                            n = min(4, q + 1 - j)
                            take(pT[q % 2][0:QT, j * QT:(j + n) * QT], QT, n * QT)

                    for q in range(NQ):
                        act.wait_ge(max_s, exp_t.value(-1))
                        pr = probs[q % 2][0:QT, 0:(q + 1) * QT]
                        lane.do(act.activation(pr, pr, ACT.Exp, bias=stat[0:QT, q % 2, 1:2], scale=SCALE,
                                               accum_out=stat[0:QT, q % 2, 2:3]), exp_t)
                        if q >= 1:
                            turn(q - 1)
                    turn(NQ - 1)
                ring.drained.leave(4, "act heads")
                exp_t.leave(4)
            meet(act, here)
            with act.Fori(0, DB // 2) as i:
                ring.drained.enter(i, 2 * 16)
                exp_t.enter(i, 2)
                for par in range(2):
                    for n in range(4):
                        for k in range(3):
                            take(cT[n % 2][:, k, :], P, 512)
                    act.wait_ge(max_s, exp_t.value(-1))
                    lane.do(act.activation(sd[0:ND, :], sd[0:ND, :], ACT.Exp, bias=dstat[0:ND, 1:2], scale=SCALE,
                                           accum_out=dstat[0:ND, 2:3]), exp_t)
                    for half in range(2):
                        take(pTd[:, half * 8:half * 8 + 8, :], P, 8 * ND, lambda b: b.rearrange("p (n r) -> p n r", n=8))
                    take(pTd[0:ND, NPG, :], ND, ND)
                    b = ring.bank()
                    for k in range(2):
                        ins = act.copy(olT[:, k, :, bass.ds(i * 2 + par, 1), :],
                                       b[:, k * ND:(k + 1) * ND].rearrange("p (h a q) -> p h a q", h=H, a=1))
                    lane.do(ins, ring.drained)
                ring.drained.leave(4, "act samples")
                exp_t.leave(4)
            meet(act, here)
            u_t, hi_t, nhi_t = Tally(u_s), Tally(hi_s), Tally(nhi_s)
            up_t, dn_t = [Tally(s) for s in up_s], [Tally(s) for s in dn_s]

            def feed(layer):
                norm(hT, norm_squares[layer], KT, mark[f"adds{layer}"])
                for n, (at, w) in enumerate(PIECES):
                    act.wait_ge(norm_s, norm_t.n - 2 + n)
                    lane.do(act.activation(n_hi[:, :, at:at + w], n32[:, :, at:at + w], ACT.Copy), nhi_t)
                act.wait_ge(nlo_s, nhi_t.n)
                down = Tally(v_filled, mark[f"feed_v{layer}"])
                with act.Fori(0, NG // 2) as i:
                    ring.drained.enter(i, 12)
                    down.enter(i, 48)
                    u_t.enter(i, 12)
                    hi_t.enter(i, 4)
                    for par in range(2):
                        for t in (up_t[par], dn_t[par]):
                            t.enter(i, 16)
                            t.expect(16)
                        act.wait_ge(up_s[par], up_t[par].value())
                        lane.do(act.activation(up_hi[:, :, :], w_up[par][:, :, :], ACT.Copy), hi_t)
                        act.wait_ge(dn_s[par], dn_t[par].value())
                        act.wait_ge(v_filled, down.value())
                        lane.do(act.activation(dn_hi[:, :, :], w_dn[par][:, :, :], ACT.Copy), hi_t)
                        down.expect(24)
                        for k in range(2):
                            for at, w in PIECES:
                                b = ring.bank()
                                u_t.expect()
                                act.wait_ge(u_s, u_t.value())
                                lane.do(act.activation(relu[(u_t.n - 1) % 4][:, 0:w], b[:, 0:w], ACT.Relu), ring.drained)
                        up_t[par].leave(NG // 2)
                        dn_t[par].leave(NG // 2)
                    ring.drained.leave(NG // 2, "act feed")
                    down.leave(NG // 2)
                    u_t.leave(NG // 2)
                    hi_t.leave(NG // 2)
                u_t.expect(4)

            feed(0)
            meet(act, here)
            norm(hT, nT, KT)
            for half in range(2):
                take(shift_out[:, half * 512:(half + 1) * 512], 9, 512)
            act.wait_ge(out_s, out_n + 32)
            stg_t = [Tally(s) for s in stg_s]

            def lay_out(first, token_major):
                per = 32 if token_major else 64
                if first:
                    for i in range(2):
                        for par in range(2):
                            if i:
                                stg_t[par].expect(per)
                                act.wait_ge(stg_s[par], stg_t[par].n)
                            block_out(par, token_major)
                    return
                with act.Fori(0, 2) as i:
                    ring.drained.enter(i, 12)
                    for par in range(2):
                        t = stg_t[par]
                        act.wait_ge(stg_s[par], i * per + t.n + 64)
                        block_out(par, token_major)
                    ring.drained.leave(2, "act mixed")
                for t in stg_t:
                    t.expect(64 + per if per == 64 else 96)

            def block_out(par, token_major):
                if token_major:
                    for tiles in [(0, 1), (2, 3), (4, 5), (6,), (7,), (8,)]:
                        rows = P if tiles[0] < 8 else TAIL
                        take(stage[par][0:rows, tiles[0] * 256:(tiles[-1] + 1) * 256], rows, 256 * len(tiles))
                else:
                    for m_ in range(2):
                        for at, w in PIECES:
                            take(stage[par][:, m_ * T + at:m_ * T + at + w], P, w)

            lay_out(True, False)
            for at, w in PIECES:
                b = ring.bank()
                lane.do(act.activation(lora[0:64, at:at + w], b[0:64, 0:w], ACT.Tanh), ring.drained)
            lay_out(False, False)
            for at, w in PIECES:
                b = ring.bank()
                lane.do(act.copy(lora[64:P, at:at + w], b[64:P, 0:w]), ring.drained)
            lay_out(False, True)
            for at, w in PIECES:
                b = ring.bank()
                lane.do(act.activation(gate[:, at:at + w], b[:, 0:w], ACT.Sigmoid), ring.drained)
            meet(act, here)

            def signal(ins, beat):
                ins.then_inc(beat.sem, 1)

            def rates(c, w):
                for dst, row, beat in ((sw, R_DW0, sw_b), (rate, R_AW0, rate_b)):
                    for half in range(2):
                        b = ring.bank()
                        for k in range(4):
                            ct = 4 * half + k
                            ins = act.activation(dst[:, ct, 0:w], b[:, k * w:(k + 1) * w], ACT.Sigmoid,
                                                 bias=prm[:, ct, row:row + 1])
                        lane.do(ins, ring.drained)
                    signal(act.drain(), beat)

            def square_keys(c, w):
                kk_b.wait(act, c)
                signal(act.activation(kx[:, :, 0:w], kk[:, :, 0:w], ACT.Square), sq_b)

            def norms(c, w):
                clamp_b.wait(act, c)
                signal(act.activation(kx[:, :, 0:w], kx[:, :, 0:w], ACT.Sqrt), root_b)

            def decays(c, w, last=False):
                cum_b.wait(act, c)
                act.activation(pinc[:, :, 0:w], cum[:, :, 0:w], ACT.Exp, scale=-W_SCALE)
                if not last:
                    act.activation(dmid[:, 0:8], mid[:, 0:8], ACT.Exp, scale=-W_SCALE)
                signal(act.activation(pinv[:, :, 0:w], cum[:, :, 0:w], ACT.Exp, scale=W_SCALE), dec_b)
                cumx_b.wait(act, c)
                signal(act.activation(sw[:, :, 0:w], sw[:, :, 0:w], ACT.Exp, scale=-W_SCALE), decx_b)

            def split(src, dst, w):
                for z in range(2):
                    part = slice(z * RN, (z + 1) * RN)
                    ins = act.copy(dst[part, :, z, 0:w], src[part, :, 0:w])
                return ins

            def split_b_part(c, w):
                b_b.wait(act, c)
                split(Bt, Bz, w)

            def split_k_part(c, w):
                bk_b.wait(act, c)
                signal(split(Kt, Kz, w), split_b)

            def tokens(w):
                for dst in (Btok, Ktok):
                    for half in range(2):
                        take(dst[0:w, half * 512:(half + 1) * 512], w, 512)

            def bonus_factors(par, w):
                for half in range(2):
                    take(coef[par][0:w, half * 8:half * 8 + 8], w, 8)
                signal(act.drain(), coef_b)

            def inverses(hg, w, levels, between):
                for l in range(levels):
                    if l < levels - 1:
                        for gi in range(2):
                            take(X[gi][0:w, 0:hg * w], w, hg * w)
                    between(l)

            def squares(c, w):
                signal(act.copy(gc[:, 0:w], gate[:, bass.ds(c * P, w)]), gc_b)
                yc_b.wait(act, c)
                signal(act.activation(pinv[0:w].rearrange("p k t -> p (k t)"), y[0:w, :], ACT.Square), ysq_b)

            def deviations(c, w):
                var_b.wait(act, c)
                signal(act.activation(var[0:w, :], var[0:w, :], ACT.Sqrt, bias=eps[0:w, 1:2], scale=1.0 / RN), ystd_b)

            def take_z(dst, w):
                for n in range(4):
                    take(dst[:, 2 * n:2 * n + 2, :], P, 2 * w, lambda b: b.rearrange("p (k w) -> p k w", k=2))

            def z_to_store(c):
                if not isinstance(c, int) or c > 0:
                    z_out.wait(act, c - 1)
                take_z(zbuf, P)
                signal(act.drain(), zt_b)

            def chunk(c, par, finish=True, prepare=True):
                tokens(P)

                def between_first(l):
                    if l == 1:
                        bonus_factors(par, P)
                    if finish and l == 1:
                        squares(c - 1, P)
                    if prepare and l == 3:
                        square_keys(c + 1, P)
                    if finish and l == 3:
                        deviations(c - 1, P)
                    if prepare and l == 5:
                        norms(c + 1, P)
                    if finish and l == 6:
                        z_to_store(c - 1)

                def between_second(l):
                    if not prepare:
                        return
                    if l == 0:
                        rates(c + 1, P)
                    if l == 2:
                        decays(c + 1, P)
                    if l == 5:
                        split_b_part(c + 1, P)
                    if l == 6:
                        split_k_part(c + 1, P)

                for d in range(2):
                    inverses(4, P, LEVELS, between_second if d else between_first)
                    take(P1, P, 512)
                    take(SA, P, 512)
                    take(y[:, d * 512:(d + 1) * 512], P, 512)
                signal(act.drain(), y_b)

            def prepare_all(c, w, last=False):
                rates(c, w)
                square_keys(c, w)
                norms(c, w)
                decays(c, w, last)
                split_b_part(c, w)
                split_k_part(c, w)

            prepare_all(0, P)
            chunk(0, 0, finish=False)
            with act.Fori(0, 3) as i:
                ring.drained.enter(i, 88)
                for u in range(2):
                    chunk(i * 2 + (u + 1), 1 - u)
                ring.drained.leave(3, "act chunks")
            chunk(7, 1, prepare=False)
            squares(7, P)
            deviations(7, P)
            z_to_store(7)
            c = 8
            prepare_all(c, TAIL, True)
            tokens(TAIL)

            def between(l):
                if l == 1:
                    bonus_factors(0, TAIL)

            inverses(8, TAIL, 4, between)

            def state_in():
                for n in range(4):
                    take(kc[:, 2 * n:2 * n + 2, :], P, 256, lambda b: b.rearrange("p (k w) -> p k w", k=2))

            with act.Fori(0, DB) as i:
                ring.drained.enter(i, 4)
                state_in()
                ring.drained.leave(DB)
            for half in range(2):
                take(SA_tail[0:TAIL, half * 512:(half + 1) * 512], TAIL, 512)
            squares(8, TAIL)
            deviations(8, TAIL)
            act.wait_ge(z_back, 16)
            take_z(zT[:, :, 8 * P:T], TAIL)

            def state_out():
                for n in range(4):
                    take(y[:, n * 256:(n + 1) * 256], P, 256)

            state_out()
            with act.Fori(0, DB) as i:
                ring.drained.enter(i, 8)
                state_in()
                act.wait_ge(st_s2, i * 32 + 32)
                state_out()
                ring.drained.leave(DB)
            meet(act, here)
            feed(1)
            meet(act, here)
            norm(hT, nT, KT)
            for t in range(NT):
                w = P if t < 8 else TAIL
                take(yout[0:w, t, 0:512], w, 512)

        @block.vector
        def _(dve):
            here = Tally(meet_s)
            lane = Lane(dve, dve_order)
            ring = Drain(dve, BV, v_filled, v_drained)
            norm_t = Tally(norm_s)

            def take(dst, rows, cols, view=None):
                b = ring.bank()[0:rows, 0:cols]
                lane.do(dve.tensor_copy(dst, b if view is None else view(b)), ring.drained)

            def norm(src, dst, n, row, at_mark):
                seen = Tally(a_drained, at_mark)
                for at, w in PIECES:
                    seen.expect()
                    dve.wait_ge(a_drained, seen.n)
                    lane.do(dve.reciprocal(std[:, at:at + w], std[:, at:at + w]))
                    lane.settle()
                    for k in range(n):
                        ins = dve.scalar_tensor_tensor(out=dst[:, k, at:at + w], in0=src[:, k, at:at + w],
                                                       scalar=prm[:, k, row:row + 1], in1=std[:, at:at + w],
                                                       op0=ALU.mult, op1=ALU.mult)
                    lane.do(ins, norm_t)

            def add_hidden(k, at, w):
                b = ring.bank()
                lane.do(dve.tensor_tensor(hT[:, k, at:at + w], hT[:, k, at:at + w], b[:, 0:w], ALU.add), ring.drained)

            dve.memset(eps[:, 0:1], EPS)
            dve.memset(eps[:, 1:2], GN_EPS).then_inc(eps_s, 1)
            take(prm[:, :, :], P, KT * NROW, lambda b: b.rearrange("p (k r) -> p k r", k=KT))
            for t in range(NT):
                w = P if t < 8 else TAIL
                take(hT[:, 4:8, t * P:t * P + w], P, 4 * w, lambda b: b.rearrange("p (k w) -> p k w", k=4))
            meet(dve, here)
            norm(hT, nT, KT, R_MIX, mark["norm0"])
            for k in range(2):
                for at, w in PIECES:
                    take(ckv[:, k, at:at + w], P, w)
            for at, w in PIECES:
                take(kraw[:, at:at + w], P, w)
            norm(cq, cq, 3, R_QN, mark["norm_q"])
            dve.wait_ge(wa_s, 64)

            def rope(raw, out, tmp):
                lane.do(dve.tensor_tensor(out, raw, cosT, ALU.mult))
                lane.settle()
                for at, w in PIECES:
                    b = ring.bank()
                    lane.do(dve.tensor_tensor(tmp[:, at:at + w], b[:, 0:w], sinT[:, at:at + w], ALU.mult), ring.drained)
                lane.settle()
                lane.do(dve.tensor_tensor(out, out, tmp, ALU.add))
                lane.settle()

            rope(kraw, kfull, kraw)
            dve.wait_ge(kz_s, 1)
            lane.do(dve.tensor_copy(kz[0:ROPE, 0, :], kfull[0:ROPE, :]))
            lane.do(dve.tensor_copy(kz[ROPE:P, 1, :], kfull[ROPE:P, :]))
            norm(ckv, ckv, 2, R_KVN, mark["norm_q"] + 3)
            meet(dve, here)
            max_t, prob_t, exp_t = Tally(max_s), Tally(prob_s), Tally(exp_s)
            with dve.Fori(0, H // 2) as i:
                ring.drained.enter(i, 6 + 2 * (3 + ATT_V))
                lane.order.enter(i, DVE_HEADS)
                for t in (max_t, prob_t, exp_t):
                    t.enter(i, 2 * NQ)
                for at, w in PIECES:
                    take(qraw[:, at:at + w], P, w)
                lane.settle()
                rope(qraw, qpe, rtmp)
                for hh in range(2):
                    half = slice(hh * ROPE, (hh + 1) * ROPE)
                    lane.do(dve.tensor_copy(qlat[half, 2, :, bass.ds((i * 2 + hh) * DS, DS)],
                                            qpe[half, NP:T].rearrange("p (b q) -> p b q", q=DS)))
                for hh in range(2):
                    for at, w in PIECES:
                        take(kn[hh][:, at:at + w], P, w)

                    def maxima(q):
                        for j in range(0, q + 1, 4):
                            n = min(4, q + 1 - j)
                            b = ring.bank()
                            last = j + n == q + 1
                            if last:
                                if n > 1:
                                    dve.tensor_copy(probs[q % 2][0:QT, j * QT:q * QT], b[0:QT, 0:(n - 1) * QT])
                                lane.do(dve.tensor_tensor(probs[q % 2][0:QT, q * QT:(q + 1) * QT],
                                                          b[0:QT, (n - 1) * QT:n * QT], tab("causal", QT), ALU.add),
                                        ring.drained)
                            else:
                                lane.do(dve.tensor_copy(probs[q % 2][0:QT, j * QT:(j + n) * QT], b[0:QT, 0:n * QT]),
                                        ring.drained)
                        lane.settle()
                        lane.do(dve.tensor_reduce(stat[0:QT, q % 2, 0:1], probs[q % 2][0:QT, 0:(q + 1) * QT], AX, ALU.max))
                        lane.settle()
                        lane.do(dve.tensor_scalar(stat[0:QT, q % 2, 1:2], stat[0:QT, q % 2, 0:1], -SCALE, None, ALU.mult),
                                max_t)

                    def scaled(q):
                        exp_t.expect()
                        dve.wait_ge(exp_s, exp_t.value())
                        lane.do(dve.reciprocal(stat[0:QT, q % 2, 3:4], stat[0:QT, q % 2, 2:3]))
                        lane.settle()
                        pr = probs[q % 2][0:QT, 0:(q + 1) * QT]
                        lane.do(dve.tensor_scalar(pr, pr, stat[0:QT, q % 2, 3:4], None, ALU.mult), prob_t)

                    for q in range(NQ + 2):
                        if q < NQ:
                            maxima(q)
                        if q >= 2:
                            take(oT[:, bass.ds(i * 2 + hh, 1), (q - 2) * QT:(q - 1) * QT], P, QT,
                                 lambda b: b.rearrange("p (a w) -> p a w", a=1))
                        if 1 <= q <= NQ:
                            scaled(q - 1)
                ring.drained.leave(4, "dve heads v")
                lane.order.leave(4, "DVE_HEADS")
                for t in (max_t, prob_t, exp_t):
                    t.leave(4)
            meet(dve, here)
            qcur_t = Tally(qcur_s)
            with dve.Fori(0, DB // 2) as i:
                ring.drained.enter(i, 2 * 6)
                lane.order.enter(i, DVE_SAMPLES)
                for t in (max_t, exp_t, qcur_t):
                    t.enter(i, 2)
                for par in range(2):
                    b_ = i * 2 + par
                    lane.do(dve.tensor_copy(qcur[:, :, :], qlat[:, :, bass.ds(b_, 1), :].rearrange("p k b r -> p k (b r)")),
                            qcur_t)
                    for n in range(4):
                        take(sd[0:ND, n * 512:(n + 1) * 512], ND, 512)
                    b = ring.bank()
                    at = TABLE["new_keys"][0]
                    lane.do(dve.tensor_tensor(sd[0:ND, PAST:PAST + ND], b[0:ND, 0:ND],
                                              table[0:ND, bass.ds(b_ * ND + at, ND)], ALU.add), ring.drained)
                    lane.settle()
                    lane.do(dve.tensor_reduce(dstat[0:ND, 0:1], sd[0:ND, :], AX, ALU.max))
                    lane.settle()
                    lane.do(dve.tensor_scalar(dstat[0:ND, 1:2], dstat[0:ND, 0:1], -SCALE, None, ALU.mult), max_t)
                    exp_t.expect()
                    dve.wait_ge(exp_s, exp_t.value())
                    lane.do(dve.reciprocal(dstat[0:ND, 3:4], dstat[0:ND, 2:3]))
                    lane.settle()
                    b = ring.bank()
                    lane.do(dve.tensor_scalar(ol[0:ND, :], b[0:ND, 0:KVL], dstat[0:ND, 3:4], None, ALU.mult), ring.drained)
                ring.drained.leave(4, "dve samples v")
                lane.order.leave(4, "DVE_SAMPLES")
                for t in (max_t, exp_t, qcur_t):
                    t.leave(4)
            for h in range(H):
                take(oT[:, h, NP:T], P, ND)
            meet(dve, here)
            for at, w in PIECES:
                for k in range(KT):
                    add_hidden(k, at, w)
            u_t, nhi_t, nlo_t = Tally(u_s), Tally(nhi_s), Tally(nlo_s)

            def feed(layer):
                norm(hT, n32, KT, R_FFN + layer, mark[f"feed_norm{layer}"])
                for at, w in PIECES:
                    nhi_t.expect()
                    dve.wait_ge(nhi_s, nhi_t.n)
                    lane.do(dve.tensor_tensor(n_lo[:, :, at:at + w], n32[:, :, at:at + w], n_hi[:, :, at:at + w].bitcast(F32),
                                              ALU.subtract), nlo_t)
                u_t.add(dve.drain(), 4)
                seen = Tally(a_drained, mark[f"feed{layer}"])
                with dve.Fori(0, NG // 2) as i:
                    ring.drained.enter(i, 48)
                    seen.enter(i, 12)
                    u_t.enter(i, 12)
                    lane.order.enter(i, 24)
                    for par in range(2):
                        for k in range(2):
                            for at, w in PIECES:
                                r = relu[(seen.n - mark[f"feed{layer}"]) % 4][:, 0:w]
                                seen.expect()
                                dve.wait_ge(a_drained, seen.value())
                                lane.do(dve.tensor_tensor(r, r, r, ALU.mult))
                                lane.settle()
                                lane.do(dve.tensor_copy(u_hi[:, k, at:at + w], r))
                                lane.settle()
                                lane.do(dve.tensor_tensor(u_lo[:, k, at:at + w], r, u_hi[:, k, at:at + w].bitcast(F32),
                                                          ALU.subtract), u_t)
                        for k in range(KT):
                            for at, w in PIECES:
                                add_hidden(k, at, w)
                    ring.drained.leave(NG // 2, "dve feed v")
                    seen.leave(NG // 2)
                    u_t.leave(NG // 2)
                    lane.order.leave(NG // 2, "dve feed order")

            feed(0)
            meet(dve, here)
            norm(hT, nT, KT, R_MIX + 1, mark["norm1"])
            xm_t = Tally(xm_s)
            lane.settle()
            for n, row in enumerate((0, 1, 2, 4, 3, 5)):
                x = xm[n % 2]
                if n >= 2:
                    dve.wait_ge(xm_used, n - 1)
                lane.do(dve.tensor_tensor(x[:, :, 1:T], nT[:, :, 0:T - 1], nT[:, :, 1:T], ALU.subtract))
                lane.do(dve.tensor_scalar(x[:, :, 0:1], nT[:, :, 0:1], -1.0, None, ALU.mult))
                lane.settle()
                lane.do(dve.tensor_tensor(x[:, :, NP:T:DS], prm[:, :, R_SHIFT:NROW], nT[:, :, NP:T:DS], ALU.subtract))
                lane.settle()
                for k in range(KT):
                    ins = dve.scalar_tensor_tensor(out=x[:, k, :], in0=x[:, k, :], scalar=prm[:, k, R_MU + row:R_MU + row + 1],
                                                   in1=nT[:, k, :], op0=ALU.mult, op1=ALU.add)
                lane.do(ins, xm_t)
            meet(dve, here)
            dve.wait_ge(mixw_s, mixw_n)
            dve.wait_ge(zero_s, 2)
            hiddens = None

            def signal(ins, beat):
                lane.do(ins, beat.tally)

            def wide(row, w):
                return prm[:, :, row:row + 1].broadcast_to([P, 8, w])

            def flat(t, w):
                return t[0:w].rearrange("p k t -> p (k t)")

            def tt(out, a, b, op):
                lane.do(dve.tensor_tensor(out, a, b, op))

            def clamp(c, w):
                for half in range(2):
                    b = ring.bank()
                    lane.do(dve.tensor_scalar(kx[:, 4 * half:4 * half + 4, 0:w], b[:, 0:4 * w].rearrange("p (k w) -> p k w", k=4),
                                              1e-24, None, ALU.max), ring.drained)
                signal(dve.drain(), clamp_b)

            def sums(c, w, last=False):
                t = slice(0, w)
                sw_b.wait(dve, c)
                if last:
                    for k in range(8):
                        ins = dve.tensor_tensor_scan(cum[:, k, t], mix("tail_restart"), sw[:, k, t], 0.0, ALU.mult, ALU.add)
                    signal(ins, cum_b)
                    lane.settle()
                else:
                    lane.do(dve.tensor_tensor_scan(flat(cum, P), mix("restart"), flat(sw, P), 0.0, ALU.mult, ALU.add))
                    lane.settle()
                    lane.do(dve.tensor_copy(mid[:, 0:8].unsqueeze(2), cum[:, :, 63:64]))
                    lane.settle()
                    signal(dve.tensor_tensor(cum[:, :, t], cum[:, :, t], mid[:, 0:8].unsqueeze(2).broadcast_to([P, 8, w]),
                                             ALU.subtract), cum_b)

            def inverse_norms(c, w):
                root_b.wait(dve, c)
                lane.do(dve.reciprocal(kx[:, :, 0:w], kx[:, :, 0:w]))

            def normed_keys(c, par, w):
                t = slice(0, w)
                lane.settle()
                tt(kk[:, :, t], kk[:, :, t], kx[:, :, t], ALU.mult)
                lane.settle()
                rate_b.wait(dve, c)
                lane.do(dve.scalar_tensor_tensor(out=kx[:, :, t], in0=rate[:, :, t], scalar=-1.0, in1=wide(R_KA, w),
                                                 op0=ALU.add, op1=ALU.mult))

            def a_keys(c, par, w):
                t = slice(0, w)
                decx_b.wait(dve, c)
                lane.do(dve.scalar_tensor_tensor(out=AR[par][:, :, 0, t], in0=kk[:, :, t], scalar=-1.0, in1=sw[:, :, t],
                                                 op0=ALU.mult, op1=ALU.mult))

                lane.settle()
                tt(kk[:, :, t], kk[:, :, t], rate[:, :, t], ALU.mult)

            def b_keys(c, w):
                t = slice(0, w)
                dec_b.wait(dve, c)
                lane.settle()
                signal(dve.tensor_tensor(Bt[:, :, t], kk[:, :, t], pinv[:, :, t], ALU.mult), b_b)

                lane.do(dve.scalar_tensor_tensor(out=kx[:, :, t], in0=kx[:, :, t], scalar=1.0, in1=kc[:, :, t],
                                                 op0=ALU.add, op1=ALU.mult))

            def k_keys(c, w):
                t = slice(0, w)
                lane.settle()
                signal(dve.tensor_tensor(Kt[:, :, t], kx[:, :, t], pinv[:, :, t], ALU.mult), bk_b)

            def scale_state():
                lane.do(dve.tensor_copy(dend[:, 0:8].unsqueeze(2), pinc[:, :, P - 1:P]))
                signal(dve.tensor_tensor(Sm[:, :, :], S[:, :, :], dmid[:, 0:8].unsqueeze(2).broadcast_to([P, 8, P]),
                                         ALU.mult), s_b)

            def inverses(hg, w, levels, between):
                hb = hg // 2
                at = MIXTAB["below" if w == P else "tail_below"][0]
                masks = mixtab[0:w, at:at + 2 * w].unsqueeze(1).broadcast_to([w, hb, 2 * w])
                for gi in range(2):
                    for dst in (MR, NR):
                        for half in range(2):
                            b = ring.bank()
                            lane.do(dve.tensor_tensor(
                                dst[gi][0:w, half * hb * 2 * w:(half + 1) * hb * 2 * w].rearrange("p (h w) -> p h w", h=hb),
                                b[0:w, 0:hb * 2 * w].rearrange("p (h w) -> p h w", h=hb), masks, ALU.mult), ring.drained)
                    lane.settle()
                    xt = XT[gi][0:w, 0:hg * w].rearrange("p (h w) -> p h w", h=hg)
                    mt = MR[gi][0:w, 0:hg * 2 * w].rearrange("p (h a w) -> p h a w", h=hg, a=2)[:, :, 0, :]
                    tt(xt, mt, mix("first_pairs", w)[:, 0:w].unsqueeze(1).broadcast_to([w, hg, w]), ALU.mult)
                    lane.settle()
                    signal(dve.tensor_tensor(xt, xt, ident[0:w, 0:w].unsqueeze(1).broadcast_to([w, hg, w]), ALU.add), x1_b)
                between(0)
                for l in range(1, levels):
                    at = MIXTAB["siblings"][0] + (l - 1) * P
                    m = mixtab[0:w, at:at + w].unsqueeze(1).broadcast_to([w, hg, w])
                    for gi in range(2):
                        b = ring.bank()
                        lane.do(dve.tensor_tensor(W[gi][0:w, 0:hg * w].rearrange("p (h w) -> p h w", h=hg),
                                                  b[0:w, 0:hg * w].rearrange("p (h w) -> p h w", h=hg), m, ALU.mult), ring.drained)
                    for gi in range(2):
                        b = ring.bank()
                        xt = XT[gi][0:w, 0:hg * w]
                        lane.do(dve.tensor_tensor(xt, xt, b[0:w, 0:hg * w], ALU.add), ring.drained)
                    between(l)

            def head_view(t, w):
                return t.rearrange("p (h n) -> p h n", n=RN)[0:w]

            def bc(t, w):
                return t[0:w, 0:RH].unsqueeze(2).broadcast_to([w, RH, RN])

            def centre(c, w):
                yh = head_view(y, w)
                lane.do(dve.tensor_reduce(mean[0:w, 0:RH].unsqueeze(2), yh, AX, ALU.add))
                lane.settle()
                lane.do(dve.tensor_scalar(mean[0:w, :], mean[0:w, :], -1.0 / RN, None, ALU.mult))
                lane.settle()
                signal(dve.tensor_tensor(yh, yh, bc(mean, w), ALU.add), yc_b)

            def variances(c, w):
                ysq_b.wait(dve, c)
                signal(dve.tensor_reduce(var[0:w, 0:RH].unsqueeze(2), head_view(flat(pinv, P), w), AX, ALU.add), var_b)

            def scale_outputs(c, w):
                yh = head_view(y, w)
                ystd_b.wait(dve, c)
                lane.do(dve.reciprocal(var[0:w, :], var[0:w, :]))
                lane.settle()
                signal(dve.tensor_tensor(yh, yh, bc(var, w), ALU.mult), scaled_b)

            def gated(c, w):
                gn_b.wait(dve, c)
                for n in range(4):
                    b = ring.bank()
                    part = y[0:w, n * 256:(n + 1) * 256]
                    lane.do(dve.tensor_tensor(part, part, b[0:w, 0:256], ALU.mult), ring.drained)
                signal(dve.drain(), z_b)

            def finish_all(c, w):
                centre(c, w)
                variances(c, w)
                scale_outputs(c, w)
                gated(c, w)

            def prepare_all(c, par, w, last=False):
                clamp(c, w)
                sums(c, w, last)
                inverse_norms(c, w)
                normed_keys(c, par, w)
                a_keys(c, par, w)
                b_keys(c, w)
                k_keys(c, w)

            def chunk(c, par, finish=True, prepare=True):
                def between_first(l):
                    if l == 0:
                        if finish:
                            y_b.wait(dve, c - 1)
                        scale_state()
                    if finish and l == 1:
                        centre(c - 1, P)
                    if finish and l == 2:
                        variances(c - 1, P)
                    if finish and l == 3:
                        scale_outputs(c - 1, P)
                    if prepare and l == 4:
                        clamp(c + 1, P)
                    if finish and l == 5:
                        gated(c - 1, P)
                    if prepare and l == 6:
                        inverse_norms(c + 1, P)

                def between_second(l):
                    if not prepare:
                        return
                    if l == 1:
                        sums(c + 1, P)
                    if l == 2:
                        normed_keys(c + 1, 1 - par, P)
                    if l == 3:
                        a_keys(c + 1, 1 - par, P)
                    if l == 4:
                        b_keys(c + 1, P)
                    if l == 5:
                        k_keys(c + 1, P)

                for d in range(2):
                    inverses(4, P, LEVELS, between_second if d else between_first)
                    b = ring.bank()
                    cts = slice(4 * d, 4 * d + 4)
                    new = P1.rearrange("p (k w) -> p k w", k=4)
                    lane.do(dve.tensor_tensor(new, b[:, :].rearrange("p (k w) -> p k w", k=4),
                                              halves.unsqueeze(1).broadcast_to([P, 4, P]), ALU.mult), ring.drained)
                    lane.settle()
                    tt(new, new, Sm[:, cts, :], ALU.add)
                    lane.settle()
                    tt(S[:, cts, :], new, dend[:, 4 * d:4 * d + 4].unsqueeze(2).broadcast_to([P, 4, P]), ALU.mult)
                lane.settle()

            beats = [cum_b, clamp_b, b_b, bk_b, s_b, x1_b, yc_b, var_b, scaled_b, z_b]
            for beat in beats:
                beat.tally = Tally(beat.sem)
            prepare_all(0, 0, P)
            chunk(0, 0, finish=False)
            with dve.Fori(0, 3) as i:
                ring.drained.enter(i, 144)
                lane.order.enter(i, DVE_CHUNK)
                for beat in beats:
                    beat.tally.enter(i, 2 * beat.per)
                for u in range(2):
                    chunk(i * 2 + (u + 1), 1 - u)
                ring.drained.leave(3, "dve chunks")
                lane.order.leave(3, "DVE_CHUNK")
                for beat in beats:
                    beat.tally.leave(3)
            chunk(7, 1, prepare=False)
            y_b.wait(dve, 7)
            finish_all(7, P)
            c, w = 8, TAIL
            prepare_all(c, 0, w, True)

            def between(l):
                pass

            inverses(8, w, 4, between)
            arm_t = Tally(arm_s)
            cols_at, rows_at = MIXTAB["seq_cols"][0], MIXTAB["seq_rows"][0]

            def mask_queries(s):
                for u in range(2):
                    ins = dve.tensor_tensor(Bz[:, :, u, 0:w], AR[0][:, :, u, 0:w],
                                            mixtab[:, bass.ds(s * w + cols_at, w)].unsqueeze(1).broadcast_to([P, 8, w]), ALU.mult)
                lane.do(ins, arm_t)

            mask_queries(0)
            with dve.Fori(0, DB) as i:
                arm_t.enter(i, 1)
                dve.wait_ge(arm_used, i + 1)
                mask_queries(i + 1)
                arm_t.leave(DB)
            for half in range(2):
                take(P1_tail[0:w, half * 512:(half + 1) * 512], w, 512)
            for half in range(2):
                take(y[0:w, half * 512:(half + 1) * 512], w, 512)
            lane.settle()
            finish_all(c, w)
            bm_t, sn_t = Tally(bm_s), Tally(snew_s)

            def new_state(s, state):
                for dst, src in ((Bm, Btok), (Km, Ktok)):
                    ins = dve.tensor_tensor(dst[0:w, :], src[0:w, :],
                                            mixtab[0:w, bass.ds(s + rows_at, 1)].broadcast_to([w, D]), ALU.mult)
                lane.do(ins, bm_t)
                for n in range(4):
                    b = ring.bank()
                    lane.do(dve.tensor_tensor(kx[:, 2 * n:2 * n + 2, :], b[:, 0:256].rearrange("p (k w) -> p k w", k=2),
                                              halves.unsqueeze(1).broadcast_to([P, 2, P]), ALU.mult), ring.drained)
                lane.settle()
                tt(kx[:, :, :], kx[:, :, :], state[:, :, :], ALU.add)
                lane.settle()
                lane.do(dve.tensor_tensor(kx[:, :, :], kx[:, :, :],
                                          pinc[:, :, bass.ds(s * DS + NMETA - 1, 1)].broadcast_to([P, 8, P]), ALU.mult), sn_t)

            new_state(0, S)
            with dve.Fori(0, DB) as i:
                ring.drained.enter(i, 4)
                lane.order.enter(i, 1)
                bm_t.enter(i, 1)
                sn_t.enter(i, 1)
                dve.wait_ge(bm_used, i + 1)
                dve.wait_ge(a_drained, i * 8 + mark["state_out"] + 8)
                new_state(i + 1, kc)
                ring.drained.leave(DB, "dve states")
                lane.order.leave(DB, "dve states order")
                bm_t.leave(DB)
                sn_t.leave(DB)
            meet(dve, here)
            dve.wait_ge(hid_s, 16 + 16 * KT)
            for at, w in PIECES:
                for k in range(KT):
                    add_hidden(k, at, w)
            feed(1)
            meet(dve, here)
            norm(hT, nT, KT, R_FIN, mark["norm_final"])
            for t in range(NT):
                w = P if t < 8 else TAIL
                take(yout[0:w, t, 512:1024], w, 512)


_INS = ["x_prompt", "x_sample", "cache_kv_latent", "cache_k_rope", "state_wkv", "state_shift", "page_table",
        "meta_tokens", "norm_mix", "norm_ffn", "norm_final", "mla_w_qkv_a", "mla_q_a_norm", "mla_kv_a_norm",
        "mla_w_q_b", "mla_w_kv_b", "mla_w_o", "rwkv_mu", "rwkv_w_r", "rwkv_w_k", "rwkv_w_v", "rwkv_w_o",
        "rwkv_decay_w0", "rwkv_decay_w1", "rwkv_decay_w2", "rwkv_a_w0", "rwkv_a_w1", "rwkv_a_w2", "rwkv_g_w1",
        "rwkv_g_w2", "rwkv_k_k", "rwkv_k_a", "rwkv_r_k", "rwkv_ln_w", "rwkv_ln_b", "ffn_w_up", "ffn_w_down"]
_OUTS = [("y_prompt", (1, SEQ, D)), ("y_sample", (DB, DS, D)), ("lat_p", (1, 1, NP, KVL)), ("rope_p", (1, 1, NP, ROPE)),
         ("lat_s", (1, DB, DS, KVL)), ("rope_s", (1, DB, DS, ROPE)), ("wkv_p", (1, 1, RH, RN, RN)),
         ("shift_p", (1, 1, D)), ("wkv_s", (1, DB, RH, RN, RN)), ("shift_s", (1, DB, D))]


def constants():
    import numpy as np

    stays, mixing = np.zeros((P, NTABLE), np.float32), np.zeros((P, NMIXTAB), np.float32)

    def put(name, v):
        t = stays if name in TABLE else mixing
        at, n = TABLE[name] if name in TABLE else MIXTAB[name]
        v = np.asarray(v, np.float32)
        t[:v.shape[0], at:at + n] = v.reshape(v.shape[0], n)

    p = np.arange(P)
    row, col = p[:, None], p[None, :]
    put("ident", row == col)
    put("ones", np.ones((P, P)))
    put("halves", row // RN == col // RN)
    c = col % ROPE
    put("rot", np.where((c < 32) & (row == col + 32), -1.0, 0.0) + np.where((c >= 32) & (row == col - 32), 1.0, 0.0))
    put("below", row < col)
    put("upto", row <= col)
    s = np.arange(TAIL)
    of = np.where(s < NMETA, 0, 1 + (s - NMETA) // DS)
    same = of[:, None] == of[None, :]
    put("tail_below", same & (s[:, None] < s[None, :]))
    put("tail_upto", same & (s[:, None] <= s[None, :]))
    put("first_pairs", (col % 2 == 1) & (row == col - 1))
    put("siblings", np.stack([((row >> l) == (col >> l) + 1) & ((col >> l) % 2 == 0) for l in range(1, 7)], 1))
    q = np.arange(QT)
    put("causal", np.where(q[None, :] <= q[:, None], 0.0, NEG))
    r = np.arange(ND)
    b = np.arange(DB)
    new = (r[None, None, :] // DS == b[None, :, None]) & (r[None, None, :] % DS <= r[:, None, None] % DS)
    put("new_keys", np.where(new, 0.0, NEG))
    put("restart", np.tile(np.tile(p != 0, 8), (P, 1)))
    starts = np.r_[1, np.diff(of)] != 0
    put("tail_restart", np.tile(~starts, (P, 1)))
    put("seq_rows", of[:, None] == np.arange(9)[None, :])
    put("seq_cols", np.tile((of[None, :] == np.arange(9)[:, None]).reshape(-1), (P, 1)))
    put("head_cols", row // RN == np.arange(2)[None, :])
    half = ROPE // 2
    freq = (np.float32(10000.0) ** (-np.arange(half, dtype=np.float32) / np.float32(half))).astype(np.float32)
    pos = np.r_[np.arange(NP), np.tile(PAST + np.arange(DS), DB)].astype(np.float32)
    ang = (freq[:, None] * pos[None, :]).astype(np.float32)
    return {"table": stays, "mixtable": mixing, "cos": np.tile(np.cos(ang), (4, 1)), "sin": np.tile(np.sin(ang), (4, 1))}


def kernel(**inputs):
    import numpy as np
    import concourse.bacc as bacc
    from concourse.bass_utils import run_bass_kernel_spmd

    nc = bacc.Bacc("TRN2", target_bir_lowering=False, num_devices=1)
    arrays, ins, outs = {}, {}, {}
    given = {name: inputs[name] for name in _INS}
    given.update(constants())
    for name, a in given.items():
        a = np.ascontiguousarray(a)
        arrays["in_" + name] = a
        ins[name] = nc.dram_tensor("in_" + name, a.shape, mybir.dt.from_np(a.dtype), kind="ExternalInput").ap()
    for name, shape in _OUTS:
        outs[name] = nc.dram_tensor("out_" + name, shape, F32, kind="ExternalOutput").ap()
    program(nc, ins, outs)
    r = run_bass_kernel_spmd(nc, [arrays], core_ids=[0])
    return tuple(r.results[0]["out_" + name] for name, _ in _OUTS)
```
